# Optimizing a Trainium2 kernel written in Bass

```python
import math
import jax
import jax.numpy as jnp
from jax import lax
import numpy as np

"""Hybrid parallel-branch diffusion backbone (2 layers) over latent tokens with a context prefix.

Inputs:  x (BATCH, SEQ, D_MODEL) latent tokens on a GRID_W-wide grid, c (BATCH, D_MODEL) conditioning,
         ctx (BATCH, CTX_LEN, D_MODEL) context tokens, c_ctx (D_MODEL,) learned context conditioning,
         plus per-layer weights stacked on a leading DEPTH axis.
Output:  (BATCH, SEQ, D_MODEL) final-RMSNorm latent stream.
Each layer: adaLN-modulated RMSNorm -> one combined input projection -> three parallel mixers
(bidirectional chunked GLA, GQA with QK-RMSNorm + 2-D axial rotary, order-2 bidirectional Hyena),
each multiplied by its own SiLU gate path, projected to D_MODEL, merged with per-channel sigmoid
gates, one output projection, adaLN-gated residual add.
"""

D_MODEL = 1024
BATCH = 1
SEQ = 512
DEPTH = 2

GRID_W = 64
CTX_LEN = 256
BRANCH_W = D_MODEL // 2
N_BRANCH = 3
EPS = 1e-6
GLA_HEADS = 4
GLA_DV = BRANCH_W // GLA_HEADS
GLA_DK = GLA_DV // 2
GLA_KW = GLA_HEADS * GLA_DK
GLA_VW = GLA_HEADS * GLA_DV
GLA_RANK = 16
GLA_GATE_NORM = 16.0
GLA_CHUNK = 64
ATTN_HD = 64
ATTN_HEADS = BRANCH_W // ATTN_HD
ATTN_KV_HEADS = ATTN_HEADS // 4
ATTN_GROUP = ATTN_HEADS // ATTN_KV_HEADS
ATTN_QW = ATTN_HEADS * ATTN_HD
ATTN_KVW = ATTN_KV_HEADS * ATTN_HD
Q_BLOCK = 128
ROPE_THETA = 10000.0
HY_W = BRANCH_W
HY_ORDER = 2
HY_EMB = 33
HY_BANDS = (HY_EMB - 1) // 2
HY_FFN = 64
HY_SHORT = 3
HY_MOD_SHIFT = 0.05
HY_DECAY_SHORT_PCT = 0.3
HY_DECAY_LONG_PCT = 1.5
HY_DECAY_TARGET = 1e-2
N_FILT = 2 * HY_ORDER * HY_W
SPLITS = (GLA_KW, GLA_KW, GLA_VW, GLA_VW, GLA_RANK, GLA_RANK,
          ATTN_QW, ATTN_KVW, ATTN_KVW, ATTN_QW,
          (HY_ORDER + 1) * HY_W, HY_W,
          N_BRANCH * D_MODEL)
N_IN = sum(SPLITS)

kernel_name = "hybrid_gla_gqa_hyena_prefix_dit"

def rms_norm(a):
    af = a.astype(jnp.float32)
    return (af * lax.rsqrt(jnp.mean(af * af, axis=-1, keepdims=True) + EPS)).astype(a.dtype)

def heads(a, n):
    return a.reshape(a.shape[:-1] + (n, a.shape[-1] // n))

def rev(a):
    return a[:, ::-1]

def split_proj(p):
    idx = [int(i) for i in np.cumsum(SPLITS)[:-1]]
    return jnp.split(p, idx, axis=-1)

def axial_rope_angles(L):
    t = jnp.arange(L)
    row = (t // GRID_W).astype(jnp.float32)
    col = (t % GRID_W).astype(jnp.float32)
    half = ATTN_HD // 2
    inv = ROPE_THETA ** (-jnp.arange(0, half, 2, dtype=jnp.float32) / half)
    return jnp.concatenate([row[:, None] * inv, col[:, None] * inv], axis=-1)

def apply_rope(a, ang):
    af = a.astype(jnp.float32).reshape(a.shape[:-1] + (ATTN_HD // 2, 2))
    cos = jnp.cos(ang)[None, :, None, :]
    sin = jnp.sin(ang)[None, :, None, :]
    a0, a1 = af[..., 0], af[..., 1]
    out = jnp.stack([a0 * cos - a1 * sin, a0 * sin + a1 * cos], axis=-1)
    return out.reshape(a.shape).astype(a.dtype)

def gla_decays(af, ab, wa_f, ba_f, wa_b, ba_b):
    gf = jax.nn.log_sigmoid((af @ wa_f + ba_f).astype(jnp.float32)) / GLA_GATE_NORM
    gb = jax.nn.log_sigmoid((ab @ wa_b + ba_b).astype(jnp.float32)) / GLA_GATE_NORM
    return heads(gf, GLA_HEADS), heads(gb, GLA_HEADS)

def gla_scan(q, k, v, g, s0):
    b_, L, H, _ = q.shape
    dv = v.shape[-1]
    nc = L // GLA_CHUNK

    def chunks(a):
        return a.reshape(b_, nc, GLA_CHUNK, H, a.shape[-1]).transpose(1, 0, 3, 2, 4)

    mask = jnp.tril(jnp.ones((GLA_CHUNK, GLA_CHUNK), dtype=bool))[:, :, None]

    def step(s, inp):
        qc, kc, vc, gc = inp
        bcum = jnp.cumsum(gc, axis=2)
        blast = bcum[:, :, -1:, :]
        diff = bcum[:, :, :, None, :] - bcum[:, :, None, :, :]
        decay = jnp.exp(jnp.where(mask, diff, -jnp.inf))
        att = jnp.einsum('bhid,bhjd,bhijd->bhij', qc, kc, decay)
        o = (jnp.einsum('bhij,bhjv->bhiv', att, vc)
             + jnp.einsum('bhid,bhdv->bhiv', qc * jnp.exp(bcum), s))
        s_new = (jnp.exp(blast[:, :, 0, :])[..., None] * s
                 + jnp.einsum('bhjd,bhjv->bhdv', kc * jnp.exp(blast - bcum), vc))
        return s_new, o

    s_fin, o = lax.scan(step, s0, (chunks(q), chunks(k), chunks(v), chunks(g)))
    o = o.transpose(1, 0, 3, 2, 4).reshape(b_, L, H, dv)
    return o, s_fin

def gla_final_state(k, v, g):
    bcum = jnp.cumsum(g, axis=1)
    w = jnp.exp(bcum[:, -1:] - bcum)
    return jnp.einsum('blhd,blhv->bhdv', k * w, v)

def gla_out(o, norm_w, z):
    o = rms_norm(o) * norm_w.astype(jnp.float32)
    return o.reshape(o.shape[:2] + (GLA_VW,)).astype(z.dtype) * jax.nn.silu(z)

def attend(qg, keys, vals):
    s = jnp.einsum('bqgrd,bkgd->bgrqk', qg, keys).astype(jnp.float32) * (ATTN_HD ** -0.5)
    p = jax.nn.softmax(s, axis=-1).astype(vals.dtype)
    return jnp.einsum('bgrqk,bkgd->bqgrd', p, vals)

def attn_latent(q, k, v, k_ctx, v_ctx):
    b_, L = q.shape[0], q.shape[1]
    nb = L // Q_BLOCK
    keys = jnp.concatenate([k, k_ctx], axis=1)
    vals = jnp.concatenate([v, v_ctx], axis=1)
    qb = q.reshape(b_, nb, Q_BLOCK, ATTN_KV_HEADS, ATTN_GROUP, ATTN_HD).transpose(1, 0, 2, 3, 4, 5)
    o = lax.map(lambda qblk: attend(qblk, keys, vals), qb)
    return o.transpose(1, 0, 2, 3, 4, 5).reshape(b_, L, ATTN_QW)

def qk_norm(a, gain):
    return rms_norm(a) * gain

def short_conv(u, w, bias):
    L = u.shape[1]
    pad = HY_SHORT // 2
    up = jnp.pad(u, ((0, 0), (pad, pad), (0, 0)))
    out = bias
    for i in range(HY_SHORT):
        out = out + up[:, i:i + L] * w[i]
    return out

def hyena_filters(L, f1_w, f1_b, f1_freq, f2_w, f2_b, f2_freq, f3_w):
    f32 = jnp.float32
    t = jnp.linspace(0.0, 1.0, L, dtype=f32)[:, None]
    w = 2.0 * math.pi * jnp.arange(L, dtype=f32)[:, None] / L
    fr = jnp.linspace(1e-4, HY_BANDS - 1, HY_BANDS, dtype=f32)[None]
    emb = jnp.concatenate([t, jnp.cos(fr * w), -jnp.sin(fr * w)], axis=-1)
    h = jnp.sin(f1_freq.astype(f32) * (emb @ f1_w.astype(f32) + f1_b.astype(f32)))
    h = jnp.sin(f2_freq.astype(f32) * (h @ f2_w.astype(f32) + f2_b.astype(f32)))
    h = h @ f3_w.astype(f32)
    deltas = jnp.abs(jnp.linspace(math.log(HY_DECAY_TARGET) / HY_DECAY_SHORT_PCT,
                                  math.log(HY_DECAY_TARGET) / HY_DECAY_LONG_PCT, N_FILT, dtype=f32))
    h = h * (jnp.exp(-t * deltas) + HY_MOD_SHIFT)
    h = h / jnp.sum(jnp.abs(h), axis=0, keepdims=True)
    return h.reshape(L, HY_ORDER, 2, HY_W)

def bidir_long_conv(z, hf, hb):
    L = z.shape[1]
    filt = jnp.concatenate([hf, jnp.zeros_like(hf[:1]), hb[:0:-1]], axis=0)
    ff = jnp.fft.rfft(filt, axis=0)
    zf = jnp.fft.rfft(z, n=2 * L, axis=1)
    return jnp.fft.irfft(zf * ff[None], n=2 * L, axis=1)[:, :L]

def hyena_mix(u, conv_w, conv_b, f1_w, f1_b, f1_freq, f2_w, f2_b, f2_freq, f3_w, skip):
    L = u.shape[1]
    u = short_conv(u, conv_w, conv_b)
    v, x1, x2 = jnp.split(u, HY_ORDER + 1, axis=-1)
    h = hyena_filters(L, f1_w, f1_b, f1_freq, f2_w, f2_b, f2_freq, f3_w)
    z = v.astype(jnp.float32)
    for o, gt in enumerate((x1, x2)):
        z = gt.astype(jnp.float32) * (bidir_long_conv(z, h[:, o, 0], h[:, o, 1])
                                      + skip[o].astype(jnp.float32) * z)
    return z.astype(u.dtype)

def merge_branches(y_gla, y_attn, y_hy, mg, w_g, w_a, w_h, w_o):
    m = jax.nn.sigmoid(mg.astype(jnp.float32)).astype(y_gla.dtype)
    m_g, m_a, m_h = jnp.split(m, N_BRANCH, axis=-1)
    y = m_g * (y_gla @ w_g) + m_a * (y_attn @ w_a) + m_h * (y_hy @ w_h)
    return y @ w_o

def setup_inputs(seed: int = 0) -> dict:
    key = jax.random.key(seed)
    ks = jax.random.split(key, 32)
    f32 = jnp.float32
    D = D_MODEL

    def nrm(k, shape, scale):
        return scale * jax.random.normal(k, shape, f32)

    return {
        'x': nrm(ks[0], (BATCH, SEQ, D), 1.0),
        'c': nrm(ks[1], (BATCH, D), 1.0),
        'ctx': nrm(ks[2], (BATCH, CTX_LEN, D), 1.0),
        'c_ctx': nrm(ks[3], (D,), 1.0),
        'w_ada': nrm(ks[4], (DEPTH, D, 3 * D), 0.5 * D ** -0.5),
        'b_ada': nrm(ks[5], (DEPTH, 3 * D), 0.02),
        'w_in': nrm(ks[6], (DEPTH, D, N_IN), D ** -0.5),
        'gla_wa_f': nrm(ks[7], (DEPTH, GLA_RANK, GLA_KW), GLA_RANK ** -0.5),
        'gla_ba_f': nrm(ks[8], (DEPTH, GLA_KW), 0.1),
        'gla_wa_b': nrm(ks[9], (DEPTH, GLA_RANK, GLA_KW), GLA_RANK ** -0.5),
        'gla_ba_b': nrm(ks[10], (DEPTH, GLA_KW), 0.1),
        'gla_norm': 1.0 + nrm(ks[11], (DEPTH, GLA_DV), 0.02),
        'attn_qnorm': 1.0 + nrm(ks[12], (DEPTH, ATTN_HD), 0.02),
        'attn_knorm': 1.0 + nrm(ks[13], (DEPTH, ATTN_HD), 0.02),
        'hy_conv_w': nrm(ks[14], (DEPTH, HY_SHORT, (HY_ORDER + 1) * HY_W), HY_SHORT ** -0.5),
        'hy_conv_b': nrm(ks[15], (DEPTH, (HY_ORDER + 1) * HY_W), 0.02),
        'hy_f1_w': nrm(ks[16], (DEPTH, HY_EMB, HY_FFN), HY_EMB ** -0.5),
        'hy_f1_b': nrm(ks[17], (DEPTH, HY_FFN), 0.1),
        'hy_f1_freq': 1.0 + nrm(ks[18], (DEPTH, HY_FFN), 0.02),
        'hy_f2_w': nrm(ks[19], (DEPTH, HY_FFN, HY_FFN), HY_FFN ** -0.5),
        'hy_f2_b': nrm(ks[20], (DEPTH, HY_FFN), 0.1),
        'hy_f2_freq': 1.0 + nrm(ks[21], (DEPTH, HY_FFN), 0.02),
        'hy_f3_w': nrm(ks[22], (DEPTH, HY_FFN, N_FILT), HY_FFN ** -0.5),
        'hy_skip': nrm(ks[23], (DEPTH, HY_ORDER, HY_W), 0.5),
        'w_br_gla': nrm(ks[24], (DEPTH, BRANCH_W, D), BRANCH_W ** -0.5),
        'w_br_attn': nrm(ks[25], (DEPTH, BRANCH_W, D), BRANCH_W ** -0.5),
        'w_br_hy': nrm(ks[26], (DEPTH, BRANCH_W, D), BRANCH_W ** -0.5),
        'w_out': nrm(ks[27], (DEPTH, D, D), D ** -0.5),
        'final_norm': 1.0 + nrm(ks[28], (D,), 0.02),
    }

def reference(x, c, ctx, c_ctx, w_ada, b_ada, w_in, gla_wa_f, gla_ba_f, gla_wa_b, gla_ba_b,
              gla_norm, attn_qnorm, attn_knorm, hy_conv_w, hy_conv_b, hy_f1_w, hy_f1_b,
              hy_f1_freq, hy_f2_w, hy_f2_b, hy_f2_freq, hy_f3_w, hy_skip, w_br_gla, w_br_attn,
              w_br_hy, w_out, final_norm):
    b_ = x.shape[0]
    L = x.shape[1]
    Lc = ctx.shape[1]
    ang = axial_rope_angles(L)
    s_lat = jax.nn.silu(c)
    s_ctx = jax.nn.silu(c_ctx)
    zero_state = jnp.zeros((b_, GLA_HEADS, GLA_DK, GLA_DV), jnp.float32)
    gla_scale = GLA_DK ** -0.5

    for l in range(DEPTH):
        need_ctx = l < DEPTH - 1
        shift, scale, gate = jnp.split(s_lat @ w_ada[l] + b_ada[l], 3, axis=-1)
        shift_c, scale_c, gate_c = jnp.split(s_ctx @ w_ada[l] + b_ada[l], 3, axis=-1)
        h = rms_norm(x) * (1.0 + scale[:, None]) + shift[:, None]
        hc = rms_norm(ctx) * (1.0 + scale_c) + shift_c
        (g_q, g_k, g_v, g_z, g_af, g_ab, a_q, a_k, a_v, a_z, y_u, y_z, m_lat) = split_proj(h @ w_in[l])
        (gc_q, gc_k, gc_v, gc_z, gc_af, gc_ab, ac_q, ac_k, ac_v, ac_z, yc_u, yc_z, m_ctx) = split_proj(hc @ w_in[l])
        gla_p = (gla_wa_f[l], gla_ba_f[l], gla_wa_b[l], gla_ba_b[l])
        hy_p = (hy_conv_w[l], hy_conv_b[l], hy_f1_w[l], hy_f1_b[l], hy_f1_freq[l],
                hy_f2_w[l], hy_f2_b[l], hy_f2_freq[l], hy_f3_w[l], hy_skip[l])

        k, v = heads(g_k, GLA_HEADS), heads(g_v, GLA_HEADS)
        q = heads(g_q, GLA_HEADS) * gla_scale
        gf, gb = gla_decays(g_af, g_ab, *gla_p)
        kc, vc = heads(gc_k, GLA_HEADS), heads(gc_v, GLA_HEADS)
        gfc, gbc = gla_decays(gc_af, gc_ab, *gla_p)
        if need_ctx:
            qc = heads(gc_q, GLA_HEADS) * gla_scale
            oc_f, sc_f = gla_scan(qc, kc, vc, gfc, zero_state)
            oc_b, sc_b = gla_scan(rev(qc), rev(kc), rev(vc), rev(gbc), zero_state)
            yc_gla = gla_out(oc_f + rev(oc_b), gla_norm[l], gc_z)
        else:
            sc_f = gla_final_state(kc, vc, gfc)
            sc_b = gla_final_state(rev(kc), rev(vc), rev(gbc))
        o_f, _ = gla_scan(q, k, v, gf, sc_f)
        o_b, _ = gla_scan(rev(q), rev(k), rev(v), rev(gb), sc_b)
        y_gla = gla_out(o_f + rev(o_b), gla_norm[l], g_z)

        kc_a = qk_norm(heads(ac_k, ATTN_KV_HEADS), attn_knorm[l])
        vc_a = heads(ac_v, ATTN_KV_HEADS)
        q_a = apply_rope(qk_norm(heads(a_q, ATTN_HEADS), attn_qnorm[l]), ang)
        k_a = apply_rope(qk_norm(heads(a_k, ATTN_KV_HEADS), attn_knorm[l]), ang)
        y_attn = attn_latent(q_a, k_a, heads(a_v, ATTN_KV_HEADS), kc_a, vc_a) * jax.nn.silu(a_z)

        y_hy = hyena_mix(y_u, *hy_p) * jax.nn.silu(y_z)

        out = merge_branches(y_gla, y_attn, y_hy, m_lat, w_br_gla[l], w_br_attn[l], w_br_hy[l], w_out[l])
        x_new = x + gate[:, None] * out

        if need_ctx:
            qc_a = qk_norm(heads(ac_q, ATTN_HEADS), attn_qnorm[l])
            qc_g = qc_a.reshape(b_, Lc, ATTN_KV_HEADS, ATTN_GROUP, ATTN_HD)
            yc_attn = attend(qc_g, kc_a, vc_a).reshape(b_, Lc, ATTN_QW) * jax.nn.silu(ac_z)
            yc_hy = hyena_mix(yc_u, *hy_p) * jax.nn.silu(yc_z)
            out_c = merge_branches(yc_gla, yc_attn, yc_hy, m_ctx, w_br_gla[l], w_br_attn[l], w_br_hy[l], w_out[l])
            ctx = ctx + gate_c * out_c
        x = x_new

    return rms_norm(x) * final_norm


_drawn_inputs = setup_inputs


def setup_inputs(seed=0):
    import zlib

    import numpy as np

    out = dict(_drawn_inputs(seed))
    spreads = {}
    factors = {'ctx': 2.942,
     'c_ctx': 2.823,
     'b_ada': 3.479,
     'gla_wa_f': 2.862,
     'gla_ba_f': 8.0,
     'gla_wa_b': 3.063,
     'gla_ba_b': 8.0,
     'gla_norm': 8.0,
     'attn_qnorm': 21.456,
     'attn_knorm': 8.0,
     'hy_conv_b': 32.231,
     'hy_f1_b': 8.0,
     'hy_f1_freq': 26.855,
     'hy_f2_b': 7.21,
     'hy_f2_freq': 64.0,
     'final_norm': 7.443}
    for name, (base, spread) in spreads.items():
        noise = np.random.default_rng([zlib.crc32(name.encode()), seed]).standard_normal(out[name].shape)
        drawn = base * np.exp(spread * noise) if base else spread * noise
        out[name] = jnp.asarray(drawn.astype(out[name].dtype))
    for name, factor in factors.items():
        out[name] = (out[name] * factor).astype(out[name].dtype)
    return out
```

```python
import math
from contextlib import ExitStack

import numpy as np
import concourse.bass as bass
from concourse import mybir

F32 = mybir.dt.float32
ALU = mybir.AluOpType
ACT = mybir.ActivationFunctionType
AX = mybir.AxisListType

P = 128
D = 1024
KD = D // P
DEPTH = 2
BW = 512
LAT, CTX = 512, 256
TOK = LAT + CTX
EPS = 1e-6
GRID_W = 64
STREAMS = {"lat": (0, LAT), "ctx": (LAT, CTX)}
LEVELS = [64, 32, 16, 8, 4, 2, 1]
FACTORS = {"lat": 4, "ctx": 2}
ROOT2 = math.sqrt(2.0)
TWO_PI_1, TWO_PI_2 = 6.28125, 0.0019350051879882812
TWO_PI_3 = 2 * math.pi - TWO_PI_1 - TWO_PI_2
ROUND_MAGIC = 1.5 * 2.0 ** 23
PI_BELOW = 3.1415925

HY_TILES = [("u", i) for i in range(12)] + [("hz", i) for i in range(4)]
GLA_TILES = [("ga", 0), ("gk", 0), ("gk", 1), ("gq", 0), ("gq", 1)] + [("gv", i) for i in range(4)] + [("gz", i) for i in range(4)]
ATT_TILES = [("ak", 0), ("av", 0)] + [("aq", i) for i in range(4)] + [("az", i) for i in range(4)]
GATE_TILES = [("m", 3 * j + b) for j in range(KD) for b in range(3)]
IN_TILES = HY_TILES + GLA_TILES + ATT_TILES + GATE_TILES
IN_INDEX = {t: i for i, t in enumerate(IN_TILES)}


def streams_of(layer):
    return ["ctx", "lat"] if layer < DEPTH - 1 else ["lat"]


def streams_for(layer, tile):
    return ["lat", "ctx"] if layer < DEPTH - 1 or tile[0] in ("ga", "gk", "gv", "ak", "av") else ["lat"]


class Counts:

    def __init__(self, nc, stack, known=None, stages=()):
        self.nc, self.stack, self.known = nc, stack, known
        self.sems, self.count, self.at, self.latest, self.engine = {}, {}, {}, {}, None
        for s in stages:
            self.sem(s)

    def sem(self, stage):
        if stage not in self.sems:
            self.sems[stage] = self.stack.enter_context(self.nc.semaphore(stage))
            self.count[stage] = 0
        return self.sems[stage]

    def done(self, stage, *key, also=(), by=1):
        sem = self.sem(stage)
        self.count[stage] += by
        for label in [(stage, *key), *also]:
            self.at[label] = (stage, self.count[stage])
        if by == 1:
            self.latest[self.engine] = (stage, self.count[stage])
        return sem, by

    def after(self, *label):
        if self.known is None:
            return self.sem("any"), 1
        stage, n = self.known[label]
        return self.sem(stage), n

    def phase_end(self, phase):
        self.at[("end", self.engine, phase)] = self.latest[self.engine]


class Psum:

    def __init__(self, counts, banks):
        self.c, self.banks, self.next, self.holder = counts, banks, 0, {}
        self.where = {}

    def take(self, pe, *key, n=1, at=None):
        if at is None:
            at = self.next
            if at % 8 + n > 8 or (n == 2 and at % 2):
                at += 1
            self.next = (at + n) % 8
        at %= 8
        for b in range(at, at + n):
            if b in self.holder:
                pe.wait_ge(*self.c.after("freed", *self.holder[b]))
            self.holder[b] = key
        self.where[key] = (at, n)
        return self.banks[:, at:at + n, :].rearrange("p b n -> p (b n)")

    def of(self, *key):
        if key not in self.where:
            key_at = (0, 2)
        else:
            key_at = self.where[key]
        at, n = key_at
        return self.banks[:, at:at + n, :].rearrange("p b n -> p (b n)")


def carve(tensor, at, *shape):
    n = int(np.prod(shape))
    v = tensor[:, at:at + n]
    if len(shape) == 2:
        v = v.rearrange("p (a b) -> p a b", a=shape[0])
    if len(shape) == 3:
        v = v.rearrange("p (a b c) -> p a b c", a=shape[0], b=shape[1])
    if len(shape) == 4:
        v = v.rearrange("p (a b c d) -> p a b c d", a=shape[0], b=shape[1], c=shape[2])
    return v, at + n


def build_program(nc, d, known=None, stages=()):
    stack = ExitStack()
    with stack:
        c = Counts(nc, stack, known, stages)

        def sb(name, *shape, dt=F32):
            return stack.enter_context(nc.sbuf_tensor(name, [P, *shape], dt))

        H = sb("H", KD, TOK)
        YB = sb("YB", 12 * TOK)
        YBT = YB[:, :].rearrange("p (a t) -> p a t", a=12)
        NSLOT = 4
        RING = sb("RING", NSLOT, KD, P)
        TRI = sb("TRI", 2, P)
        IDENT = sb("IDENT", P)
        ONES = sb("ONES", 3, P)
        MASK = sb("MASK", len(LEVELS), P, dt=mybir.dt.uint8)
        DIAG2 = sb("DIAG2", P)
        COLS = sb("COLS", 90)
        ADA = sb("ADA", 24, 2)
        SC = sb("SC", KD, 2)
        SMALL = sb("SMALL", 256)
        ARENA_N = 31900
        AR = sb("AR", ARENA_N)
        banks = stack.enter_context(nc.psum_tensor("banks", [P, 8, 512], F32))
        ps = Psum(c, banks)
        B_ADA, GNORM, CONVW, CONVB, FINALN = COLS[:, 0:24], COLS[:, 24:25], COLS[:, 25:61], COLS[:, 61:73], COLS[:, 73:81]
        EPSC, NOT0, TNEG = COLS[:, 81:82], COLS[:, 82:83], COLS[:, 83:83]
        TCOL, _ = carve(SMALL, 0, 12)
        C64, _ = carve(SMALL, 12, 4)
        NMAX, _ = carve(SMALL, 16, 48)
        SUMS, _ = carve(SMALL, 64, 48)
        RINV, _ = carve(SMALL, 112, 48)
        MSQ, _ = carve(SMALL, 160, 60)
        DEC, _ = carve(SMALL, 220, 2, 2, 4)

        X, n0 = carve(AR, 0, KD, TOK)
        SQ, n = carve(AR, n0, 2, TOK)
        RS, n = carve(AR, n, TOK)
        YM, n = carve(AR, n0, KD, TOK)
        BRW, n = carve(AR, n, 2, 12, P)
        MG, n = carve(AR, n, 2, 3, TOK)
        MT, n = carve(AR, n, 2, TOK)
        OUTB, _ = carve(AR, n0 + 3 * TOK, KD, LAT)
        assert n <= ARENA_N
        MASK32 = carve(AR, n, len(LEVELS), P)[0].bitcast(mybir.dt.int32)
        G, n = carve(AR, 0, 8, LAT)
        FM, n = carve(AR, n, 16, P)
        UD, n = carve(AR, n, 4, TOK)
        HX, _ = carve(UD.rearrange("p a b -> p (a b)"), 0, 3, 1024)
        TOKM, n = carve(AR, n, 2, 6, BW)
        FW, n = carve(AR, n, 8, BW)
        EMB, _ = carve(FW.rearrange("p a b -> p (a b)"), 0, 1536)
        R, n = carve(AR, n, 8, BW)
        FH, n = carve(AR, n, 9, BW)
        H2, n = carve(AR, n, 1536)
        Y = FW
        assert n <= ARENA_N, n
        F3, n = carve(YB, 0, 4, BW)
        TT, n = carve(YB, n, 4, BW)
        RN, n = carve(YB, n, 2, BW)
        DEL, n = carve(YB, n, BW)
        F12, n = carve(YB, n, 2, 64)
        assert n <= 8 * TOK
        SKIP, _ = carve(TT.rearrange("p a b -> p (a b)"), 3 * BW, BW)
        GK, n = carve(AR, 0, 2, TOK)
        GQ, n = carve(AR, n, 2, TOK)
        GV, n = carve(AR, n, 6, BW)
        GZ, n = carve(AR, n, 4, TOK)
        GA, n = carve(AR, n, TOK)
        WA, n = carve(AR, n, BW)
        GG, n = carve(AR, n, 4, BW)
        ATT = GG
        B, n = carve(AR, n, 2, 2, LAT)
        EL, n = carve(AR, n, 2, 2, 2 * LAT)
        QH, n = carve(AR, n, 2, 2, LAT)
        KH, nk = carve(AR, n, 2, 2, LAT)
        OS, n = carve(AR, n, 6, BW)
        KT, n = carve(AR, n, 2, 2, LAT)
        ST, n = carve(AR, n, 2, 2, 6 * P)
        GT, n = carve(AR, n, 2, BW)
        assert n <= ARENA_N, n
        QK, n = carve(AR, 0, 6, 640)
        VA, n = carve(AR, n, 6, P)
        AZ, n = carve(AR, n, 4, TOK)
        QT, n = carve(AR, n, 5, TOK)
        TA, n = carve(AR, n, 4, 4 * 320)
        PR, n = carve(AR, n, 2, TOK)
        PT, n = carve(AR, n, 2, TOK)
        AO, n = carve(AR, n, 2, BW)
        GAIN, n = carve(AR, n, 640)
        ROPE, n = carve(AR, n, 2, 4, 32)
        assert n <= ARENA_N, n

        block = stack.enter_context(nc.Block())

        PHASES = []
        for l in range(DEPTH):
            PHASES += [("norm", l), ("hyena", l), ("gla", l), ("attn", l), ("merge", l)]
        PHASES.append(("norm", DEPTH))
        BEFORE = dict(zip(PHASES[1:], PHASES[:-1]))

        def weight_order():
            for l in range(DEPTH):
                for j in range(24):
                    yield l, "ada", j
                for t in HY_TILES + GLA_TILES + ATT_TILES:
                    yield (l, *t)
                for t in GATE_TILES:
                    yield (l, *t)
                for j in range(KD):
                    yield l, "out", j

        ORDER = list(weight_order())
        WHERE = {k: i for i, k in enumerate(ORDER)}

        def barrier(eng, *phase):
            if phase in BEFORE:
                for e in ("pe", "act", "dve", "pool"):
                    if e != c.engine:
                        eng.wait_ge(*c.after("end", e, BEFORE[phase]))

        def prev_conv(l, s, o):
            return (l, s, 0) if o == 1 else (l, streams_of(l)[0], 1)

        def pair_group(nt, g):
            b, u = divmod(g, nt // 2)
            return [(64 * b, 2 * u + i, p, (2 * i + p) * P) for i in range(2) for p in range(2)]

        def att_of(nt, h, t):
            col = (2 * (t % 2) + h // 2) * P
            return ATT[:, (h % 2) * (nt // 2) + t // 2, col:col + P]

        def filter_blocks(s, f):
            if s == "ctx" or f < 2:
                return R[:, 2 * f], R[:, 2 * f + 1]
            return (FW[:, 6], FW[:, 7]) if f == 2 else (R[:, 4], R[:, 5])

        def signal_blocks(s, f, o):
            if s == "ctx":
                return TOKM[:, 0, 4], TOKM[:, 0, 5]
            return R[:, 2 * f], R[:, 2 * f + 1]

        def attn_steps(l):
            return [(s, t, hh) for s in ("lat", "ctx") if s in streams_of(l) for t in range(STREAMS[s][1] // P) for hh in range(8)]

        @block.sync
        def _(sp):
            c.engine = "sp"

            def load(name, dst, src, *key):
                sp.dma_start(dst, src).then_inc(*c.done("load_" + name, *key, by=16))

            load("x", X, d["xT"], 0)
            load("cond", SC[:, :, :], d["cond"])
            load("const", TRI[:, :, :], d["tri"])
            load("const", IDENT[:, :], d["ident"])
            load("const", ONES[:, :, :], d["ones"])
            load("mask", MASK32, d["mask"])
            load("const", DIAG2[:, :], d["diag2"])
            load("const", TCOL, d["tcol"], "all")
            n_w = [0]

            def weights(l, kind, j):
                n = n_w[0]
                assert ORDER[n] == (l, kind, j)
                n_w[0] += 1
                if n >= NSLOT:
                    sp.wait_ge(*c.after("weights_used", n - NSLOT))
                if kind == "ada":
                    src = d["w_ada"][l, j]
                elif kind == "out":
                    src = d["w_out"][l, j]
                else:
                    src = d["w_in"][l, IN_INDEX[kind, j]]
                load(f"slot{n % NSLOT}", RING[:, n % NSLOT], src, n)

            for l in range(DEPTH):
                if l:
                    barrier(sp, "norm", l)
                load("cols", COLS[:, 0:83], d["cols"][l], l)
                for j in range(24):
                    weights(l, "ada", j)
                barrier(sp, "hyena", l)
                load("hy", G, d["G"], l, 0)
                load("hy", FM, d["FM"], l, 1)
                load("hy", C64[0:64], d["c64"][l], l, 2)
                load("hy", EMB[0:33], d["emb"], l, 3)
                load("hy", F12[0:33, 0], d["f1"][l], l, 4)
                load("hy", F12[0:64, 1], d["f2"][l], l, 5)
                load("hy", F3[0:64], d["f3"][l], l, "all")
                for t in HY_TILES:
                    weights(l, *t)
                for s in streams_of(l):
                    for o in range(2):
                        sp.wait_ge(*c.after("filter_rest", l, s, o)) if False else None
                        if (l, s, o) != (l, streams_of(l)[0], 0):
                            sp.wait_ge(*c.after("conv_free", *prev_conv(l, s, o)))
                        load("skip", SKIP[0:1], d["skip"][l, o:o + 1], l, s, o)
                        for r in range(2):
                            if r:
                                sp.wait_ge(*c.after("window_last", l, s, o, 0))
                            load("delta", DEL, d["delta"][2 * o + r:2 * o + r + 1].to_broadcast([P, BW]), l, s, o, r)
                barrier(sp, "gla", l)
                load("gla", WA[0:33], d["wa"][l], l)
                for t in GLA_TILES:
                    weights(l, *t)
                barrier(sp, "attn", l)
                load("attn", GAIN, d["gain"][l:l + 1].to_broadcast([P, 640]), l, 0)
                load("attn", ROPE, d["rope"], l, "all")
                for t in ATT_TILES:
                    weights(l, *t)
                barrier(sp, "merge", l)
                load("x", X, d["xT"] if l == 0 else d["x_mid"], "merge", l)
                for j in range(KD):
                    for b in range(3):
                        weights(l, "m", 3 * j + b)
                    if j >= 2:
                        sp.wait_ge(*c.after("branch_used", l, j - 2))
                    load(f"branch{j % 2}", BRW[:, j % 2], d["w_br"][l, j], l, j)
                for j in range(KD):
                    weights(l, "out", j)
                if l < DEPTH - 1:
                    sp.wait_ge(*c.after("x_new", l, "all"))
                    sp.dma_start(d["x_mid"], X).then_inc(*c.done("store_x", by=16))
                    sp.wait_ge(*c.after("store_x"))
            for k in range(KD):
                sp.wait_ge(*c.after("final", k))
                sp.dma_start(d["out"][k], OUTB[:, k]).then_inc(*c.done("store_out", k, by=16))
            sp.wait_ge(*c.after("store_out", KD - 1))

        @block.tensor
        def _(pe):
            c.engine = "pe"
            n_w = [0]

            def weights(l, kind, j):
                n = n_w[0]
                assert ORDER[n] == (l, kind, j), (n, ORDER[n], l, kind, j)
                n_w[0] += 1
                pe.wait_ge(*c.after(f"load_slot{n % NSLOT}", n))
                return RING[:, n % NSLOT], ("weights_used", n)

            def project(l, kind, j, m=P):
                w, used = weights(l, kind, j)
                ss = streams_for(l, (kind, j))
                for s in ss:
                    off, T = STREAMS[s]
                    out = ps.take(pe, kind, l, j, s)
                    for k in range(KD):
                        mm = pe.matmul(out[0:m, 0:T], w[:, k, 0:m], H[:, k, off:off + T], start=k == 0, stop=k == KD - 1)
                    mm.then_inc(*c.done(kind, l, j, s, also=[used] if s == ss[-1] else []))

            def project_tokens(l, kind, j):
                w, used = weights(l, kind, j)
                ss = streams_for(l, (kind, j))
                for s in ss:
                    off, T = STREAMS[s]
                    out = ps.take(pe, kind, l, j, s)
                    for t in range(T // P):
                        for k in range(KD):
                            mm = pe.matmul(out[:, t * P:(t + 1) * P], H[:, k, off + t * P:off + (t + 1) * P], w[:, k, :],
                                           start=k == 0, stop=k == KD - 1)
                    mm.then_inc(*c.done(kind, l, j, s, also=[used] if s == ss[-1] else []))

            def norm(l, ss):
                outs = {s: ps.take(pe, "ms", l, s) for s in ss}
                for k in range(KD):
                    pe.wait_ge(*c.after("squares", l, k))
                    for s in ss:
                        off, T = STREAMS[s]
                        mm = pe.matmul(outs[s][:, 0:T], ONES[:, 0, :], SQ[:, k % 2, off:off + T], start=k == 0, stop=k == KD - 1)
                        mm.then_inc(*c.done("ms", l, s, k, also=([("squares_used", l, k)] if s == ss[-1] else []) +
                                            ([("ms", l, s)] if k == KD - 1 else [])))

            def adaln(l):
                if l == 0:
                    pe.wait_ge(*c.after("cond_silu"))
                out = ps.take(pe, "ada", l)
                for j in range(24):
                    w, used = weights(l, "ada", j)
                    for k in range(KD):
                        mm = pe.matmul(out[:, 2 * j:2 * j + 2], w[:, k, :], SC[:, k, :], start=k == 0, stop=k == KD - 1)
                    mm.then_inc(*c.done("ada", l, j, also=[used] + ([("ada", l)] if j == 23 else [])))

            def hyena(l):
                pe.wait_ge(*c.after("load_hy", l, "all"))
                for s in streams_of(l):
                    T = STREAMS[s][1]
                    for layer in range(2):
                        for h in range(2 * T // BW):
                            out = ps.take(pe, "ffn", l, s, layer, h)
                            at = (0 if s == "lat" else 2 * LAT) + h * BW
                            if layer == 0:
                                mm = pe.matmul(out[0:64, :], F12[0:33, 0], EMB[0:33, at:at + BW], start=True, stop=True)
                            else:
                                pe.wait_ge(*c.after("sine", l, s, 0))
                                mm = pe.matmul(out[0:64, :], F12[0:64, 1], H2[0:64, at:at + BW], start=True, stop=True)
                            mm.then_inc(*c.done("ffn", l, s, layer, h))
                pe.wait_ge(*c.after("h", l, "all"))
                for which in range(2):
                    for j in range(4):
                        project(l, "u", 4 * which + j)
                    for s in streams_of(l):
                        off, T = STREAMS[s]
                        pe.wait_ge(*c.after("short_conv", l, 4 * which + 3, s))
                        for t in range(T // P):
                            out = ps.take(pe, "uT", l, which, s, t)
                            for j in range(4):
                                mm = pe.transpose(out[:, j * P:(j + 1) * P], UD[:, j, off + t * P:off + (t + 1) * P], IDENT[:, :])
                            mm.then_inc(*c.done("uT", l, which, s, t))
                for j in range(8, 12):
                    project(l, "u", j)
                for j in range(4):
                    project(l, "hz", j)
                for s in streams_of(l):
                    off, T = STREAMS[s]
                    nt, nf = T // P, FACTORS[s]
                    for o in range(2):
                        pe.wait_ge(*c.after("sine", l, s, 1))
                        base = 0 if s == "lat" else 2 * LAT

                        def magnitudes(r, m):
                            pe.wait_ge(*c.after("magnitude", l, s, o, r * nt + m))
                            mm = pe.matmul(total, ONES[:, 2, :], TT[:, 2 + m % 1], start=m == 0, stop=m == nt - 1)
                            mm.then_inc(*c.done("tap_sum", l, s, o, r, m, also=[("tap_sum", l, s, o, r)] if m == nt - 1 else []))

                        for r in range(2):
                            total = ps.take(pe, "tap_sum", l, s, o, r)
                            for m in range(nt):
                                out = ps.take(pe, "taps", l, s, o, r * nt + m)
                                at = base + (r * nt + m) * P
                                mm = pe.matmul(out, H2[0:64, at:at + P], F3[0:64, 2 * o + r], start=True, stop=True)
                                mm.then_inc(*c.done("taps", l, s, o, r * nt + m))
                                if m:
                                    magnitudes(r, m - 1)
                            magnitudes(r, nt - 1)
                        pe.wait_ge(*c.after("filter_parts", l, s, o))
                        for f in range(nf):
                            blocks = filter_blocks(s, f)
                            for p in range(2):
                                out = ps.take(pe, "fdft", l, s, o, f, p)
                                for b in range(2):
                                    mm = pe.matmul(out, FM[:, 4 * f + 2 * b + p], blocks[b], start=b == 0, stop=b == 1)
                                mm.then_inc(*c.done("fdft", l, s, o, f, p))
                        pe.wait_ge(*c.after("signal_parts", l, s, o))
                        for f in range(nf):
                            blocks = signal_blocks(s, f, o)
                            for p in range(2):
                                out = ps.take(pe, "zdft", l, s, o, f, p)
                                for b in range(2):
                                    mm = pe.matmul(out, FM[:, 4 * f + 2 * b + p], blocks[b], start=b == 0, stop=b == 1)
                                mm.then_inc(*c.done("zdft", l, s, o, f, p))
                        pe.wait_ge(*c.after("spectrum", l, s, o))
                        if o == 0:
                            for m in range(nt):
                                out = ps.take(pe, "conv", l, s, o, m)
                                for q in range(2 * nf):
                                    mm = pe.matmul(out, G[:, q, m * P:(m + 1) * P], Y[:, q], start=q == 0, stop=q == 2 * nf - 1)
                                mm.then_inc(*c.done("conv", l, s, o, m))
                        else:
                            for m in range(4):
                                out = ps.take(pe, "conv", l, s, o, m)
                                for q in range(2 * nf):
                                    mm = pe.matmul(out[:, 0:T], Y[:, q, m * P:(m + 1) * P], G[:, q, 0:T], start=q == 0, stop=q == 2 * nf - 1)
                                mm.then_inc(*c.done("conv", l, s, o, m))

            def gla(l):
                for t in GLA_TILES:
                    if t[0] == "ga":
                        project(l, *t, m=32)
                    elif t[0] == "gv":
                        project_tokens(l, *t)
                    else:
                        project(l, *t)
                for s in ("ctx", "lat"):
                    off, T = STREAMS[s]
                    nt = T // P
                    full = s in streams_of(l)
                    pe.wait_ge(*c.after("load_gla", l))
                    pe.wait_ge(*c.after("rank", l, s))
                    for t in range(nt):
                        out = ps.take(pe, "gpre", l, s, t)
                        pe.matmul(out, GA[0:33, off + t * P:off + (t + 1) * P], WA[0:33], start=True, stop=True)\
                          .then_inc(*c.done("gpre", l, s, t))
                    for r in range(2):
                        for p in range(2):
                            out = ps.take(pe, "cum", l, s, r, p)
                            for t in range(nt):
                                pe.wait_ge(*c.after("log_decay", l, s, t))
                                mm = pe.matmul(out[:, t * P:(t + 1) * P], GG[:, t, r * 256 + p * P:r * 256 + (p + 1) * P],
                                               TRI[:, r, :], start=True, stop=True)
                            mm.then_inc(*c.done("cum", l, s, r, p))
                    if full:
                        pe.wait_ge(*c.after("qk_ready", l, s))
                        for t in range(nt):
                            out = ps.take(pe, "pairs", l, s, -1, t)
                            for b, chunk, p, col in pair_group(nt, t):
                                cols = slice(off + chunk * P, off + (chunk + 1) * P)
                                mm = pe.matmul(out[:, col:col + P], GK[b:b + 64, p, cols], GQ[b:b + 64, p, cols], start=True, stop=True)
                            mm.then_inc(*c.done("pairs", l, s, -1, t))
                    for r in range(2):
                        for p in range(2):
                            pe.wait_ge(*c.after("k_decayed", l, s))
                            out = ps.take(pe, "kT", l, s, r, p)
                            for t in range(nt):
                                mm = pe.transpose(out[:, t * P:(t + 1) * P], KH[:, r, p, t * P:(t + 1) * P], IDENT[:, :])
                            mm.then_inc(*c.done("kT", l, s, r, p))
                    for r in range(2):
                        for i in range(nt if s == "ctx" else nt - 1):
                            t = i if r == 0 else nt - 1 - i
                            pe.wait_ge(*c.after("k_tokens", l, s, r, 1))
                            out = ps.take(pe, "kv", l, s, r, i)
                            for h in range(4):
                                b, p = 64 * (h % 2), h // 2
                                mm = pe.matmul(out[b:b + 64, p * P:(p + 1) * P], KT[:, r, p, t * P + b:t * P + b + 64],
                                               GV[:, off // P + t, h * P:(h + 1) * P], start=True, stop=True)
                            mm.then_inc(*c.done("kv", l, s, r, i))
                    if not full:
                        continue
                    for v in range(len(LEVELS)):
                        pe.wait_ge(*c.after("level_q", l, s, v))
                        pe.wait_ge(*c.after("level_k", l, s, v))
                        for t in range(nt):
                            out = ps.take(pe, "pairs", l, s, v, t)
                            for b, chunk, p, col in pair_group(nt, t):
                                mm = pe.matmul(out[:, col:col + P], EL[b:b + 64, v % 2, p, T + chunk * P:T + (chunk + 1) * P],
                                               EL[b:b + 64, v % 2, p, chunk * P:(chunk + 1) * P], start=True, stop=True)
                            mm.then_inc(*c.done("pairs", l, s, v, t))
                    pe.wait_ge(*c.after("pairs_all", l, s))
                    pe.wait_ge(*c.after("state", l, s, 1, nt - 2 if s == "lat" else nt - 1, 1))
                    for h in range(4):
                        b, p = 64 * (h % 2), h // 2
                        out = ps.take(pe, "o", l, s, h)
                        for t in range(nt):
                            cols = slice(t * P, (t + 1) * P)
                            first = 0 if s == "ctx" else 2
                            pe.matmul(out[:, cols], GV[:, off // P + t, h * P:(h + 1) * P], att_of(nt, h, t), start=True, stop=False)
                            for r in range(2):
                                at = first + (t if r == 0 else nt - 1 - t)
                                mm = pe.matmul(out[:, cols], ST[b:b + 64, r, p, at * P:(at + 1) * P], QH[b:b + 64, r, p, cols],
                                               start=False, stop=r == 1)
                        mm.then_inc(*c.done("o", l, s, h))
                        if h:
                            gla_ms(l, s, h - 1, T)
                    gla_ms(l, s, 3, T)

            def gla_ms(l, s, h, T):
                pe.wait_ge(*c.after("o_sq", l, s, h))
                out = ps.take(pe, "oms", l, s, h)
                pe.matmul(out[:, 0:T], ONES[:, 1, :], OS[:, 2 + h % 2, 0:T], start=True, stop=True).then_inc(*c.done("oms", l, s, h))

            def attn(l):
                for t in ATT_TILES:
                    (project if t[0] == "az" else project_tokens)(l, *t)
                for s in ("lat", "ctx"):
                    off, T = STREAMS[s]
                    pe.wait_ge(*c.after("qk_normed", l, s))
                    for j in ([4] if s not in streams_of(l) else [4, 0, 1, 2, 3]):
                        out = ps.take(pe, "qkT", l, s, j)
                        for t in range(T // P):
                            mm = pe.transpose(out[:, t * P:(t + 1) * P], QK[:, off // P + t, j * P:(j + 1) * P], IDENT[:, :])
                        mm.then_inc(*c.done("qkT", l, s, j))
                steps = attn_steps(l)

                def scores(i):
                    s, t, hh = steps[i]
                    off = STREAMS[s][0] + t * P
                    b, j = 64 * (hh % 2), hh // 2
                    if i == 0:
                        for s2 in ("lat", "ctx"):
                            pe.wait_ge(*c.after("qkT_kept", l, s2, 4))
                    if t == 0 and hh == 0:
                        pe.wait_ge(*c.after("qkT_kept", l, s, 3))
                    out = ps.take(pe, "score", l, s, t, hh, n=2, at=2 * (i % 2))
                    q = QT[b:b + 64, j, off:off + P]
                    if s == "lat":
                        pe.matmul(out[:, 0:512], q, QT[b:b + 64, 4, 0:512], start=True, stop=True)
                        mm = pe.matmul(out[:, 512:768], q, QT[b:b + 64, 4, 512:768], start=True, stop=True)
                    else:
                        mm = pe.matmul(out[:, 0:256], q, QT[b:b + 64, 4, 512:768], start=True, stop=True)
                    mm.then_inc(*c.done("score", l, s, t, hh))

                def transposes(i):
                    s, t, hh = steps[i]
                    pe.wait_ge(*c.after("prob", l, s, t, hh))
                    out = ps.take(pe, "probT", l, s, t, hh, n=2, at=4)
                    for k in range(6 if s == "lat" else 2):
                        mm = pe.transpose(out[:, k * P:(k + 1) * P], PR[:, i % 2, k * P:(k + 1) * P], IDENT[:, :])
                    mm.then_inc(*c.done("probT", l, s, t, hh))

                def values(i):
                    s, t, hh = steps[i]
                    pe.wait_ge(*c.after("probT_kept", l, s, t, hh))
                    if hh == 0:
                        values.out = ps.take(pe, "ao", l, s, t, at=6)
                    tiles = range(6) if s == "lat" else range(4, 6)
                    for k in tiles:
                        mm = pe.matmul(values.out[:, hh * 64:(hh + 1) * 64], PT[:, i % 2, (k - tiles[0]) * P:(k - tiles[0] + 1) * P],
                                       VA[:, k, 64 * (hh % 2):64 * (hh % 2) + 64], start=k == tiles[0], stop=k == tiles[-1])
                    mm.then_inc(*c.done("ao", l, s, t, hh, also=[("ao", l, s, t)] if hh == 7 else []))

                def out_transposes(s, t):
                    pe.wait_ge(*c.after("ao_kept", l, s, t))
                    out = ps.take(pe, "aoT", l, s, t, at=7)
                    for j in range(4):
                        mm = pe.transpose(out[:, j * P:(j + 1) * P], AO[:, t % 2, j * P:(j + 1) * P], IDENT[:, :])
                    mm.then_inc(*c.done("aoT", l, s, t))

                scores(0)
                scores(1)
                for i in range(len(steps)):
                    transposes(i)
                    if i + 2 < len(steps):
                        scores(i + 2)
                    values(i)
                    if i % 8 == 1 and i > 8:
                        out_transposes(*steps[i - 8][:2])
                out_transposes(*steps[-1][:2])

            def merge(l):
                ss = streams_for(l, ("m", 0))
                for j in range(KD):
                    for b in range(3):
                        project(l, "m", 3 * j + b)
                    pe.wait_ge(*c.after(f"load_branch{j % 2}", l, j))
                    for b in range(3):
                        for s in ss:
                            off, T = STREAMS[s]
                            out = ps.take(pe, "branch", l, j, b, s)
                            for k in range(4):
                                mm = pe.matmul(out[:, 0:T], BRW[:, j % 2, 4 * b + k, :], YBT[:, 4 * b + k, off:off + T], start=k == 0, stop=k == 3)
                            mm.then_inc(*c.done("branch", l, j, b, s, also=[("branch_used", l, j)] if b == 2 and s == ss[-1] else []))
                for j in range(KD):
                    pe.wait_ge(*c.after("merged", l, "all"))
                    w, used = weights(l, "out", j)
                    for s in ss:
                        off, T = STREAMS[s]
                        out = ps.take(pe, "out", l, j, s)
                        for k in range(KD):
                            mm = pe.matmul(out[:, 0:T], w[:, k, :], YM[:, k, off:off + T], start=k == 0, stop=k == KD - 1)
                        mm.then_inc(*c.done("out", l, j, s, also=[used] if s == ss[-1] else []))

            pe.wait_ge(*c.after("load_const", "all"))
            for l in range(DEPTH):
                adaln(l)
                norm(l, ["lat", "ctx"])
                c.phase_end(("norm", l))
                hyena(l)
                c.phase_end(("hyena", l))
                gla(l)
                c.phase_end(("gla", l))
                attn(l)
                c.phase_end(("attn", l))
                merge(l)
                c.phase_end(("merge", l))
            norm(DEPTH, ["lat"])
            c.phase_end(("norm", DEPTH))

        @block.scalar
        def _(act):
            c.engine = "act"
            chain = [0]

            def link(ins):
                ins.then_inc(*c.done("act_chain", chain[0]))
                act.wait_ge(*c.after("act_chain", chain[0]))
                chain[0] += 1

            def norm(l, ss):
                off, T = (0, TOK) if len(ss) == 2 else (0, LAT)
                if l == 0:
                    act.wait_ge(*c.after("load_cond"))
                    link(act.activation(RS[:, 0:16], SC[:, :, :].rearrange("p a b -> p (a b)"), ACT.Silu))
                    act.activation(SC[:, :, :].rearrange("p a b -> p (a b)"), RS[:, 0:16], ACT.Copy).then_inc(*c.done("cond_silu"))
                    act.wait_ge(*c.after("load_x", 0))
                    act.wait_ge(*c.after("load_cols", 0))
                else:
                    barrier(act, "norm", l)
                for k in range(KD):
                    if k >= 2:
                        act.wait_ge(*c.after("squares_used", l, k - 2))
                    act.activation(SQ[:, k % 2, off:off + T], X[:, k, off:off + T], ACT.Square).then_inc(*c.done("squares", l, k))
                for s in ss:
                    o, t = STREAMS[s]
                    act.wait_ge(*c.after("ms", l, s))
                    act.wait_ge(*c.after("squares_used", l, KD - 1))
                    link(act.activation(SQ[:, 0, o:o + t], ps.of("ms", l, s)[:, 0:t], ACT.Ln, bias=EPSC))
                    act.activation(RS[:, o:o + t], SQ[:, 0, o:o + t], ACT.Exp, scale=-0.5).then_inc(
                        *c.done("rms", l, s, also=[("freed", "ms", l, s)]))

            def hyena(l):
                barrier(act, "hyena", l)
                for s in streams_of(l):
                    T2 = 2 * STREAMS[s][1]
                    base = 0 if s == "lat" else 2 * LAT
                    for layer in range(2):
                        act.wait_ge(*c.after("reduced", l, s, layer))
                        act.activation(H2[0:64, base:base + T2], HX[0:64, 2, 0:T2], ACT.Sin).then_inc(*c.done("sine", l, s, layer))
                act.wait_ge(*c.after("sine", l, streams_of(l)[-1], 1))
                for which in range(2):
                    for j in range(4):
                        conv_centre(l, 4 * which + j)
                    for s in streams_of(l):
                        o = STREAMS[s][0] // P
                        for t in range(STREAMS[s][1] // P):
                            act.wait_ge(*c.after("uT", l, which, s, t))
                            act.activation(TOKM[:, which, o + t], ps.of("uT", l, which, s, t), ACT.Copy).then_inc(
                                *c.done("u_tokens", l, which, s, t, also=[("freed", "uT", l, which, s, t)]))
                for j in range(8, 12):
                    conv_centre(l, j)
                for j in range(4):
                    for s in streams_for(l, ("hz", j)):
                        off, T = STREAMS[s]
                        n = 2 * j + (s == "ctx")
                        if n >= 2 and not (l == DEPTH - 1 and j < 1):
                            act.wait_ge(*c.after("z_used", l, j - 1, s))
                        act.wait_ge(*c.after("hz", l, j, s))
                        act.activation(TT[:, n % 2, 0:T], ps.of("hz", l, j, s)[:, 0:T], ACT.Silu).then_inc(
                            *c.done("hz_silu", l, j, s, also=[("freed", "hz", l, j, s)]))
                for s in streams_of(l):
                    T = STREAMS[s][1]
                    nt, nf = T // P, FACTORS[s]
                    tbase = 0 if s == "lat" else 8
                    for o in range(2):
                        if (s, o) == (streams_of(l)[0], 0):
                            for s2 in streams_of(l):
                                act.wait_ge(*c.after("z_used", l, 3, s2))
                        else:
                            act.wait_ge(*c.after("conv_free", *prev_conv(l, s, o)))
                        for r in range(2):
                            act.wait_ge(*c.after("load_delta", l, s, o, r))
                            for m in range(nt):
                                n = r * nt + m
                                if n >= 2:
                                    act.wait_ge(*c.after("taps_windowed", l, s, o, n - 2))
                                act.activation(TT[:, n % 2], DEL, ACT.Exp, scale=TCOL[:, tbase + n:tbase + n + 1]).then_inc(
                                    *c.done("window", l, s, o, n, also=[("window_last", l, s, o, r)] if m == nt - 1 else []))
                                act.wait_ge(*c.after("taps_windowed", l, s, o, n))
                                if m:
                                    act.wait_ge(*c.after("tap_sum", l, s, o, r, m - 1))
                                act.activation(TT[:, 2], FW[:, n], ACT.Abs).then_inc(*c.done("magnitude", l, s, o, n))
                            act.wait_ge(*c.after("tap_sum", l, s, o, r))
                            link(act.activation(RN[:, r], ps.of("tap_sum", l, s, o, r), ACT.Ln, scale=float(2 * T)))
                            act.activation(RN[:, r], RN[:, r], ACT.Exp, scale=-1.0).then_inc(
                                *c.done("tap_norm", l, s, o, r, also=[("freed", "tap_sum", l, s, o, r)]))
                        for f in range(nf):
                            for p in range(2):
                                act.wait_ge(*c.after("fdft", l, s, o, f, p))
                                src = ps.of("fdft", l, s, o, f, p)
                                if f == 0 and p == 1:
                                    link(act.activation(FH[:, 1], src, ACT.Copy, scale=NOT0))
                                    act.activation(FH[0:1, 8], src[0:1], ACT.Copy).then_inc(
                                        *c.done("filter_spec", l, s, o, f, p, also=[("freed", "fdft", l, s, o, f, p)]))
                                    continue
                                if f == 0:
                                    link(act.activation(FH[:, 8], src, ACT.Copy))
                                act.activation(FH[:, 2 * f + p], src, ACT.Copy).then_inc(
                                    *c.done("filter_spec", l, s, o, f, p, also=[("freed", "fdft", l, s, o, f, p)]))

            def conv_centre(l, j):
                for s in streams_for(l, ("u", j)):
                    off, T = STREAMS[s]
                    act.wait_ge(*c.after("u", l, j, s))
                    if 4 <= j < 8:
                        act.wait_ge(*c.after("uT", l, 0, s, T // P - 1))
                    dst = UD[:, j % 4, off:off + T] if j < 8 else YBT[:, j, off:off + T]
                    act.activation(dst, ps.of("u", l, j, s)[:, 0:T], ACT.Identity, bias=CONVB[:, j:j + 1],
                                   scale=CONVW[:, 12 + j:13 + j]).then_inc(*c.done("centre", l, j, s))

            def gla(l):
                barrier(act, "gla", l)
                for kind, j in GLA_TILES:
                    if kind in ("gq", "gk", "gz"):
                        dst = {"gq": GQ, "gk": GK, "gz": GZ}[kind]
                        for s in streams_for(l, (kind, j)):
                            off, T = STREAMS[s]
                            act.wait_ge(*c.after(kind, l, j, s))
                            act.activation(dst[:, j, off:off + T], ps.of(kind, l, j, s)[:, 0:T],
                                           ACT.Silu if kind == "gz" else ACT.Copy,
                                           scale=0.125 if kind == "gq" else 1.0).then_inc(
                                *c.done(kind + "_kept", l, j, s, also=[("freed", kind, l, j, s)] +
                                        ([("qk_ready", l, s)] if (kind, j) == ("gq", 1) else [])))
                for s in ("ctx", "lat"):
                    T = STREAMS[s][1]
                    nt = T // P
                    full = s in streams_of(l)
                    for t in range(nt):
                        act.wait_ge(*c.after("gpre", l, s, t))
                        if t >= 2:
                            act.wait_ge(*c.after("log_decay", l, s, t - 2))
                        elif s == "lat":
                            act.wait_ge(*c.after("log_decay", l, "ctx", t))
                        link(act.activation(GT[:, t % 2], ps.of("gpre", l, s, t), ACT.Abs))
                        link(act.activation(GT[:, t % 2], GT[:, t % 2], ACT.Exp, scale=-1.0))
                        act.activation(GT[:, t % 2], GT[:, t % 2], ACT.Ln, bias=1.0).then_inc(*c.done("softplus", l, s, t))
                    if s == "lat" and streams_of(l)[0] == "ctx":
                        act.wait_ge(*c.after("k_tokens", l, "ctx", 1, 1))
                    for r in range(2):
                        for p in range(2):
                            act.wait_ge(*c.after("cum", l, s, r, p))
                            act.activation(B[:, r, p, 0:T], ps.of("cum", l, s, r, p)[:, 0:T], ACT.Copy).then_inc(
                                *c.done("cum_kept", l, s, r, p, also=[("freed", "cum", l, s, r, p)]))
                    if full or True:
                        act.wait_ge(*c.after("cum_kept", l, s, 1, 1))
                        if s == "lat" and "ctx" in streams_of(l):
                            act.wait_ge(*c.after("oms", l, "ctx", 3))
                        for r in range(2):
                            last = act.activation(QH[:, r, :, 0:T], B[:, r, :, 0:T], ACT.Exp)
                            last.then_inc(*c.done("q_decay", l, s, r))
                    act.wait_ge(*c.after("k_offsets", l, s))
                    for r in range(2):
                        act.activation(KH[:, r, :, 0:T], KH[:, r, :, 0:T], ACT.Exp).then_inc(*c.done("k_decay", l, s, r))
                    for r in range(2):
                        for p in range(2):
                            act.wait_ge(*c.after("kT", l, s, r, p))
                            if s == "lat":
                                act.wait_ge(*c.after("kv", l, "ctx", 1, 1))
                            act.activation(KT[:, r, p, 0:T], ps.of("kT", l, s, r, p)[:, 0:T], ACT.Copy).then_inc(
                                *c.done("k_tokens", l, s, r, p, also=[("freed", "kT", l, s, r, p)]))
                    if not full:
                        continue
                    for v in range(len(LEVELS)):
                        act.wait_ge(*c.after("level_args", l, s, v))
                        act.activation(EL[:, v % 2, :, 0:2 * T], EL[:, v % 2, :, 0:2 * T], ACT.Exp).then_inc(*c.done("level_exp", l, s, v))
                    for h in range(4):
                        act.wait_ge(*c.after("o", l, s, h))
                        act.wait_ge(*c.after("kT", l, s, 1, 1))
                        if h >= 2:
                            act.wait_ge(*c.after("gla_y", l, s, h - 2))
                        elif s == "lat" and "ctx" in streams_of(l):
                            act.wait_ge(*c.after("gla_y", l, "ctx", h + 2))
                        act.activation(OS[:, h % 2, 0:T], ps.of("o", l, s, h)[:, 0:T], ACT.Copy).then_inc(*c.done("o_kept", l, s, h))
                        act.activation(OS[:, 2 + h % 2, 0:T], ps.of("o", l, s, h)[:, 0:T], ACT.Square).then_inc(
                            *c.done("o_sq", l, s, h, also=[("freed", "o", l, s, h)]))
                        if h:
                            gla_rms(l, s, h - 1, T)
                    gla_rms(l, s, 3, T)

            def gla_rms(l, s, h, T):
                act.wait_ge(*c.after("oms", l, s, h))
                link(act.activation(OS[:, 4 + h % 2, 0:T], ps.of("oms", l, s, h)[:, 0:T], ACT.Ln, bias=EPSC))
                act.activation(OS[:, 4 + h % 2, 0:T], OS[:, 4 + h % 2, 0:T], ACT.Exp, scale=-0.5).then_inc(
                    *c.done("o_rms", l, s, h, also=[("freed", "oms", l, s, h)]))

            def attn(l):
                barrier(act, "attn", l)
                for kind, j in ATT_TILES:
                    if kind == "az":
                        for s in streams_for(l, (kind, j)):
                            off, T = STREAMS[s]
                            act.wait_ge(*c.after(kind, l, j, s))
                            act.activation(AZ[:, j, off:off + T], ps.of(kind, l, j, s)[:, 0:T], ACT.Silu).then_inc(
                                *c.done("az_kept", l, j, s, also=[("freed", kind, l, j, s)]))
                for s in ("lat", "ctx"):
                    nh = (STREAMS[s][1] // P) * 10
                    act.wait_ge(*c.after("head_ms", l, s))
                    link(act.activation(MSQ[:, 0:nh], MSQ[:, 0:nh], ACT.Ln, scale=1.0 / 64, bias=EPSC))
                    act.activation(MSQ[:, 0:nh], MSQ[:, 0:nh], ACT.Exp, scale=-0.5).then_inc(*c.done("head_rms", l, s))
                for s in ("lat", "ctx"):
                    off, T = STREAMS[s]
                    for j in ([4] if s not in streams_of(l) else [4, 0, 1, 2, 3]):
                        act.wait_ge(*c.after("qkT", l, s, j))
                        act.activation(QT[:, j, off:off + T], ps.of("qkT", l, s, j)[:, 0:T], ACT.Copy).then_inc(
                            *c.done("qkT_kept", l, s, j, also=[("freed", "qkT", l, s, j)]))
                steps = attn_steps(l)

                def keep(i):
                    s, t, hh = steps[i]
                    N = 768 if s == "lat" else 256
                    act.wait_ge(*c.after("probT", l, s, t, hh))
                    if i >= 2:
                        act.wait_ge(*c.after("ao", l, *steps[i - 2]))
                    act.activation(PT[:, i % 2, 0:N], ps.of("probT", l, s, t, hh)[:, 0:N], ACT.Copy).then_inc(
                        *c.done("probT_kept", l, s, t, hh, also=[("freed", "probT", l, s, t, hh)]))

                for i, (s, t, hh) in enumerate(steps):
                    N = 768 if s == "lat" else 256
                    col = 8 * (t + (4 if s == "ctx" else 0)) + hh
                    act.wait_ge(*c.after("row_max", l, s, t, hh))
                    if i >= 2:
                        act.wait_ge(*c.after("probT", l, *steps[i - 2]))
                    act.activation(PR[:, i % 2, 0:N], ps.of("score", l, s, t, hh)[:, 0:N], ACT.Exp, bias=NMAX[:, col:col + 1],
                                   accum_out=SUMS[:, col:col + 1]).then_inc(
                        *c.done("prob", l, s, t, hh, also=[("freed", "score", l, s, t, hh)]))
                    if i and (i - 1) % 2 == 0:
                        keep(i - 1)
                if (len(steps) - 1) % 2 == 0:
                    keep(len(steps) - 1)

            def merge(l):
                barrier(act, "merge", l)
                for j in range(KD):
                    for b in range(3):
                        for s in streams_for(l, ("m", 0)):
                            off, T = STREAMS[s]
                            act.wait_ge(*c.after("m", l, 3 * j + b, s))
                            if j >= 2:
                                act.wait_ge(*c.after("gated", l, j - 2, b, s))
                            act.activation(MG[:, j % 2, b, off:off + T], ps.of("m", l, 3 * j + b, s)[:, 0:T], ACT.Sigmoid).then_inc(
                                *c.done("gate", l, j, b, s, also=[("freed", "m", l, 3 * j + b, s)]))

            for l in range(DEPTH):
                norm(l, ["lat", "ctx"])
                c.phase_end(("norm", l))
                hyena(l)
                c.phase_end(("hyena", l))
                gla(l)
                c.phase_end(("gla", l))
                attn(l)
                c.phase_end(("attn", l))
                merge(l)
                c.phase_end(("merge", l))
            norm(DEPTH, ["lat"])
            c.phase_end(("norm", DEPTH))

        @block.vector
        def _(dve):
            c.engine = "dve"
            chain = [0]

            def link(ins):
                ins.then_inc(*c.done("dve_chain", chain[0]))
                dve.wait_ge(*c.after("dve_chain", chain[0]))
                chain[0] += 1

            def norm(l, ss):
                if l == 0:
                    dve.wait_ge(*c.after("load_mask"))
                    dve.tensor_copy(MASK[:, :, :], MASK32).then_inc(*c.done("mask_kept"))
                if l < DEPTH:
                    dve.wait_ge(*c.after("load_cols", l))
                    dve.wait_ge(*c.after("ada", l))
                    pa = ps.of("ada", l)[:, 0:48].rearrange("p (a b) -> p a b", b=2)
                    link(dve.tensor_tensor(ADA[:, :, :], pa, B_ADA.unsqueeze(2).to_broadcast([P, 24, 2]), ALU.add))
                    dve.tensor_scalar(ADA[:, 8:16, :], ADA[:, 8:16, :], 1.0, None, ALU.add).then_inc(
                        *c.done("adaln", l, also=[("freed", "ada", l)]))
                    dve.wait_ge(*c.after("adaln", l))
                if l:
                    barrier(dve, "norm", l)
                for s in ss:
                    off, T = STREAMS[s]
                    e = 0 if s == "lat" else 1
                    dve.wait_ge(*c.after("rms", l, s))
                    for k in range(KD):
                        x, rs = X[:, k, off:off + T], RS[:, off:off + T]
                        if l == DEPTH:
                            dve.scalar_tensor_tensor(OUTB[:, k], x, FINALN[:, k:k + 1], rs, ALU.mult, ALU.mult).then_inc(
                                *c.done("final", k))
                        else:
                            h = H[:, k, off:off + T]
                            dve.scalar_tensor_tensor(h, x, ADA[:, 8 + k, e:e + 1], rs, ALU.mult, ALU.mult).then_inc(
                                *c.done("h_scaled", l, s, k))
                if l == DEPTH:
                    return
                for s in ss:
                    off, T = STREAMS[s]
                    e = 0 if s == "lat" else 1
                    for k in range(KD):
                        h = H[:, k, off:off + T]
                        dve.wait_ge(*c.after("h_scaled", l, s, k))
                        dve.tensor_scalar(h, h, ADA[:, k, e:e + 1], None, ALU.add).then_inc(
                            *c.done("h", l, s, k, also=[("h", l, "all")] if (s, k) == (ss[-1], KD - 1) else []))

            def conv_sides(l, j):
                for s in streams_for(l, ("u", j)):
                    off, T = STREAMS[s]
                    dst = UD[:, j % 4, off:off + T] if j < 8 else YBT[:, j, off:off + T]
                    u = ps.of("u", l, j, s)
                    dve.wait_ge(*c.after("centre", l, j, s))
                    link(dve.scalar_tensor_tensor(dst[:, 1:T], u[:, 0:T - 1], CONVW[:, j:j + 1], dst[:, 1:T], ALU.mult, ALU.add))
                    dve.scalar_tensor_tensor(dst[:, 0:T - 1], u[:, 1:T], CONVW[:, 24 + j:25 + j], dst[:, 0:T - 1], ALU.mult, ALU.add)\
                       .then_inc(*c.done("short_conv", l, j, s, also=[("freed", "u", l, j, s)]))

            def hyena(l):
                barrier(dve, "hyena", l)
                dve.wait_ge(*c.after("load_hy", l, "all"))
                for s in streams_of(l):
                    T2 = 2 * STREAMS[s][1]
                    for layer in range(2):
                        if (s, layer) != (streams_of(l)[0], 0):
                            dve.wait_ge(*c.after("sine", l, *((s, 0) if layer else (streams_of(l)[0], 1))))
                        for h in range(T2 // BW):
                            dve.wait_ge(*c.after("ffn", l, s, layer, h))
                            dve.tensor_scalar(HX[0:64, 0, h * BW:(h + 1) * BW], ps.of("ffn", l, s, layer, h)[0:64],
                                              C64[0:64, 2 * layer:2 * layer + 1], C64[0:64, 2 * layer + 1:2 * layer + 2],
                                              ALU.add, ALU.mult).then_inc(
                                *c.done("phase", l, s, layer, h, also=[("freed", "ffn", l, s, layer, h)]))
                        dve.wait_ge(*c.after("phase", l, s, layer, T2 // BW - 1))
                        x, k, r = (HX[0:64, i, 0:T2] for i in range(3))
                        link(dve.tensor_scalar(k, x, 1.0 / (2 * math.pi), ROUND_MAGIC, ALU.mult, ALU.add))
                        link(dve.tensor_scalar(k, k, ROUND_MAGIC, None, ALU.subtract))
                        link(dve.scalar_tensor_tensor(r, k, -TWO_PI_1, x, ALU.mult, ALU.add))
                        link(dve.scalar_tensor_tensor(r, k, -TWO_PI_2, r, ALU.mult, ALU.add))
                        link(dve.scalar_tensor_tensor(r, k, -TWO_PI_3, r, ALU.mult, ALU.add))
                        dve.tensor_scalar(r, r, -PI_BELOW, PI_BELOW, ALU.max, ALU.min).then_inc(*c.done("reduced", l, s, layer))
                for j in range(12):
                    conv_sides(l, j)
                for s in streams_of(l):
                    T = STREAMS[s][1]
                    nt, nf = T // P, FACTORS[s]
                    ot = STREAMS[s][0] // P
                    for o in range(2):
                        if (s, o) != (streams_of(l)[0], 0):
                            dve.wait_ge(*c.after("conv_free", *prev_conv(l, s, o)))
                        for r in range(2):
                            for m in range(nt):
                                n = r * nt + m
                                dve.wait_ge(*c.after("taps", l, s, o, n))
                                dve.wait_ge(*c.after("window", l, s, o, n))
                                dve.scalar_tensor_tensor(FW[:, n], TT[:, n % 2], 0.05, ps.of("taps", l, s, o, n), ALU.add, ALU.mult)\
                                   .then_inc(*c.done("taps_windowed", l, s, o, n, also=[("freed", "taps", l, s, o, n)]))
                            dve.wait_ge(*c.after("tap_norm", l, s, o, r))
                            for m in range(nt):
                                n = r * nt + m
                                ins = dve.tensor_tensor(FW[:, n], FW[:, n], RN[:, r], ALU.mult)
                                ins.then_inc(*c.done("taps_normed", l, s, o, n))
                            dve.wait_ge(*c.after("taps_normed", l, s, o, (r + 1) * nt - 1))
                        dve.wait_ge(*c.after("load_skip", l, s, o))
                        link(dve.scalar_tensor_tensor(FW[0:1, 0], SKIP[0:1], 1.0 / (2 * T), FW[0:1, 0], ALU.mult, ALU.add))
                        link(dve.memset(FW[0:1, nt], 0.0))
                        if s == "ctx":
                            for m in range(2):
                                dve.tensor_tensor(R[:, m], FW[:, m], FW[:, m + 2], ALU.add).then_inc(*c.done("parts", l, s, o, m))
                                last = dve.tensor_tensor(R[:, 2 + m], FW[:, m], FW[:, m + 2], ALU.subtract)
                                last.then_inc(*c.done("parts", l, s, o, 2 + m, also=[("filter_parts", l, s, o)] if m == 1 else []))
                        else:
                            for m in range(4):
                                dve.tensor_tensor(R[:, 4 + m], FW[:, m], FW[:, m + 4], ALU.subtract).then_inc(*c.done("parts", l, s, o, m))
                                link(dve.tensor_tensor(FW[:, m], FW[:, m], FW[:, m + 4], ALU.add))
                            for m in range(2):
                                dve.tensor_tensor(R[:, m], FW[:, m], FW[:, m + 2], ALU.add).then_inc(*c.done("parts", l, s, o, 4 + m))
                                dve.tensor_tensor(R[:, 2 + m], FW[:, m], FW[:, m + 2], ALU.subtract).then_inc(*c.done("parts", l, s, o, 6 + m))
                            link(dve.tensor_tensor(FW[:, 4], R[:, 4], R[:, 6], ALU.subtract))
                            link(dve.tensor_tensor(FW[:, 5], R[:, 5], R[:, 7], ALU.add))
                            link(dve.scalar_tensor_tensor(FW[:, 6], R[:, 7], -ROOT2, FW[:, 4], ALU.mult, ALU.add))
                            link(dve.scalar_tensor_tensor(FW[:, 7], R[:, 6], ROOT2, FW[:, 5], ALU.mult, ALU.add))
                            link(dve.scalar_tensor_tensor(R[:, 4], R[:, 7], ROOT2, FW[:, 4], ALU.mult, ALU.add))
                            dve.scalar_tensor_tensor(R[:, 5], R[:, 6], -ROOT2, FW[:, 5], ALU.mult, ALU.add).then_inc(
                                *c.done("parts", l, s, o, 8, also=[("filter_parts", l, s, o)]))
                        dve.wait_ge(*c.after("fdft", l, s, o, nf - 1, 1))
                        if o == 0:
                            dve.wait_ge(*c.after("u_tokens", l, 0, s, nt - 1))
                            dve.wait_ge(*c.after("u_tokens", l, 1, s, nt - 1))
                        z = [TOKM[:, 0, ot + t] for t in range(nt)]
                        if s == "ctx":
                            dve.tensor_copy(TT[:, 3, 0:1], z[0][:, 0:1]).then_inc(*c.done("signal_parts", l, s, o))
                        else:
                            link(dve.tensor_tensor(R[:, 2], z[0], z[2], ALU.subtract))
                            link(dve.tensor_tensor(R[:, 1], z[1], z[3], ALU.add))
                            dve.tensor_tensor(R[:, 0], z[0], z[2], ALU.add).then_inc(*c.done("sig", l, s, o, 0))
                            dve.tensor_tensor(R[:, 3], z[1], z[3], ALU.subtract).then_inc(*c.done("sig", l, s, o, 1))
                            dve.scalar_tensor_tensor(R[:, 4], z[3], -ROOT2, R[:, 2], ALU.mult, ALU.add).then_inc(*c.done("sig", l, s, o, 2))
                            dve.scalar_tensor_tensor(R[:, 5], z[2], ROOT2, R[:, 1], ALU.mult, ALU.add).then_inc(*c.done("sig", l, s, o, 3))
                            dve.scalar_tensor_tensor(R[:, 6], z[3], ROOT2, R[:, 2], ALU.mult, ALU.add).then_inc(*c.done("sig", l, s, o, 4))
                            dve.scalar_tensor_tensor(R[:, 7], z[2], -ROOT2, R[:, 1], ALU.mult, ALU.add).then_inc(*c.done("signal_parts", l, s, o))
                        for f in range(nf):
                            for p in range(2):
                                dve.wait_ge(*c.after("zdft", l, s, o, f, p))
                                dve.wait_ge(*c.after("filter_spec", l, s, o, f, p))
                            re, im = ps.of("zdft", l, s, o, f, 0), ps.of("zdft", l, s, o, f, 1)
                            if f:
                                dve.wait_ge(*c.after("spec", l, s, o, f - 1, 1))
                            dve.tensor_tensor(Y[:, 2 * f], re, FH[:, 2 * f], ALU.mult).then_inc(*c.done("prod", l, s, o, f, 0))
                            dve.tensor_tensor(Y[:, 2 * f + 1], re, FH[:, 2 * f + 1], ALU.mult).then_inc(
                                *c.done("prod", l, s, o, f, 1, also=[("freed", "zdft", l, s, o, f, 0)]))
                            dve.tensor_tensor(TT[:, 0], im, FH[:, 2 * f + 1], ALU.mult).then_inc(*c.done("prod", l, s, o, f, 2))
                            dve.tensor_tensor(TT[:, 1], im, FH[:, 8 if f == 0 else 2 * f], ALU.mult).then_inc(
                                *c.done("prod", l, s, o, f, 3, also=[("freed", "zdft", l, s, o, f, 1)]))
                        for m in range(nt if o == 0 else 4):
                            dve.wait_ge(*c.after("conv", l, s, o, m))
                            src = ps.of("conv", l, s, o, m)
                            also = [("freed", "conv", l, s, o, m)] + ([("conv_free", l, s, o)] if m == (nt if o == 0 else 4) - 1 else [])
                            if o == 0:
                                dve.tensor_tensor(TOKM[:, 0, ot + m], src, TOKM[:, 1, ot + m], ALU.mult).then_inc(
                                    *c.done("gated_conv", l, s, o, m, also=also))
                            else:
                                off = STREAMS[s][0]
                                dve.wait_ge(*c.after("z_used", l, m, s))
                                dve.tensor_tensor(YBT[:, 8 + m, off:off + T], src[:, 0:T], YBT[:, 8 + m, off:off + T], ALU.mult).then_inc(
                                    *c.done("gated_conv", l, s, o, m, also=also))
                        if o == 0:
                            dve.wait_ge(*c.after("gated_conv", l, s, 0, nt - 1))

            def gla(l):
                barrier(dve, "gla", l)
                dve.memset(GA[32:33, :], 1.0).then_inc(*c.done("rank_one", l))
                link(dve.memset(ST[:, :, :, 0:P], 0.0))
                for s in ("lat", "ctx"):
                    off, T = STREAMS[s]
                    dve.wait_ge(*c.after("ga", l, 0, s))
                    dve.tensor_copy(GA[0:32, off:off + T], ps.of("ga", l, 0, s)[0:32, 0:T]).then_inc(
                        *c.done("rank", l, s, also=[("freed", "ga", l, 0, s)]))
                for j in range(4):
                    for s in ("lat", "ctx"):
                        off, T = STREAMS[s]
                        dve.wait_ge(*c.after("gv", l, j, s))
                        dve.tensor_copy(GV[:, off // P:(off + T) // P, j * P:(j + 1) * P],
                                        ps.of("gv", l, j, s)[:, 0:T].rearrange("p (t n) -> p t n", n=P)).then_inc(
                            *c.done("gv_kept", l, j, s, also=[("freed", "gv", l, j, s)]))
                for s in ("ctx", "lat"):
                    off, T = STREAMS[s]
                    nt = T // P
                    full = s in streams_of(l)
                    if s == "lat" and "ctx" in streams_of(l):
                        dve.wait_ge(*c.after("o", l, "ctx", 3))
                    elif s == "lat":
                        dve.wait_ge(*c.after("cum", l, "ctx", 1, 1))
                    for t in range(nt):
                        dve.wait_ge(*c.after("softplus", l, s, t))
                        dve.scalar_tensor_tensor(GG[:, t], ps.of("gpre", l, s, t), 0.0, GT[:, t % 2], ALU.min, ALU.subtract).then_inc(
                            *c.done("log_decay", l, s, t, also=[("freed", "gpre", l, s, t)]))
                    for r in range(2):
                        for p in range(2):
                            dve.wait_ge(*c.after("cum_kept", l, s, r, p))

                    def split(ap, width):
                        return ap.rearrange("p (n w) -> p n w", w=width)

                    if s == "lat":
                        dve.wait_ge(*c.after("kT", l, "ctx", 1, 1))
                        if "ctx" in streams_of(l):
                            dve.wait_ge(*c.after("gla_y", l, "ctx", 3))
                    for r in range(2):
                        for p in range(2):
                            b = split(B[:, r, p, 0:T], P)
                            ref = b[:, :, P - 1:P] if r == 0 else b[:, :, 0:1]
                            dve.tensor_tensor(split(KH[:, r, p, 0:T], P), ref.to_broadcast([P, nt, P]), b, ALU.subtract).then_inc(
                                *c.done("k_offset", l, s, r, p, also=[("k_offsets", l, s)] if (r, p) == (1, 1) else []))
                    for r in range(2):
                        dve.wait_ge(*c.after("q_decay", l, s, r))
                        q = QH[:, r, :, 0:T].rearrange("p a (n w) -> p a n w", w=P)
                        dve.tensor_copy(DEC[:, r, :, 0:nt], q[:, :, :, P - 1 if r == 0 else 0]).then_inc(*c.done("decay_cols", l, s, r))
                    dve.wait_ge(*c.after("decay_cols", l, s, 1))
                    for r in range(2):
                        if full:
                            dve.tensor_tensor(QH[:, r, :, 0:T], QH[:, r, :, 0:T], GQ[:, :, off:off + T], ALU.mult).then_inc(
                                *c.done("q_decayed", l, s, r))
                    for j in range(2):
                        dve.wait_ge(*c.after("gk_kept", l, j, s))
                    for r in range(2):
                        dve.wait_ge(*c.after("k_decay", l, s, r))
                        dve.tensor_tensor(KH[:, r, :, 0:T], KH[:, r, :, 0:T], GK[:, :, off:off + T], ALU.mult).then_inc(
                            *c.done("k_dec", l, s, r, also=[("k_decayed", l, s)] if r == 1 else []))

                    def level_args(v):
                        w = LEVELS[v]
                        if v >= 2:
                            dve.wait_ge(*c.after("pairs", l, s, v - 2, nt - 1))
                        elif s == "lat" and "ctx" in streams_of(l):
                            pass
                        for p in range(2):
                            bf, bb = (B[:, r, p, 0:T].rearrange("p (n u w) -> p n u w", u=2, w=w) for r in range(2))
                            eq = EL[:, v % 2, p, 0:T].rearrange("p (n u w) -> p n u w", u=2, w=w)
                            ek = EL[:, v % 2, p, T:2 * T].rearrange("p (n u w) -> p n u w", u=2, w=w)
                            n = T // (2 * w)
                            rf = bf[:, :, 0, w - 1:w].to_broadcast([P, n, w])
                            rb = bb[:, :, 1, 0:1].to_broadcast([P, n, w])
                            for i, (dst, a, b) in enumerate([(eq[:, :, 0], bb[:, :, 0], rb), (eq[:, :, 1], bf[:, :, 1], rf),
                                                             (ek[:, :, 0], rf, bf[:, :, 0]), (ek[:, :, 1], rb, bb[:, :, 1])]):
                                dve.tensor_tensor(dst, a, b, ALU.subtract).then_inc(
                                    *c.done("level_arg", l, s, v, p, i, also=[("level_args", l, s, v)] if (p, i) == (1, 3) else []))

                    def select(v):
                        for t in range(nt):
                            dve.wait_ge(*c.after("pairs", l, s, v, t))
                            if v < 0:
                                a = ATT[:, t].rearrange("p (h n) -> p h n", h=4)
                                src = ps.of("pairs", l, s, v, t).rearrange("p (h n) -> p h n", h=4)
                                dve.tensor_tensor(a, src, DIAG2[:, :].unsqueeze(1).to_broadcast([P, 4, P]), ALU.mult).then_inc(
                                    *c.done("select", l, s, v, t, also=[("freed", "pairs", l, s, v, t)]))
                            else:
                                dve.wait_ge(*c.after("mask_kept"))
                                dve.wait_ge(*c.after("select", l, s, v - 1, t))
                                a = ATT[:, t].rearrange("p (h n) -> p h n", h=4)
                                src = ps.of("pairs", l, s, v, t).rearrange("p (h n) -> p h n", h=4)
                                dve.copy_predicated(a, MASK[:, v, :].unsqueeze(1).to_broadcast([P, 4, P]), src).then_inc(
                                    *c.done("select", l, s, v, t, also=[("freed", "pairs", l, s, v, t)] +
                                            ([("pairs_all", l, s)] if (v, t) == (len(LEVELS) - 1, nt - 1) else [])))

                    def states():
                        base = 0 if s == "ctx" else 2
                        for r in range(2):
                            for i in range(nt if s == "ctx" else nt - 1):
                                t = i if r == 0 else nt - 1 - i
                                dve.wait_ge(*c.after("kv", l, s, r, i))
                                if i:
                                    dve.wait_ge(*c.after("state", l, s, r, i - 1, 1))
                                for p in range(2):
                                    dve.scalar_tensor_tensor(ST[:, r, p, (base + i + 1) * P:(base + i + 2) * P],
                                                             ST[:, r, p, (base + i) * P:(base + i + 1) * P], DEC[:, r, p, t:t + 1],
                                                             ps.of("kv", l, s, r, i)[:, p * P:(p + 1) * P], ALU.mult, ALU.add).then_inc(
                                        *c.done("state", l, s, r, i, p, also=[("freed", "kv", l, s, r, i)] if p else []))

                    if not full:
                        states()
                        continue
                    level_args(0)
                    select(-1)
                    states()
                    for v in range(len(LEVELS)):
                        dve.wait_ge(*c.after("level_exp", l, s, v))
                        dve.tensor_tensor(EL[:, v % 2, :, 0:T], EL[:, v % 2, :, 0:T], GQ[:, :, off:off + T], ALU.mult).then_inc(
                            *c.done("level_q", l, s, v))
                        if v + 1 < len(LEVELS):
                            level_args(v + 1)
                        select(v)
                    for h in range(4):
                        dve.wait_ge(*c.after("o_rms", l, s, h))
                        o = OS[:, h % 2, 0:T]
                        link(dve.scalar_tensor_tensor(o, o, GNORM, OS[:, 4 + h % 2, 0:T], ALU.mult, ALU.mult))
                        dve.tensor_tensor(YBT[:, h, off:off + T], o, GZ[:, h, off:off + T], ALU.mult).then_inc(*c.done("gla_y", l, s, h))

            def attn(l):
                barrier(dve, "attn", l)
                dve.wait_ge(*c.after("load_attn", l, "all"))
                link(dve.tensor_scalar(GAIN[:, 0:512], GAIN[:, 0:512], 0.125, None, ALU.mult))
                for kind, j in ATT_TILES:
                    if kind == "az":
                        continue
                    for s in streams_for(l, (kind, j)):
                        off, T = STREAMS[s]
                        a, b = off // P, (off + T) // P
                        dst = VA[:, a:b] if kind == "av" else QK[:, a:b, (4 if kind == "ak" else j) * P:((4 if kind == "ak" else j) + 1) * P]
                        dve.wait_ge(*c.after(kind, l, j, s))
                        dve.tensor_copy(dst, ps.of(kind, l, j, s)[:, 0:T].rearrange("p (t n) -> p t n", n=P)).then_inc(
                            *c.done("proj_kept", l, kind, j, s, also=[("freed", kind, l, j, s)]))
                for s in ("lat", "ctx"):
                    off, T = STREAMS[s]
                    nt = T // P
                    lo, nh = (0, 10) if s in streams_of(l) else (512, 2)
                    qk = QK[:, off // P:off // P + nt, lo:640]
                    w = 640 - lo
                    dve.wait_ge(*c.after("proj_kept", l, "aq", 3, "lat"))
                    flat = TA.rearrange("p a b -> p (a b)")
                    sq = flat[:, 0:nt * w].rearrange("p (t n) -> p t n", t=nt)
                    if s == "ctx":
                        dve.wait_ge(*c.after("qk_normed", l, "lat"))
                    link(dve.tensor_tensor(sq, qk, qk, ALU.mult))
                    dve.tensor_reduce(MSQ[:, 0:nt * nh], flat[:, 0:nt * w].rearrange("p (t n) -> p t n", n=64), AX.X, ALU.add).then_inc(
                        *c.done("head_ms", l, s))
                    if s not in streams_of(l):
                        pass
                    dve.wait_ge(*c.after("head_rms", l, s))
                    for t in range(nt):
                        q = qk[:, t].rearrange("p (h n) -> p h n", n=64)
                        r = MSQ[:, t * nh:(t + 1) * nh].unsqueeze(2).to_broadcast([P, nh, 64])
                        dve.tensor_tensor(q, q, r, ALU.mult).then_inc(*c.done("head_scaled", l, s, t))
                    dve.wait_ge(*c.after("head_scaled", l, s, nt - 1))
                    last = dve.tensor_tensor(qk, qk, GAIN[:, lo:640].unsqueeze(1).to_broadcast([P, nt, w]), ALU.mult)
                    if s == "ctx":
                        last.then_inc(*c.done("qk_normed", l, s))
                        continue
                    link(last)
                    for t in range(nt):
                        q = qk[:, t].rearrange("p (h i e) -> p h i e", h=10, e=2)
                        a0, a1 = q[:, :, :, 0], q[:, :, :, 1]
                        cos, sin = (ROPE[:, i, t].unsqueeze(1).to_broadcast([P, 10, 32]) for i in range(2))
                        tmp = [TA[:, i, 320 * t:320 * (t + 1)].rearrange("p (h i) -> p h i", h=10) for i in range(4)]
                        for i, (a, b) in enumerate([(a0, cos), (a1, sin), (a0, sin), (a1, cos)]):
                            dve.tensor_tensor(tmp[i], a, b, ALU.mult).then_inc(*c.done("rotated", l, t, i))
                        dve.wait_ge(*c.after("rotated", l, t, 3))
                        dve.tensor_tensor(a0, tmp[0], tmp[1], ALU.subtract).then_inc(*c.done("rotated", l, t, 4))
                        dve.tensor_tensor(a1, tmp[2], tmp[3], ALU.add).then_inc(
                            *c.done("rotated", l, t, 5, also=[("qk_normed", l, s)] if t == nt - 1 else []))
                steps = attn_steps(l)

                def row_max(i):
                    s, t, hh = steps[i]
                    N = 768 if s == "lat" else 256
                    col = 8 * (t + (4 if s == "ctx" else 0)) + hh
                    dve.wait_ge(*c.after("score", l, s, t, hh))
                    dve.tensor_reduce(NMAX[:, col:col + 1], ps.of("score", l, s, t, hh)[:, 0:N], AX.X, ALU.max, negate=True).then_inc(
                        *c.done("row_max", l, s, t, hh))

                def finish(s, t):
                    col = 8 * (t + (4 if s == "ctx" else 0))
                    off = STREAMS[s][0] + t * P
                    link(dve.reciprocal(RINV[:, col:col + 8], SUMS[:, col:col + 8]))
                    dve.wait_ge(*c.after("ao", l, s, t))
                    dve.tensor_tensor(AO[:, t % 2].rearrange("p (h n) -> p h n", h=8), ps.of("ao", l, s, t).rearrange("p (h n) -> p h n", h=8),
                                      RINV[:, col:col + 8].unsqueeze(2).to_broadcast([P, 8, 64]), ALU.mult).then_inc(
                        *c.done("ao_kept", l, s, t, also=[("freed", "ao", l, s, t)]))

                def finish_transposed(s, t):
                    off = STREAMS[s][0] + t * P
                    dve.wait_ge(*c.after("aoT", l, s, t))
                    dve.wait_ge(*c.after("az_kept", l, 3, s))
                    dve.tensor_tensor(YBT[:, 4:8, off:off + P], ps.of("aoT", l, s, t).rearrange("p (j n) -> p j n", j=4),
                                      AZ[:, :, off:off + P], ALU.mult).then_inc(
                        *c.done("attn_y", l, s, t, also=[("freed", "aoT", l, s, t)]))

                row_max(0)
                for i in range(len(steps)):
                    s, t, hh = steps[i]
                    if i + 1 < len(steps):
                        row_max(i + 1)
                    if i % 2:
                        N = 768 if s == "lat" else 256
                        dve.wait_ge(*c.after("probT", l, s, t, hh))
                        if i >= 2:
                            dve.wait_ge(*c.after("ao", l, *steps[i - 2]))
                        dve.tensor_copy(PT[:, i % 2, 0:N], ps.of("probT", l, s, t, hh)[:, 0:N]).then_inc(
                            *c.done("probT_kept2", l, s, t, hh, also=[("freed", "probT", l, s, t, hh), ("probT_kept", l, s, t, hh)]))
                    if hh == 7:
                        finish(s, t)
                    if hh == 2 and i > 8:
                        finish_transposed(*steps[i - 8][:2])
                finish_transposed(*steps[-1][:2])

            def merge(l):
                barrier(dve, "merge", l)
                ss = streams_for(l, ("m", 0))
                for j in range(KD):
                    for b in range(3):
                        for s in ss:
                            off, T = STREAMS[s]
                            dve.wait_ge(*c.after("branch", l, j, b, s))
                            dve.wait_ge(*c.after("gate", l, j, b, s))
                            dst = YM[:, j, off:off + T] if b == 0 else MT[:, b % 2, off:off + T]
                            if b:
                                if b == 1 and j:
                                    dve.wait_ge(*c.after("merge_add", l, j - 1, 1, s))
                                elif b == 2 and j:
                                    dve.wait_ge(*c.after("merge_add", l, j - 1, 2, s))
                            dve.tensor_tensor(dst, ps.of("branch", l, j, b, s)[:, 0:T], MG[:, j % 2, b, off:off + T], ALU.mult).then_inc(
                                *c.done("gated", l, j, b, s, also=[("freed", "branch", l, j, b, s)]))
                dve.wait_ge(*c.after("load_x", "merge", l))
                for j in range(KD):
                    for s in ss:
                        off, T = STREAMS[s]
                        e = 0 if s == "lat" else 1
                        dve.wait_ge(*c.after("out", l, j, s))
                        dve.scalar_tensor_tensor(X[:, j, off:off + T], ps.of("out", l, j, s)[:, 0:T], ADA[:, 16 + j, e:e + 1],
                                                 X[:, j, off:off + T], ALU.mult, ALU.add).then_inc(
                            *c.done("x_new", l, j, s, also=[("freed", "out", l, j, s)] +
                                    ([("x_new", l, "all")] if (j, s) == (KD - 1, ss[-1]) else [])))

            for l in range(DEPTH):
                norm(l, ["lat", "ctx"])
                c.phase_end(("norm", l))
                hyena(l)
                c.phase_end(("hyena", l))
                gla(l)
                c.phase_end(("gla", l))
                attn(l)
                c.phase_end(("attn", l))
                merge(l)
                c.phase_end(("merge", l))
            norm(DEPTH, ["lat"])
            c.phase_end(("norm", DEPTH))

        @block.gpsimd
        def _(pool):
            c.engine = "pool"
            pool.memset(SMALL[:, 255:256], 0.0).then_inc(*c.done("pool_start"))
            for l in range(DEPTH):
                c.phase_end(("norm", l))
                for j in range(4):
                    for s in streams_for(l, ("hz", j)):
                        off, T = STREAMS[s]
                        n = 2 * j + (s == "ctx")
                        pool.wait_ge(*c.after("hz_silu", l, j, s))
                        pool.wait_ge(*c.after("short_conv", l, 8 + j, s))
                        z = YBT[:, 8 + j, off:off + T]
                        pool.tensor_tensor(z, z, TT[:, n % 2, 0:T], ALU.mult).then_inc(*c.done("z_used", l, j, s))
                for s in streams_of(l):
                    for o in range(2):
                        nf = FACTORS[s]
                        for f in range(nf):
                            pool.wait_ge(*c.after("prod", l, s, o, f, 3))
                            pool.tensor_tensor(Y[:, 2 * f], Y[:, 2 * f], TT[:, 0], ALU.subtract).then_inc(*c.done("spec", l, s, o, f, 0))
                            pool.tensor_tensor(Y[:, 2 * f + 1], Y[:, 2 * f + 1], TT[:, 1], ALU.add).then_inc(
                                *c.done("spec", l, s, o, f, 1, also=[("spectrum", l, s, o)] if f == nf - 1 else []))
                c.phase_end(("hyena", l))
                for s in streams_of(l):
                    off, T = STREAMS[s]
                    for v in range(len(LEVELS)):
                        pool.wait_ge(*c.after("level_exp", l, s, v))
                        pool.tensor_tensor(EL[:, v % 2, :, T:2 * T], EL[:, v % 2, :, T:2 * T], GK[:, :, off:off + T], ALU.mult).then_inc(
                            *c.done("level_k", l, s, v))
                c.phase_end(("gla", l))
                c.phase_end(("attn", l))
                for j in range(KD):
                    for b in (1, 2):
                        for s in streams_for(l, ("m", 0)):
                            off, T = STREAMS[s]
                            pool.wait_ge(*c.after("gated", l, j, b, s))
                            if b == 2:
                                pool.wait_ge(*c.after("merge_add", l, j, 1, s))
                            y = YM[:, j, off:off + T]
                            pool.tensor_tensor(y, y, MT[:, b % 2, off:off + T], ALU.add).then_inc(
                                *c.done("merge_add", l, j, b, s, also=[("merged", l, "all")]
                                        if (j, b, s) == (KD - 1, 2, streams_for(l, ("m", 0))[-1]) else []))
                c.phase_end(("merge", l))
            c.phase_end(("norm", DEPTH))

        return c.at, list(c.sems)


def tables():
    f = np.float32
    i = np.arange(P)
    t = {}
    t["tri"] = np.stack([(i[:, None] <= i[None, :]), (i[:, None] >= i[None, :])], 1).astype(f) / f(16)
    t["ident"] = np.eye(P, dtype=f)
    t["diag2"] = 2 * np.eye(P, dtype=f)
    t["ones"] = np.broadcast_to(np.array([1 / 1024, 1 / 128, 1], f)[None, :, None], (P, 3, P)).copy()
    t["mask"] = np.stack([((i[:, None] // (2 * w)) == (i[None, :] // (2 * w))) & ((i[:, None] // w) != (i[None, :] // w))
                          for w in LEVELS], 1).astype(np.int32)
    half = 32
    inv = (f(10000.0) ** (-np.arange(0, half, 2, dtype=f) / f(half))).astype(f)
    tok = np.arange(LAT)
    ang = np.concatenate([(tok // GRID_W).astype(f)[:, None] * inv, (tok % GRID_W).astype(f)[:, None] * inv], -1)
    rope = np.stack([np.cos(ang), np.sin(ang)]).astype(f)
    t["rope"] = rope.reshape(2, 4, P, 32).transpose(2, 0, 1, 3).copy()
    emb, tcol = [], []
    for L in (LAT, CTX):
        lin = linspace(0.0, 1.0, L)
        w = (f(2.0 * math.pi) * np.arange(L, dtype=f) / f(L)).astype(f)
        fr = linspace(1e-4, 15, 16)
        e = np.concatenate([lin[:, None], np.cos(fr[None] * w[:, None]), -np.sin(fr[None] * w[:, None])], -1).astype(f)
        pos = np.concatenate([np.arange(L), [0], np.arange(L - 1, 0, -1)])
        emb.append(e[pos].T)
        tcol.append(-lin[pos].reshape(2 * L // P, P).T)
    t["emb"] = np.ascontiguousarray(np.concatenate(emb, 1))
    t["tcol"] = np.ascontiguousarray(np.concatenate(tcol, 1))
    t["delta"] = np.abs(linspace(math.log(1e-2) / 0.3, math.log(1e-2) / 1.5, 2048)).reshape(4, BW)
    freqs = [4 * i, 4 * i + 2, np.sort(np.concatenate([8 * np.arange(64) + 1, 8 * np.arange(64) + 7])),
             np.sort(np.concatenate([8 * np.arange(64) + 3, 8 * np.arange(64) + 5]))]
    FM, G = np.zeros((P, 16, P)), np.zeros((P, 8, LAT))
    for q, fq in enumerate(freqs):
        for b in range(2):
            a = 2 * np.pi * np.outer(i + P * b, fq) / 1024
            FM[:, 4 * q + 2 * b] = np.cos(a)
            FM[:, 4 * q + 2 * b + 1] = -np.sin(a)
            if q == 0:
                FM[:, 4 * q + 2 * b + 1, 0] = (-1.0) ** i
        a = 2 * np.pi * np.outer(fq, np.arange(LAT)) / 1024
        G[:, 2 * q], G[:, 2 * q + 1] = 2 * np.cos(a), -2 * np.sin(a)
        if q == 0:
            G[0, 0], G[0, 1] = 1.0, (-1.0) ** np.arange(LAT)
    t["FM"], t["G"] = FM.astype(f), G.astype(f)
    return t


def linspace(a, b, n):
    f = np.float32
    step = np.arange(n - 1, dtype=f) / f(n - 1)
    out = f(a) * (f(1) - step) + f(b) * step
    return np.append(out, f(b)).astype(f)


def kernel(**inputs):
    import numpy as _np
    import concourse.bacc as _bacc
    from concourse import mybir as _mybir
    from concourse.bass_utils import run_bass_kernel_spmd as _run

    a = {k: _np.asarray(v) for k, v in inputs.items()}
    tile = lambda w: _np.ascontiguousarray(w.reshape(w.shape[0] // P, P, w.shape[1] // P, P).transpose(2, 1, 0, 3))
    perm = _np.concatenate([_np.r_[64 * j:64 * j + 64, 64 * (j + 4):64 * (j + 4) + 64] for j in range(4)])
    widths = [256, 256, 512, 512, 16, 16, 512, 128, 128, 512, 1536, 512, 3072]
    edge = _np.cumsum([0] + widths)
    seg = [slice(edge[i], edge[i + 1]) for i in range(13)]
    w_in, w_br, wa, cols = [], [], [], []
    for l in range(DEPTH):
        w = a["w_in"][l]
        rank = _np.zeros((D, P), w.dtype)
        rank[:, 0:32] = w[:, edge[4]:edge[6]]
        gates = w[:, seg[12]].reshape(D, 3, KD, P).transpose(0, 2, 1, 3).reshape(D, 3 * D)
        order = [w[:, seg[10]], w[:, seg[11]], rank, w[:, seg[1]], w[:, seg[0]], w[:, seg[2]], w[:, seg[3]],
                 w[:, seg[7]], w[:, seg[8]], w[:, seg[6]][:, perm], w[:, seg[9]][:, perm], gates]
        w_in.append(tile(_np.concatenate(order, 1)))
        br = [tile(a["w_br_gla"][l]), tile(a["w_br_attn"][l][perm]), tile(a["w_br_hy"][l])]
        w_br.append(_np.concatenate(br, 2))
        m = _np.zeros((33, 512), _np.float32)
        m[0:16, 0:256], m[16:32, 256:512] = a["gla_wa_f"][l], a["gla_wa_b"][l]
        m[32, 0:256], m[32, 256:512] = a["gla_ba_f"][l], a["gla_ba_b"][l]
        wa.append(m)
        col = lambda v: v.reshape(-1, P).T
        eps, not0 = _np.full((P, 1), EPS, _np.float32), _np.ones((P, 1), _np.float32)
        not0[0] = 0
        cols.append(_np.concatenate([col(a["b_ada"][l]), col(a["gla_norm"][l]), col(a["hy_conv_w"][l].reshape(-1)),
                                     col(a["hy_conv_b"][l]), col(a["final_norm"]), eps, not0], 1))
    x = _np.concatenate([a["x"][0], a["ctx"][0]], 0).T.reshape(KD, P, TOK).transpose(1, 0, 2)
    cond = _np.stack([a["c"][0], a["c_ctx"]], -1).reshape(KD, P, 2).transpose(1, 0, 2)
    gain = _np.concatenate([_np.tile(a["attn_qnorm"], (1, 8)), _np.tile(a["attn_knorm"], (1, 2))], 1)
    host = {
        "xT": x, "cond": cond, "w_in": _np.stack(w_in), "w_br": _np.stack(w_br), "wa": _np.stack(wa), "cols": _np.stack(cols),
        "w_ada": _np.stack([tile(a["w_ada"][l]) for l in range(DEPTH)]),
        "w_out": _np.stack([tile(a["w_out"][l]) for l in range(DEPTH)]),
        "gain": gain, "f1": a["hy_f1_w"], "f2": a["hy_f2_w"], "f3": a["hy_f3_w"].reshape(DEPTH, 64, 4, BW),
        "c64": _np.stack([a["hy_f1_b"], a["hy_f1_freq"], a["hy_f2_b"], a["hy_f2_freq"]], -1), "skip": a["hy_skip"],
    }
    host.update(tables())

    def declare(nc):
        arrays, aps = {}, {}
        for name, v in host.items():
            v = _np.ascontiguousarray(v)
            arrays["in_" + name] = v
            aps[name] = nc.dram_tensor("in_" + name, v.shape, _mybir.dt.from_np(v.dtype), kind="ExternalInput").ap()
        aps["x_mid"] = nc.dram_tensor("x_mid", (P, KD, TOK), F32, kind="Internal").ap()
        aps["out"] = nc.dram_tensor("out_0", (KD, P, LAT), F32, kind="ExternalOutput").ap()
        return arrays, aps

    scratch = _bacc.Bacc("TRN2", target_bir_lowering=False, num_devices=1)
    known, stages = build_program(scratch, declare(scratch)[1])
    nc = _bacc.Bacc("TRN2", target_bir_lowering=False, num_devices=1)
    arrays, aps = declare(nc)
    build_program(nc, aps, known, [s for s in stages if s != "any"])
    r = _run(nc, [arrays], core_ids=[0])
    return r.results[0]["out_0"].reshape(D, LAT).T[None]
```

```python
import math
from contextlib import ExitStack

import numpy as np
import concourse.bass as bass
from concourse import mybir

F32 = mybir.dt.float32
F32R = mybir.dt.float32r
ALU = mybir.AluOpType
ACT = mybir.ActivationFunctionType
AX = mybir.AxisListType

P = 128
D = 1024
KD = D // P
DEPTH = 2
BW = 512
LAT, CTX = 512, 256
TOK = LAT + CTX
EPS = 1e-6
GRID_W = 64
STREAMS = {"lat": (0, LAT), "ctx": (LAT, CTX)}
LEVELS = [64, 32, 16, 8, 4, 2, 1]
FACTORS = {"lat": 4, "ctx": 2}
ROOT2 = math.sqrt(2.0)
TWO_PI_1, TWO_PI_2 = 6.28125, 0.0019350051879882812
TWO_PI_3 = 2 * math.pi - TWO_PI_1 - TWO_PI_2
ROUND_MAGIC = 1.5 * 2.0 ** 23
PI_BELOW = 3.1415925

HY_TILES = [("u", i) for i in range(12)] + [("hz", i) for i in range(4)]
GLA_TILES = [("ga", 0), ("gk", 0), ("gk", 1), ("gq", 0), ("gq", 1)] + [("gv", i) for i in range(4)] + [("gz", i) for i in range(4)]
ATT_TILES = [("ak", 0), ("av", 0)] + [("aq", i) for i in range(4)] + [("az", i) for i in range(4)]
GATE_TILES = [("m", 3 * j + b) for j in range(KD) for b in range(3)]
IN_TILES = HY_TILES + GLA_TILES + ATT_TILES + GATE_TILES
IN_INDEX = {t: i for i, t in enumerate(IN_TILES)}


def streams_of(layer):
    return ["ctx", "lat"] if layer < DEPTH - 1 else ["lat"]


def streams_for(layer, tile):
    return ["lat", "ctx"] if layer < DEPTH - 1 or tile[0] in ("ga", "gk", "gv", "ak", "av") else ["lat"]


def cores_of(layer):
    return [(s, o) for o in range(2) for s in streams_of(layer)]


def fillers(layer):
    at = {}
    u, hz = [("u", j) for j in range(8, 12)], [("hz", j) for j in range(4)]
    att = [("ak", 0), ("av", 0)] + [("aq", j) for j in range(4)] + [("az", j) for j in range(4)]
    if layer == 0:
        ada = [("ada", 0, j) for j in range(24)]
        first = streams_of(0)[0]
        points = [("mlp", s, i) for s in streams_of(0) for i in range(2)]
        points += [("taps", first, 0, n) for n in range(2 * STREAMS[first][1] // P)]
        for i, p in enumerate(points):
            at[p] = ada[2 * i:2 * i + 2]
        at["parts", first, 0] = ada[2 * len(points):]
        at["spec", "ctx", 0] = u[0:1]
        at["parts", "lat", 0] = u[1:3]
        at["spec", "lat", 0] = u[3:] + hz[0:1]
        at["parts", "ctx", 1] = hz[1:3]
        at["spec", "ctx", 1] = hz[3:]
        for i in range(3):
            at["level", "ctx", i] = att[i:i + 1]
        for i in range(7):
            at["level", "lat", i] = att[3 + i:4 + i]
        for j in range(24):
            at["attn", 2 * j] = [("ada", 1, j)]
    else:
        at["spec", "lat", 0] = u[0:2]
        at["parts", "lat", 1] = u[2:] + hz[0:2]
        at["spec", "lat", 1] = hz[2:]
        for i, (a, b) in enumerate([(0, 2), (2, 4), (4, 6), (6, 7), (7, 8), (8, 9), (9, 10)]):
            at["level", "lat", i] = att[a:b]
    return at


FILL = [fillers(l) for l in range(DEPTH)]


class Counts:

    def __init__(self, nc, stack, known=None, stages=()):
        self.nc, self.stack, self.known = nc, stack, known
        self.sems, self.count, self.at, self.latest, self.engine = {}, {}, {}, {}, None
        for s in stages:
            self.sem(s)

    def sem(self, stage):
        if stage not in self.sems:
            self.sems[stage] = self.stack.enter_context(self.nc.semaphore(stage))
            self.count[stage] = 0
        return self.sems[stage]

    def done(self, stage, *key, also=(), by=1):
        sem = self.sem(stage)
        self.count[stage] += by
        for label in [(stage, *key), *also]:
            self.at[label] = (stage, self.count[stage])
        if by == 1:
            self.latest[self.engine] = (stage, self.count[stage])
        return sem, by

    def after(self, *label):
        if self.known is None:
            return self.sem("any"), 1
        stage, n = self.known[label]
        return self.sem(stage), n

    def phase_end(self, phase):
        self.at[("end", self.engine, phase)] = self.latest[self.engine]


class Psum:

    def __init__(self, counts, banks):
        self.c, self.banks, self.next, self.holder = counts, banks, 0, {}
        self.where = {}

    def take(self, pe, *key, n=1, at=None):
        if at is None:
            at = self.next
            if at % 8 + n > 8 or (n == 2 and at % 2):
                at += 1
            self.next = (at + n) % 8
        at %= 8
        for b in range(at, at + n):
            if b in self.holder:
                pe.wait_ge(*self.c.after("freed", *self.holder[b]))
            self.holder[b] = key
        self.where[key] = (at, n)
        return self.banks[:, at:at + n, :].rearrange("p b n -> p (b n)")

    def of(self, *key):
        if key not in self.where:
            key_at = (0, 2)
        else:
            key_at = self.where[key]
        at, n = key_at
        return self.banks[:, at:at + n, :].rearrange("p b n -> p (b n)")


def carve(tensor, at, *shape):
    n = int(np.prod(shape))
    v = tensor[:, at:at + n]
    if len(shape) == 2:
        v = v.rearrange("p (a b) -> p a b", a=shape[0])
    if len(shape) == 3:
        v = v.rearrange("p (a b c) -> p a b c", a=shape[0], b=shape[1])
    if len(shape) == 4:
        v = v.rearrange("p (a b c d) -> p a b c d", a=shape[0], b=shape[1], c=shape[2])
    return v, at + n


def build_program(nc, d, known=None, stages=()):
    stack = ExitStack()
    with stack:
        c = Counts(nc, stack, known, stages)

        def sb(name, *shape, dt=F32):
            return stack.enter_context(nc.sbuf_tensor(name, [P, *shape], dt))

        H = sb("H", KD, TOK)
        YB = sb("YB", 12 * TOK)
        YBT = YB[:, :].rearrange("p (a t) -> p a t", a=12)
        NSLOT = 4
        RING = sb("RING", NSLOT, KD, P)
        TRI = sb("TRI", 2, P)
        IDENT = sb("IDENT", P)
        ONES = sb("ONES", 3, P)
        MASK = sb("MASK", len(LEVELS), P, dt=mybir.dt.uint8)
        DIAG2 = sb("DIAG2", P)
        COLS = sb("COLS", 60)
        ADAS = sb("ADAS", DEPTH, 24, 2)
        BADA = sb("BADA", DEPTH, 24)
        SC = sb("SC", KD, 2)
        SMALL = sb("SMALL", 256)
        ARENA_N = 31900
        with nc.sbuf_tensor("AR", [P, ARENA_N], F32) as AR:
            pass
        sb("AR_HEAD", ARENA_N - (4 * KD * P + 2 * KD * TOK))
        WS = sb("WS", 4, KD * P, dt=F32R)
        HS = sb("HS", 2 * KD, TOK, dt=F32R)
        banks = stack.enter_context(nc.psum_tensor("banks", [P, 8, 512], F32))
        ps = Psum(c, banks)
        GNORM, CONVW, CONVB, FINALN = COLS[:, 0:1], COLS[:, 1:37], COLS[:, 37:49], COLS[:, 49:57]
        EPSC, NOT0 = COLS[:, 57:58], COLS[:, 58:59]
        TCOL, _ = carve(SMALL, 0, 12)
        C64, _ = carve(SMALL, 12, 4)
        NMAX, _ = carve(SMALL, 16, 48)
        SUMS, _ = carve(SMALL, 64, 48)
        RINV, _ = carve(SMALL, 112, 48)
        MSQ, _ = carve(SMALL, 160, 60)
        DEC, _ = carve(SMALL, 220, 2, 2, 4)

        X, n0 = carve(AR, 0, KD, TOK)
        SQ, n = carve(AR, n0, 2, TOK)
        RS, n = carve(AR, n, TOK)
        YM = H
        BRW, n = carve(AR, n0, 2, 12, P)
        MG, n = carve(AR, n, 2, 3, TOK)
        MT, n = carve(AR, n, 2, TOK)
        OUTB, _ = carve(AR, n0 + 3 * TOK, KD, LAT)
        assert n <= ARENA_N - (4 * KD * P + 2 * KD * TOK)
        UD, n = carve(AR, 0, 4, TOK)
        TOKM, n = carve(AR, n, 2, 6, BW)
        assert n >= n0 + 3 * TOK
        G, n = carve(AR, n, 8, LAT)
        FM, n = carve(AR, n, 16, P)
        FW, n = carve(AR, n, 8, BW)
        EMB, _ = carve(FW.rearrange("p a b -> p (a b)"), 0, 1536)
        R, n = carve(AR, n, 8, BW)
        MASK32 = carve(R.rearrange("p a b -> p (a b)"), 4 * BW, len(LEVELS), P)[0].bitcast(mybir.dt.int32)
        HX, _ = carve(R.rearrange("p a b -> p (a b)"), 0, 3, 1024)
        FH, n = carve(AR, n, 9, BW)
        H2, n = carve(AR, n, 1536)
        HZ, n = carve(AR, n, 2, TOK)
        Y = FW
        assert n <= ARENA_N, n
        F3, n = carve(YB, 0, 4, BW)
        TT, n = carve(YB, n, 4, BW)
        RN, n = carve(YB, n, 2, BW)
        DEL, n = carve(YB, n, BW)
        F12, n = carve(YB, n, 2, 64)
        assert n <= 8 * TOK
        SKIP, _ = carve(TT.rearrange("p a b -> p (a b)"), 3 * BW, BW)
        QK, n = carve(AR, 0, 6, 640)
        VA, nqk = carve(AR, n, 6, P)
        QT, n = carve(AR, nqk, 5, TOK)
        TA, n = carve(AR, n, 4, 4 * 320)
        PR, n = carve(AR, n, 2, TOK)
        PT, n = carve(AR, n, 2, TOK)
        AO, n = carve(AR, n, 2, BW)
        GAIN, n = carve(AR, n, 640)
        ROPE, n = carve(AR, n, 2, 4, 32)
        assert n <= ARENA_N - 2 * KD * TOK
        GK, n = carve(AR, nqk, 2, TOK)
        GQ, n = carve(AR, n, 2, TOK)
        GV, n = carve(AR, n, 6, BW)
        GA, n = carve(AR, n, TOK)
        WA, n = carve(AR, n, BW)
        GG, n = carve(AR, n, 4, BW)
        ATT = GG
        B, n = carve(AR, n, 2, 2, LAT)
        EL, n = carve(AR, n, 2, 2, 2 * LAT)
        QH, n = carve(AR, n, 2, 2, LAT)
        KH, nk = carve(AR, n, 2, 2, LAT)
        OS, n = carve(AR, n, 8, BW)
        KT, n = carve(AR, n, 2, 2, LAT)
        ST, n = carve(AR, n, 2, 2, 6 * P)
        assert n <= ARENA_N, n

        block = stack.enter_context(nc.Block())

        PHASES = []
        for l in range(DEPTH):
            PHASES += [("hyena", l), ("gla", l), ("attn", l), ("merge", l)]
        PHASES.append(("norm", DEPTH))
        BEFORE = dict(zip(PHASES[1:], PHASES[:-1]))

        ORDER = []
        SPLIT = {}
        RAW = 3
        NSPLIT = 3 * KD - RAW + KD

        def barrier(eng, *phase):
            if phase in BEFORE:
                for e in ("pe", "act", "dve", "pool"):
                    if e != c.engine:
                        eng.wait_ge(*c.after("end", e, BEFORE[phase]))

        def prev_conv(l, s, o):
            return (l, *cores_of(l)[cores_of(l).index((s, o)) - 1])

        def pair_group(nt, g):
            b, u = divmod(g, nt // 2)
            return [(64 * b, 2 * u + i, p, (2 * i + p) * P) for i in range(2) for p in range(2)]

        def att_of(nt, h, t):
            col = (2 * (t % 2) + h // 2) * P
            return ATT[:, (h % 2) * (nt // 2) + t // 2, col:col + P]

        def filter_blocks(s, f):
            if s == "ctx" or f < 2:
                return R[:, 2 * f], R[:, 2 * f + 1]
            return (FW[:, 6], FW[:, 7]) if f == 2 else (R[:, 4], R[:, 5])

        def signal_blocks(s, f, o):
            if s == "ctx":
                return TOKM[:, 0, 4], TOKM[:, 0, 5]
            return R[:, 2 * f], R[:, 2 * f + 1]

        def attn_steps(l):
            return [(s, t, hh) for s in ("lat", "ctx") if s in streams_of(l) for t in range(STREAMS[s][1] // P) for hh in range(8)]

        @block.tensor
        def _(pe):
            c.engine = "pe"
            n_w = [0]

            def weights(l, kind, j):
                n = n_w[0]
                ORDER.append((l, kind, j))
                n_w[0] += 1
                pe.wait_ge(*c.after(f"load_slot{n % NSLOT}", n))
                return RING[:, n % NSLOT], ("weights_used", n)

            def project(l, kind, j, m=P):
                w, used = weights(l, kind, j)
                ss = streams_for(l, (kind, j))
                for s in ss:
                    off, T = STREAMS[s]
                    out = ps.take(pe, kind, l, j, s)
                    for k in range(KD):
                        mm = pe.matmul(out[0:m, 0:T], w[:, k, 0:m], H[:, k, off:off + T], start=k == 0, stop=k == KD - 1)
                    mm.then_inc(*c.done(kind, l, j, s, also=[used] if s == ss[-1] else []))

            def split_product(l, i, psum_key, label):
                SPLIT[l, i] = n_w[0]
                n_w[0] += 1
                pe.wait_ge(*c.after("weight_low", l, i))
                ss = streams_for(l, ("m", 0))
                for s in ss:
                    off, T = STREAMS[s]
                    out = ps.take(pe, *psum_key, s)
                    for k in range(KD):
                        if i == 0 and s == ss[0]:
                            pe.wait_ge(*c.after("h_low", l, k))
                        if i == 3 * KD - RAW and s == ss[0]:
                            pe.wait_ge(*c.after("merged_low", l, k))
                        for n, (a, b) in enumerate(((0, 0), (0, 1), (1, 0))):
                            mm = pe.matmul(out[:, 0:T], WS[:, 2 * (i % 2) + a, k * P:(k + 1) * P], HS[:, b * KD + k, off:off + T],
                                           start=(k, n) == (0, 0), stop=(k, n) == (KD - 1, 2))
                    mm.then_inc(*c.done(*label, s, also=[("split_used", l, i)] if s == ss[-1] else []))

            def project_tokens(l, kind, j):
                w, used = weights(l, kind, j)
                ss = streams_for(l, (kind, j))
                for s in ss:
                    off, T = STREAMS[s]
                    out = ps.take(pe, kind, l, j, s)
                    for t in range(T // P):
                        for k in range(KD):
                            mm = pe.matmul(out[:, t * P:(t + 1) * P], H[:, k, off + t * P:off + (t + 1) * P], w[:, k, :],
                                           start=k == 0, stop=k == KD - 1)
                    mm.then_inc(*c.done(kind, l, j, s, also=[used] if s == ss[-1] else []))

            def norm(l, ss):
                outs = {s: ps.take(pe, "ms", l, s) for s in ss}
                for k in range(KD):
                    pe.wait_ge(*c.after("squares", l, k))
                    for s in ss:
                        off, T = STREAMS[s]
                        mm = pe.matmul(outs[s][:, 0:T], ONES[:, 0, :], SQ[:, k % 2, off:off + T], start=k == 0, stop=k == KD - 1)
                        mm.then_inc(*c.done("ms", l, s, k, also=([("squares_used", l, k)] if s == ss[-1] else []) +
                                            ([("ms", l, s)] if k == KD - 1 else [])))

            def ada_tile(l, j):
                pe.wait_ge(*c.after("cond_silu"))
                w, used = weights(l, "ada", j)
                out = ps.take(pe, "ada", l, j, at=7 if l else None)
                for k in range(KD):
                    mm = pe.matmul(out[:, 0:2], w[:, k, :], SC[:, k, :], start=k == 0, stop=k == KD - 1)
                mm.then_inc(*c.done("ada", l, j, also=[used]))

            def fill(l, *point):
                for kind, *j in FILL[l].get(point, []):
                    if kind == "ada":
                        ada_tile(*j)
                    elif kind in ("ak", "av", "aq"):
                        project_tokens(l, kind, *j)
                    else:
                        project(l, kind, *j)

            def filter_nets(l):
                pe.wait_ge(*c.after("load_hy", l, "all"))
                for s in streams_of(l):
                    T = STREAMS[s][1]
                    for layer in range(2):
                        for h in range(2 * T // BW):
                            out = ps.take(pe, "ffn", l, s, layer, h)
                            at = (0 if s == "lat" else 2 * LAT) + h * BW
                            if layer == 0:
                                mm = pe.matmul(out[0:64, :], F12[0:33, 0], EMB[0:33, at:at + BW], start=True, stop=True)
                            else:
                                pe.wait_ge(*c.after("sine", l, s, 0))
                                mm = pe.matmul(out[0:64, :], F12[0:64, 1], H2[0:64, at:at + BW], start=True, stop=True)
                            mm.then_inc(*c.done("ffn", l, s, layer, h))
                        fill(l, "mlp", s, layer)

            def filter_spectrum(l, s, o):
                nt, nf = STREAMS[s][1] // P, FACTORS[s]
                pe.wait_ge(*c.after("sine", l, s, 1))
                base = 0 if s == "lat" else 2 * LAT

                def magnitudes(r, m):
                    pe.wait_ge(*c.after("magnitude", l, s, o, r * nt + m))
                    mm = pe.matmul(total, ONES[:, 2, :], TT[:, 2], start=m == 0, stop=m == nt - 1)
                    mm.then_inc(*c.done("tap_sum", l, s, o, r, m, also=[("tap_sum", l, s, o, r)] if m == nt - 1 else []))

                for r in range(2):
                    total = ps.take(pe, "tap_sum", l, s, o, r)
                    for m in range(nt):
                        out = ps.take(pe, "taps", l, s, o, r * nt + m)
                        at = base + (r * nt + m) * P
                        mm = pe.matmul(out, H2[0:64, at:at + P], F3[0:64, 2 * o + r], start=True, stop=True)
                        mm.then_inc(*c.done("taps", l, s, o, r * nt + m))
                        if m:
                            magnitudes(r, m - 1)
                    magnitudes(r, nt - 1)
                    for m in range(nt):
                        fill(l, "taps", s, o, r * nt + m)
                fill(l, "parts", s, o)
                pe.wait_ge(*c.after("filter_parts", l, s, o))
                for f in range(nf):
                    blocks = filter_blocks(s, f)
                    for p in range(2):
                        out = ps.take(pe, "fdft", l, s, o, f, p)
                        for b in range(2):
                            mm = pe.matmul(out, FM[:, 4 * f + 2 * b + p], blocks[b], start=b == 0, stop=b == 1)
                        mm.then_inc(*c.done("fdft", l, s, o, f, p))

            def convolve(l, s, o):
                off, T = STREAMS[s]
                nt, nf = T // P, FACTORS[s]
                pe.wait_ge(*c.after("signal_parts", l, s, o))
                for f in range(nf):
                    blocks = signal_blocks(s, f, o)
                    for p in range(2):
                        out = ps.take(pe, "zdft", l, s, o, f, p)
                        for b in range(2):
                            mm = pe.matmul(out, FM[:, 4 * f + 2 * b + p], blocks[b], start=b == 0, stop=b == 1)
                        mm.then_inc(*c.done("zdft", l, s, o, f, p))
                fill(l, "spec", s, o)
                pe.wait_ge(*c.after("spectrum", l, s, o))
                for m in range(nt if o == 0 else 4):
                    out = ps.take(pe, "conv", l, s, o, m)
                    for q in range(2 * nf):
                        if o == 0:
                            mm = pe.matmul(out, G[:, q, m * P:(m + 1) * P], Y[:, q], start=q == 0, stop=q == 2 * nf - 1)
                        else:
                            mm = pe.matmul(out[:, 0:T], Y[:, q, m * P:(m + 1) * P], G[:, q, 0:T], start=q == 0, stop=q == 2 * nf - 1)
                    mm.then_inc(*c.done("conv", l, s, o, m))

            def hyena(l):
                filter_nets(l)
                filter_spectrum(l, *cores_of(l)[0])
                norm(l, ["lat", "ctx"])
                pe.wait_ge(*c.after("h", l, "all"))
                for which in range(2):
                    for j in range(4):
                        project(l, "u", 4 * which + j)
                    for s in streams_of(l):
                        off, T = STREAMS[s]
                        pe.wait_ge(*c.after("short_conv", l, 4 * which + 3, s))
                        for t in range(T // P):
                            out = ps.take(pe, "uT", l, which, s, t)
                            for j in range(4):
                                mm = pe.transpose(out[:, j * P:(j + 1) * P], UD[:, j, off + t * P:off + (t + 1) * P], IDENT[:, :])
                            mm.then_inc(*c.done("uT", l, which, s, t))
                for i, (s, o) in enumerate(cores_of(l)):
                    if i:
                        filter_spectrum(l, s, o)
                    convolve(l, s, o)

            def gla(l):
                for t in GLA_TILES:
                    if t[0] == "ga":
                        project(l, *t, m=32)
                    elif t[0] == "gv":
                        project_tokens(l, *t)
                    else:
                        project(l, *t)
                for s in ("ctx", "lat"):
                    off, T = STREAMS[s]
                    nt = T // P
                    full = s in streams_of(l)
                    pe.wait_ge(*c.after("load_gla", l))
                    pe.wait_ge(*c.after("rank", l, s))
                    for t in range(nt):
                        out = ps.take(pe, "gpre", l, s, t)
                        pe.matmul(out, GA[0:33, off + t * P:off + (t + 1) * P], WA[0:33], start=True, stop=True)\
                          .then_inc(*c.done("gpre", l, s, t))
                    for r in range(2):
                        for p in range(2):
                            out = ps.take(pe, "cum", l, s, r, p)
                            for t in range(nt):
                                pe.wait_ge(*c.after("log_decay", l, s, t))
                                mm = pe.matmul(out[:, t * P:(t + 1) * P], GG[:, t, r * 256 + p * P:r * 256 + (p + 1) * P],
                                               TRI[:, r, :], start=True, stop=True)
                            mm.then_inc(*c.done("cum", l, s, r, p))
                    if full:
                        pe.wait_ge(*c.after("qk_ready", l, s))
                        for t in range(nt):
                            out = ps.take(pe, "pairs", l, s, -1, t)
                            for b, chunk, p, col in pair_group(nt, t):
                                cols = slice(off + chunk * P, off + (chunk + 1) * P)
                                mm = pe.matmul(out[:, col:col + P], GK[b:b + 64, p, cols], GQ[b:b + 64, p, cols], start=True, stop=True)
                            mm.then_inc(*c.done("pairs", l, s, -1, t))
                    for r in range(2):
                        for p in range(2):
                            pe.wait_ge(*c.after("k_decayed", l, s))
                            out = ps.take(pe, "kT", l, s, r, p)
                            for t in range(nt):
                                mm = pe.transpose(out[:, t * P:(t + 1) * P], KH[:, r, p, t * P:(t + 1) * P], IDENT[:, :])
                            mm.then_inc(*c.done("kT", l, s, r, p))
                    for r in range(2):
                        for i in range(nt if s == "ctx" else nt - 1):
                            t = i if r == 0 else nt - 1 - i
                            pe.wait_ge(*c.after("k_tokens", l, s, r, 1))
                            out = ps.take(pe, "kv", l, s, r, i)
                            for h in range(4):
                                b, p = 64 * (h % 2), h // 2
                                mm = pe.matmul(out[b:b + 64, p * P:(p + 1) * P], KT[:, r, p, t * P + b:t * P + b + 64],
                                               GV[:, off // P + t, h * P:(h + 1) * P], start=True, stop=True)
                            mm.then_inc(*c.done("kv", l, s, r, i))
                    if not full:
                        continue
                    for v in range(len(LEVELS)):
                        fill(l, "level", s, v)
                        pe.wait_ge(*c.after("level_q", l, s, v))
                        pe.wait_ge(*c.after("level_k", l, s, v))
                        for t in range(nt):
                            out = ps.take(pe, "pairs", l, s, v, t)
                            for b, chunk, p, col in pair_group(nt, t):
                                mm = pe.matmul(out[:, col:col + P], EL[b:b + 64, v % 2, p, T + chunk * P:T + (chunk + 1) * P],
                                               EL[b:b + 64, v % 2, p, chunk * P:(chunk + 1) * P], start=True, stop=True)
                            mm.then_inc(*c.done("pairs", l, s, v, t))
                    pe.wait_ge(*c.after("pairs_all", l, s))
                    pe.wait_ge(*c.after("state", l, s, 1, nt - 2 if s == "lat" else nt - 1, 1))
                    for h in range(4):
                        b, p = 64 * (h % 2), h // 2
                        out = ps.take(pe, "o", l, s, h)
                        for t in range(nt):
                            cols = slice(t * P, (t + 1) * P)
                            first = 0 if s == "ctx" else 2
                            pe.matmul(out[:, cols], GV[:, off // P + t, h * P:(h + 1) * P], att_of(nt, h, t), start=True, stop=False)
                            for r in range(2):
                                at = first + (t if r == 0 else nt - 1 - t)
                                mm = pe.matmul(out[:, cols], ST[b:b + 64, r, p, at * P:(at + 1) * P], QH[b:b + 64, r, p, cols],
                                               start=False, stop=r == 1)
                        mm.then_inc(*c.done("o", l, s, h))
                    for h in range(4):
                        gla_ms(l, s, h, T)

            def gla_ms(l, s, h, T):
                pe.wait_ge(*c.after("o_sq", l, s, h))
                out = ps.take(pe, "oms", l, s, h)
                pe.matmul(out[:, 0:T], ONES[:, 1, :], OS[:, 4 + h, 0:T], start=True, stop=True).then_inc(*c.done("oms", l, s, h))

            def attn(l):
                for s in ("lat", "ctx"):
                    off, T = STREAMS[s]
                    pe.wait_ge(*c.after("qk_normed", l, s))
                    for j in ([4] if s not in streams_of(l) else [4, 0, 1, 2, 3]):
                        out = ps.take(pe, "qkT", l, s, j)
                        for t in range(T // P):
                            mm = pe.transpose(out[:, t * P:(t + 1) * P], QK[:, off // P + t, j * P:(j + 1) * P], IDENT[:, :])
                        mm.then_inc(*c.done("qkT", l, s, j))
                steps = attn_steps(l)

                def scores(i):
                    s, t, hh = steps[i]
                    off = STREAMS[s][0] + t * P
                    b, j = 64 * (hh % 2), hh // 2
                    if i == 0:
                        for s2 in ("lat", "ctx"):
                            pe.wait_ge(*c.after("qkT_kept", l, s2, 4))
                    if t == 0 and hh == 0:
                        pe.wait_ge(*c.after("qkT_kept", l, s, 3))
                    out = ps.take(pe, "score", l, s, t, hh, n=2, at=2 * (i % 2))
                    q = QT[b:b + 64, j, off:off + P]
                    if s == "lat":
                        pe.matmul(out[:, 0:512], q, QT[b:b + 64, 4, 0:512], start=True, stop=True)
                        mm = pe.matmul(out[:, 512:768], q, QT[b:b + 64, 4, 512:768], start=True, stop=True)
                    else:
                        mm = pe.matmul(out[:, 0:256], q, QT[b:b + 64, 4, 512:768], start=True, stop=True)
                    mm.then_inc(*c.done("score", l, s, t, hh))

                def transposes(i):
                    s, t, hh = steps[i]
                    pe.wait_ge(*c.after("prob", l, s, t, hh))
                    out = ps.take(pe, "probT", l, s, t, hh, n=2, at=4)
                    for k in range(6 if s == "lat" else 2):
                        mm = pe.transpose(out[:, k * P:(k + 1) * P], PR[:, i % 2, k * P:(k + 1) * P], IDENT[:, :])
                    mm.then_inc(*c.done("probT", l, s, t, hh))

                def values(i):
                    s, t, hh = steps[i]
                    pe.wait_ge(*c.after("probT_kept", l, s, t, hh))
                    if hh == 0:
                        values.out = ps.take(pe, "ao", l, s, t, at=6)
                    tiles = range(6) if s == "lat" else range(4, 6)
                    for k in tiles:
                        mm = pe.matmul(values.out[:, hh * 64:(hh + 1) * 64], PT[:, i % 2, (k - tiles[0]) * P:(k - tiles[0] + 1) * P],
                                       VA[:, k, 64 * (hh % 2):64 * (hh % 2) + 64], start=k == tiles[0], stop=k == tiles[-1])
                    mm.then_inc(*c.done("ao", l, s, t, hh, also=[("ao", l, s, t)] if hh == 7 else []))

                def out_transposes(s, t):
                    pe.wait_ge(*c.after("ao_kept", l, s, t))
                    out = ps.take(pe, "aoT", l, s, t, at=7)
                    for j in range(4):
                        mm = pe.transpose(out[:, j * P:(j + 1) * P], AO[:, t % 2, j * P:(j + 1) * P], IDENT[:, :])
                    mm.then_inc(*c.done("aoT", l, s, t))

                scores(0)
                scores(1)
                for i in range(len(steps)):
                    transposes(i)
                    if i + 2 < len(steps):
                        scores(i + 2)
                    fill(l, "attn", i)
                    values(i)
                    if i % 8 == 1 and i > 8:
                        out_transposes(*steps[i - 8][:2])
                out_transposes(*steps[-1][:2])

            def merge(l):
                ss = streams_for(l, ("m", 0))
                for j in range(KD):
                    for b in range(3):
                        g = 3 * j + b
                        if g < RAW:
                            project(l, "m", g)
                        else:
                            ORDER.append((l, "m", g))
                            split_product(l, g - RAW, ("m", l, g), ("m", l, g))
                    ORDER.append((l, "branch", j))
                    pe.wait_ge(*c.after(f"load_branch{j % 2}", l, j))
                    for b in range(3):
                        for s in ss:
                            off, T = STREAMS[s]
                            out = ps.take(pe, "branch", l, j, b, s)
                            for k in range(4):
                                mm = pe.matmul(out[:, 0:T], BRW[:, j % 2, 4 * b + k, :], YBT[:, 4 * b + k, off:off + T], start=k == 0, stop=k == 3)
                            mm.then_inc(*c.done("branch", l, j, b, s, also=[("branch_used", l, j)] if b == 2 and s == ss[-1] else []))
                for j in range(KD):
                    ORDER.append((l, "out", j))
                    split_product(l, 3 * KD - RAW + j, ("out", l, j), ("out", l, j))

            pe.wait_ge(*c.after("load_const", "all"))
            for l in range(DEPTH):
                hyena(l)
                c.phase_end(("hyena", l))
                gla(l)
                c.phase_end(("gla", l))
                attn(l)
                c.phase_end(("attn", l))
                merge(l)
                c.phase_end(("merge", l))
            norm(DEPTH, ["lat"])
            c.phase_end(("norm", DEPTH))

        @block.sync
        def _(sp):
            c.engine = "sp"
            sources = {"ada": d["w_ada"], "out": d["w_out"], "branch": d["w_br"]}
            ring = []
            for n, (l, kind, j) in enumerate(ORDER):
                if kind == "branch":
                    if j >= 2:
                        sp.wait_ge(*c.after("branch_used", l, j - 2))
                    elif l:
                        sp.wait_ge(*c.after("end", "dve", ("attn", l)))
                        sp.wait_ge(*c.after("end", "act", ("attn", l)))
                        sp.wait_ge(*c.after("end", "pe", ("attn", l)))
                    else:
                        sp.wait_ge(*c.after("end", "dve", ("attn", l)))
                        sp.wait_ge(*c.after("end", "act", ("attn", l)))
                        sp.wait_ge(*c.after("end", "pe", ("attn", l)))
                    sp.dma_start(BRW[:, j % 2], sources[kind][l, j]).then_inc(*c.done(f"load_branch{j % 2}", l, j, by=16))
                    continue
                m = len(ring)
                if m >= NSLOT:
                    sp.wait_ge(*c.after("weights_used", m - NSLOT))
                src = sources[kind][l, j] if kind in sources else d["w_in"][l, IN_INDEX[kind, j]]
                sp.dma_start(RING[:, m % NSLOT], src).then_inc(*c.done(f"load_slot{m % NSLOT}", m, by=16))
                ring.append((l, kind, j))
            for k in range(KD):
                sp.wait_ge(*c.after("final", k))
                sp.dma_start(d["out"][k], OUTB[:, k]).then_inc(*c.done("store_out", k, by=16))
            sp.wait_ge(*c.after("store_out", KD - 1))

        @block.scalar
        def _(act):
            c.engine = "act"
            chain = [0]

            def link(ins):
                ins.then_inc(*c.done("act_chain", chain[0]))
                act.wait_ge(*c.after("act_chain", chain[0]))
                chain[0] += 1

            def norm(l, ss):
                off, T = (0, TOK) if len(ss) == 2 else (0, LAT)
                if l == DEPTH:
                    barrier(act, "norm", l)
                for k in range(KD):
                    if k >= 2:
                        act.wait_ge(*c.after("squares_used", l, k - 2))
                    act.activation(SQ[:, k % 2, off:off + T], X[:, k, off:off + T], ACT.Square).then_inc(*c.done("squares", l, k))
                for s in ss:
                    o, t = STREAMS[s]
                    act.wait_ge(*c.after("ms", l, s))
                    act.wait_ge(*c.after("squares_used", l, KD - 1))
                    link(act.activation(SQ[:, 0, o:o + t], ps.of("ms", l, s)[:, 0:t], ACT.Ln, bias=EPSC))
                    act.activation(RS[:, o:o + t], SQ[:, 0, o:o + t], ACT.Exp, scale=-0.5).then_inc(
                        *c.done("rms", l, s, also=[("freed", "ms", l, s)]))

            def load(name, dst, src, *key):
                act.dma_start(dst, src).then_inc(*c.done("load_" + name, *key, by=16))

            def start():
                load("cond", SC[:, :, :], d["cond"])
                load("x", X, d["xT"], 0)
                load("const", BADA[:, :, :], d["b_ada"])
                load("const", TRI[:, :, :], d["tri"])
                load("const", IDENT[:, :], d["ident"])
                load("const", ONES[:, :, :], d["ones"])
                load("const", DIAG2[:, :], d["diag2"])
                load("const", TCOL, d["tcol"], "all")
                load("mask", MASK32, d["mask"])
                act.wait_ge(*c.after("load_cond"))
                cond = SC[:, :, :].rearrange("p a b -> p (a b)")
                link(act.activation(RS[:, 0:16], cond, ACT.Silu))
                act.activation(cond, RS[:, 0:16], ACT.Copy).then_inc(*c.done("cond_silu"))

            def fill(l, *point):
                for kind, *j in FILL[l].get(point, []):
                    if kind == "u":
                        conv_centre(l, *j)
                    elif kind == "hz":
                        branch_gate(l, *j)
                    elif kind != "ada":
                        keep_attn(l, kind, *j)

            def branch_gate(l, j):
                for s in streams_for(l, ("hz", j)):
                    off, T = STREAMS[s]
                    if j >= 2:
                        act.wait_ge(*c.after("z_used", l, j - 2, s))
                    act.wait_ge(*c.after("hz", l, j, s))
                    act.activation(HZ[:, j % 2, off:off + T], ps.of("hz", l, j, s)[:, 0:T], ACT.Silu).then_inc(
                        *c.done("hz_silu", l, j, s, also=[("freed", "hz", l, j, s)]))

            def keep_attn(l, kind, j):
                for s in streams_for(l, (kind, j)):
                    off, T = STREAMS[s]
                    act.wait_ge(*c.after(kind, l, j, s))
                    src = ps.of(kind, l, j, s)[:, 0:T]
                    if kind == "az":
                        act.activation(YBT[:, 4 + j, off:off + T], src, ACT.Silu).then_inc(
                            *c.done("az_kept", l, j, s, also=[("freed", kind, l, j, s)]))
                        continue
                    a, b = off // P, (off + T) // P
                    col = 0 if kind == "av" else (4 if kind == "ak" else j) * P
                    dst = VA[:, a:b] if kind == "av" else QK[:, a:b, col:col + P]
                    act.activation(dst, src.rearrange("p (t n) -> p t n", n=P), ACT.Copy).then_inc(
                        *c.done("proj_kept", l, kind, j, s, also=[("freed", kind, l, j, s)]))

            def filter_nets(l):
                barrier(act, "hyena", l)
                load("cols", COLS[:, 0:59], d["cols"][l], l)
                load("hy", C64[0:64], d["c64"][l], l, 2)
                load("hy", EMB[0:33], d["emb"], l, 3)
                load("hy", F12[0:33, 0], d["f1"][l], l, 4)
                load("hy", F12[0:64, 1], d["f2"][l], l, 5)
                load("hy", F3[0:64], d["f3"][l], l, 6)
                load("hy", FM, d["FM"], l, "all")
                load("G", G, d["G"], l)
                for s in streams_of(l):
                    T2 = 2 * STREAMS[s][1]
                    base = 0 if s == "lat" else 2 * LAT
                    for layer in range(2):
                        act.wait_ge(*c.after("reduced", l, s, layer))
                        act.activation(H2[0:64, base:base + T2], HX[0:64, 2, 0:T2], ACT.Sin).then_inc(*c.done("sine", l, s, layer))
                        fill(l, "mlp", s, layer)

            def filter_spectrum(l, s, o):
                T = STREAMS[s][1]
                nt, nf = T // P, FACTORS[s]
                tbase = 0 if s == "lat" else 8
                if (s, o) != cores_of(l)[0]:
                    act.wait_ge(*c.after("conv_free", *prev_conv(l, s, o)))
                load("skip", SKIP[0:1], d["skip"][l, o:o + 1], l, s, o)
                for r in range(2):
                    if r:
                        act.wait_ge(*c.after("window_last", l, s, o, 0))
                    elif (s, o) != cores_of(l)[0]:
                        act.wait_ge(*c.after("window_last", *prev_conv(l, s, o), 1))
                    load("delta", DEL, d["delta"][2 * o + r:2 * o + r + 1].to_broadcast([P, BW]), l, s, o, r)
                    act.wait_ge(*c.after("load_delta", l, s, o, r))
                    for m in range(nt):
                        n = r * nt + m
                        if n >= 2:
                            act.wait_ge(*c.after("taps_windowed", l, s, o, n - 2))
                        act.activation(TT[:, n % 2], DEL, ACT.Exp, scale=TCOL[:, tbase + n:tbase + n + 1]).then_inc(
                            *c.done("window", l, s, o, n, also=[("window_last", l, s, o, r)] if m == nt - 1 else []))
                        act.wait_ge(*c.after("taps_windowed", l, s, o, n))
                        if m:
                            act.wait_ge(*c.after("tap_sum", l, s, o, r, m - 1))
                        elif r:
                            act.wait_ge(*c.after("tap_sum", l, s, o, 0))
                        act.activation(TT[:, 2], FW[:, n], ACT.Abs).then_inc(*c.done("magnitude", l, s, o, n))
                    act.wait_ge(*c.after("tap_sum", l, s, o, r))
                    link(act.activation(RN[:, r], ps.of("tap_sum", l, s, o, r), ACT.Ln, scale=float(2 * T)))
                    act.activation(RN[:, r], RN[:, r], ACT.Exp, scale=-1.0).then_inc(
                        *c.done("tap_norm", l, s, o, r, also=[("freed", "tap_sum", l, s, o, r)]))
                    for m in range(nt):
                        fill(l, "taps", s, o, r * nt + m)
                fill(l, "parts", s, o)
                act.wait_ge(*c.after("load_cols", l))
                for f in range(nf):
                    for p in range(2):
                        act.wait_ge(*c.after("fdft", l, s, o, f, p))
                        src = ps.of("fdft", l, s, o, f, p)
                        if f == 0 and p == 1:
                            link(act.activation(FH[:, 1], src, ACT.Copy, scale=NOT0))
                            act.activation(FH[0:1, 8], src[0:1], ACT.Copy).then_inc(
                                *c.done("filter_spec", l, s, o, f, p, also=[("freed", "fdft", l, s, o, f, p)]))
                            continue
                        if f == 0:
                            link(act.activation(FH[:, 8], src, ACT.Copy))
                        act.activation(FH[:, 2 * f + p], src, ACT.Copy).then_inc(
                            *c.done("filter_spec", l, s, o, f, p, also=[("freed", "fdft", l, s, o, f, p)]))

            def hyena(l):
                filter_nets(l)
                filter_spectrum(l, *cores_of(l)[0])
                if l == 0:
                    act.wait_ge(*c.after("load_x", 0))
                else:
                    act.wait_ge(*c.after("x_new", l - 1, "all"))
                    act.dma_start(d["x_mid"], X).then_inc(*c.done("store_x", l, by=16))
                norm(l, ["lat", "ctx"])
                if l:
                    act.wait_ge(*c.after("store_x", l))
                for which in range(2):
                    for j in range(4):
                        conv_centre(l, 4 * which + j)
                    for s in streams_of(l):
                        o = STREAMS[s][0] // P
                        for t in range(STREAMS[s][1] // P):
                            act.wait_ge(*c.after("uT", l, which, s, t))
                            act.activation(TOKM[:, which, o + t], ps.of("uT", l, which, s, t), ACT.Copy).then_inc(
                                *c.done("u_tokens", l, which, s, t, also=[("freed", "uT", l, which, s, t)]))
                for i, (s, o) in enumerate(cores_of(l)):
                    if i:
                        filter_spectrum(l, s, o)
                    fill(l, "spec", s, o)

            def conv_centre(l, j):
                for s in streams_for(l, ("u", j)):
                    off, T = STREAMS[s]
                    act.wait_ge(*c.after("u", l, j, s))
                    if 4 <= j < 8:
                        act.wait_ge(*c.after("uT", l, 0, s, T // P - 1))
                    dst = UD[:, j % 4, off:off + T] if j < 8 else YBT[:, j, off:off + T]
                    act.activation(dst, ps.of("u", l, j, s)[:, 0:T], ACT.Identity, bias=CONVB[:, j:j + 1],
                                   scale=CONVW[:, 12 + j:13 + j]).then_inc(*c.done("centre", l, j, s))

            def gla(l):
                barrier(act, "gla", l)
                load("gla", WA[0:33], d["wa"][l], l)
                for kind, j in GLA_TILES:
                    if kind in ("gq", "gk", "gz"):
                        dst = {"gq": GQ, "gk": GK, "gz": YBT}[kind]
                        for s in streams_for(l, (kind, j)):
                            off, T = STREAMS[s]
                            act.wait_ge(*c.after(kind, l, j, s))
                            act.activation(dst[:, j, off:off + T], ps.of(kind, l, j, s)[:, 0:T],
                                           ACT.Silu if kind == "gz" else ACT.Copy,
                                           scale=0.125 if kind == "gq" else 1.0).then_inc(
                                *c.done(kind + "_kept", l, j, s, also=[("freed", kind, l, j, s)] +
                                        ([("qk_ready", l, s)] if (kind, j) == ("gq", 1) else [])))
                for s in ("ctx", "lat"):
                    T = STREAMS[s][1]
                    nt = T // P
                    full = s in streams_of(l)
                    if s == "lat":
                        act.wait_ge(*c.after("o" if "ctx" in streams_of(l) else "cum", l, "ctx", *((3,) if "ctx" in streams_of(l) else (1, 1))))
                    for t in range(nt):
                        act.wait_ge(*c.after("gpre", l, s, t))
                        act.activation(GG[:, t], ps.of("gpre", l, s, t), ACT.Abs).then_inc(*c.done("gate_abs", l, s, t))
                    for t in range(nt):
                        act.wait_ge(*c.after("gate_abs", l, s, t))
                        act.activation(GG[:, t], GG[:, t], ACT.Exp, scale=-1.0).then_inc(*c.done("gate_exp", l, s, t))
                    for t in range(nt):
                        act.wait_ge(*c.after("gate_exp", l, s, t))
                        act.activation(GG[:, t], GG[:, t], ACT.Ln, bias=1.0).then_inc(*c.done("softplus", l, s, t))
                    if s == "lat" and streams_of(l)[0] == "ctx":
                        act.wait_ge(*c.after("k_tokens", l, "ctx", 1, 1))
                    for r in range(2):
                        for p in range(2):
                            act.wait_ge(*c.after("cum", l, s, r, p))
                            act.activation(B[:, r, p, 0:T], ps.of("cum", l, s, r, p)[:, 0:T], ACT.Copy).then_inc(
                                *c.done("cum_kept", l, s, r, p, also=[("freed", "cum", l, s, r, p)]))
                    if full or True:
                        act.wait_ge(*c.after("cum_kept", l, s, 1, 1))
                        if s == "lat" and "ctx" in streams_of(l):
                            act.wait_ge(*c.after("oms", l, "ctx", 3))
                        for r in range(2):
                            last = act.activation(QH[:, r, :, 0:T], B[:, r, :, 0:T], ACT.Exp)
                            last.then_inc(*c.done("q_decay", l, s, r))
                    act.wait_ge(*c.after("k_offsets", l, s))
                    for r in range(2):
                        act.activation(KH[:, r, :, 0:T], KH[:, r, :, 0:T], ACT.Exp).then_inc(*c.done("k_decay", l, s, r))
                    for r in range(2):
                        for p in range(2):
                            act.wait_ge(*c.after("kT", l, s, r, p))
                            if s == "lat":
                                act.wait_ge(*c.after("kv", l, "ctx", 1, 1))
                            act.activation(KT[:, r, p, 0:T], ps.of("kT", l, s, r, p)[:, 0:T], ACT.Copy).then_inc(
                                *c.done("k_tokens", l, s, r, p, also=[("freed", "kT", l, s, r, p)]))
                    if not full:
                        continue
                    for v in range(len(LEVELS)):
                        fill(l, "level", s, v)
                        act.wait_ge(*c.after("level_args", l, s, v))
                        act.activation(EL[:, v % 2, :, 0:2 * T], EL[:, v % 2, :, 0:2 * T], ACT.Exp).then_inc(*c.done("level_exp", l, s, v))
                    act.wait_ge(*c.after("kT", l, s, 1, 1))
                    if s == "lat" and "ctx" in streams_of(l):
                        act.wait_ge(*c.after("gla_y", l, "ctx", 3))
                    for h in range(4):
                        act.wait_ge(*c.after("o", l, s, h))
                        act.activation(OS[:, h, 0:T], ps.of("o", l, s, h)[:, 0:T], ACT.Copy).then_inc(*c.done("o_kept", l, s, h))
                        act.activation(OS[:, 4 + h, 0:T], ps.of("o", l, s, h)[:, 0:T], ACT.Square).then_inc(
                            *c.done("o_sq", l, s, h, also=[("freed", "o", l, s, h)]))
                    for h in range(4):
                        act.wait_ge(*c.after("oms", l, s, h))
                        act.activation(OS[:, 4 + h, 0:T], ps.of("oms", l, s, h)[:, 0:T], ACT.Ln, bias=EPSC).then_inc(
                            *c.done("o_log", l, s, h, also=[("freed", "oms", l, s, h)]))
                    for h in range(4):
                        act.wait_ge(*c.after("o_log", l, s, h))
                        act.activation(OS[:, 4 + h, 0:T], OS[:, 4 + h, 0:T], ACT.Exp, scale=-0.5).then_inc(*c.done("o_rms", l, s, h))

            def attn(l):
                barrier(act, "attn", l)
                load("attn", GAIN, d["gain"][l:l + 1].to_broadcast([P, 640]), l, 0)
                load("attn", ROPE, d["rope"], l, "all")
                for s in ("lat", "ctx"):
                    nh = (STREAMS[s][1] // P) * 10
                    act.wait_ge(*c.after("head_ms", l, s))
                    link(act.activation(MSQ[:, 0:nh], MSQ[:, 0:nh], ACT.Ln, scale=1.0 / 64, bias=EPSC))
                    act.activation(MSQ[:, 0:nh], MSQ[:, 0:nh], ACT.Exp, scale=-0.5).then_inc(*c.done("head_rms", l, s))
                for s in ("lat", "ctx"):
                    off, T = STREAMS[s]
                    for j in ([4] if s not in streams_of(l) else [4, 0, 1, 2, 3]):
                        act.wait_ge(*c.after("qkT", l, s, j))
                        act.activation(QT[:, j, off:off + T], ps.of("qkT", l, s, j)[:, 0:T], ACT.Copy).then_inc(
                            *c.done("qkT_kept", l, s, j, also=[("freed", "qkT", l, s, j)]))
                steps = attn_steps(l)

                def keep(i):
                    s, t, hh = steps[i]
                    N = 768 if s == "lat" else 256
                    act.wait_ge(*c.after("probT", l, s, t, hh))
                    if i >= 2:
                        act.wait_ge(*c.after("ao", l, *steps[i - 2]))
                    act.activation(PT[:, i % 2, 0:N], ps.of("probT", l, s, t, hh)[:, 0:N], ACT.Copy).then_inc(
                        *c.done("probT_kept", l, s, t, hh, also=[("freed", "probT", l, s, t, hh)]))

                for i, (s, t, hh) in enumerate(steps):
                    N = 768 if s == "lat" else 256
                    col = 8 * (t + (4 if s == "ctx" else 0)) + hh
                    act.wait_ge(*c.after("row_max", l, s, t, hh))
                    if i >= 2:
                        act.wait_ge(*c.after("probT", l, *steps[i - 2]))
                    act.activation(PR[:, i % 2, 0:N], ps.of("score", l, s, t, hh)[:, 0:N], ACT.Exp, bias=NMAX[:, col:col + 1],
                                   accum_out=SUMS[:, col:col + 1]).then_inc(
                        *c.done("prob", l, s, t, hh, also=[("freed", "score", l, s, t, hh)]))
                    if i and (i - 1) % 2 == 0:
                        keep(i - 1)
                if (len(steps) - 1) % 2 == 0:
                    keep(len(steps) - 1)

            def merge(l):
                barrier(act, "merge", l)
                load("x", X, d["xT"] if l == 0 else d["x_mid"], "merge", l)

                def weight_high(i):
                    n = SPLIT[l, i]
                    act.wait_ge(*c.after(f"load_slot{n % NSLOT}", n))
                    if i >= 2:
                        act.wait_ge(*c.after("split_used", l, i - 2))
                    act.activation(WS[:, 2 * (i % 2)], RING[:, n % NSLOT].rearrange("p a b -> p (a b)"), ACT.Copy).then_inc(
                        *c.done("weight_high", l, i))

                weight_high(0)
                weight_high(1)
                for j in range(KD):
                    for b in range(3):
                        if 3 * j + b > RAW - 1:
                            weight_high(3 * j + b - RAW + 2)
                        for s in streams_for(l, ("m", 0)):
                            off, T = STREAMS[s]
                            act.wait_ge(*c.after("m", l, 3 * j + b, s))
                            if j >= 2:
                                act.wait_ge(*c.after("gated", l, j - 2, b, s))
                            act.activation(MG[:, j % 2, b, off:off + T], ps.of("m", l, 3 * j + b, s)[:, 0:T], ACT.Sigmoid).then_inc(
                                *c.done("gate", l, j, b, s, also=[("freed", "m", l, 3 * j + b, s)]))
                ss = streams_for(l, ("m", 0))
                cols = sum(STREAMS[s][1] for s in ss)
                for k in range(KD):
                    act.wait_ge(*c.after("merge_add", l, k, 2, ss[-1]))
                    act.activation(HS[:, k, 0:cols], YM[:, k, 0:cols], ACT.Copy).then_inc(*c.done("merged_high", l, k))
                for i in range(3 * KD - RAW + 2, NSPLIT):
                    weight_high(i)

            start()
            for l in range(DEPTH):
                hyena(l)
                c.phase_end(("hyena", l))
                gla(l)
                c.phase_end(("gla", l))
                attn(l)
                c.phase_end(("attn", l))
                merge(l)
                c.phase_end(("merge", l))
            norm(DEPTH, ["lat"])
            c.phase_end(("norm", DEPTH))

        @block.vector
        def _(dve):
            c.engine = "dve"
            chain = [0]

            def link(ins):
                ins.then_inc(*c.done("dve_chain", chain[0]))
                dve.wait_ge(*c.after("dve_chain", chain[0]))
                chain[0] += 1

            def norm(l, ss):
                if l < DEPTH:
                    ADA = ADAS[:, l]
                    dve.wait_ge(*c.after("adaln", l, 23))
                else:
                    barrier(dve, "norm", l)
                for s in ss:
                    off, T = STREAMS[s]
                    e = 0 if s == "lat" else 1
                    dve.wait_ge(*c.after("rms", l, s))
                    for k in range(KD):
                        x, rs = X[:, k, off:off + T], RS[:, off:off + T]
                        if l == DEPTH:
                            dve.scalar_tensor_tensor(OUTB[:, k], x, FINALN[:, k:k + 1], rs, ALU.mult, ALU.mult).then_inc(
                                *c.done("final", k))
                        else:
                            h = H[:, k, off:off + T]
                            dve.scalar_tensor_tensor(h, x, ADA[:, 8 + k, e:e + 1], rs, ALU.mult, ALU.mult).then_inc(
                                *c.done("h_scaled", l, s, k))
                if l == DEPTH:
                    return
                for s in ss:
                    off, T = STREAMS[s]
                    e = 0 if s == "lat" else 1
                    for k in range(KD):
                        h = H[:, k, off:off + T]
                        dve.wait_ge(*c.after("h_scaled", l, s, k))
                        dve.tensor_scalar(h, h, ADA[:, k, e:e + 1], None, ALU.add).then_inc(
                            *c.done("h", l, s, k, also=[("h", l, "all")] if (s, k) == (ss[-1], KD - 1) else []))

            def conv_sides(l, j):
                for s in streams_for(l, ("u", j)):
                    off, T = STREAMS[s]
                    dst = UD[:, j % 4, off:off + T] if j < 8 else YBT[:, j, off:off + T]
                    u = ps.of("u", l, j, s)
                    dve.wait_ge(*c.after("centre", l, j, s))
                    link(dve.scalar_tensor_tensor(dst[:, 1:T], u[:, 0:T - 1], CONVW[:, j:j + 1], dst[:, 1:T], ALU.mult, ALU.add))
                    dve.scalar_tensor_tensor(dst[:, 0:T - 1], u[:, 1:T], CONVW[:, 24 + j:25 + j], dst[:, 0:T - 1], ALU.mult, ALU.add)\
                       .then_inc(*c.done("short_conv", l, j, s, also=[("freed", "u", l, j, s)]))

            def fill(l, *point):
                for kind, *j in FILL[l].get(point, []):
                    if kind == "u":
                        conv_sides(l, *j)
                    elif kind == "ada":
                        ada_tile(*j)

            def ada_tile(l, j):
                if (l, j) == (0, 0):
                    dve.wait_ge(*c.after("load_const", "all"))
                dve.wait_ge(*c.after("ada", l, j))
                dve.tensor_scalar(ADAS[:, l, j], ps.of("ada", l, j)[:, 0:2], BADA[:, l, j:j + 1], 1.0 if 8 <= j < 16 else 0.0,
                                  ALU.add, ALU.add).then_inc(*c.done("adaln", l, j, also=[("freed", "ada", l, j)]))

            def filter_nets(l):
                if l == 0:
                    dve.wait_ge(*c.after("load_mask"))
                    dve.tensor_copy(MASK[:, :, :], MASK32).then_inc(*c.done("mask_kept"))
                    dve.wait_ge(*c.after("mask_kept"))
                barrier(dve, "hyena", l)
                dve.wait_ge(*c.after("load_hy", l, "all"))
                for s in streams_of(l):
                    T2 = 2 * STREAMS[s][1]
                    for layer in range(2):
                        if (s, layer) != (streams_of(l)[0], 0):
                            dve.wait_ge(*c.after("sine", l, *((s, 0) if layer else (streams_of(l)[0], 1))))
                        for h in range(T2 // BW):
                            dve.wait_ge(*c.after("ffn", l, s, layer, h))
                            dve.tensor_scalar(HX[0:64, 0, h * BW:(h + 1) * BW], ps.of("ffn", l, s, layer, h)[0:64],
                                              C64[0:64, 2 * layer:2 * layer + 1], C64[0:64, 2 * layer + 1:2 * layer + 2],
                                              ALU.add, ALU.mult).then_inc(
                                *c.done("phase", l, s, layer, h, also=[("freed", "ffn", l, s, layer, h)]))
                        dve.wait_ge(*c.after("phase", l, s, layer, T2 // BW - 1))
                        x, k, r = (HX[0:64, i, 0:T2] for i in range(3))
                        link(dve.tensor_scalar(k, x, 1.0 / (2 * math.pi), ROUND_MAGIC, ALU.mult, ALU.add))
                        link(dve.tensor_scalar(k, k, ROUND_MAGIC, None, ALU.subtract))
                        link(dve.scalar_tensor_tensor(r, k, -TWO_PI_1, x, ALU.mult, ALU.add))
                        link(dve.scalar_tensor_tensor(r, k, -TWO_PI_2, r, ALU.mult, ALU.add))
                        link(dve.scalar_tensor_tensor(r, k, -TWO_PI_3, r, ALU.mult, ALU.add))
                        dve.tensor_scalar(r, r, -PI_BELOW, PI_BELOW, ALU.max, ALU.min).then_inc(*c.done("reduced", l, s, layer))
                        fill(l, "mlp", s, layer)

            def filter_spectrum(l, s, o):
                T = STREAMS[s][1]
                nt, nf = T // P, FACTORS[s]
                if (s, o) != cores_of(l)[0]:
                    dve.wait_ge(*c.after("conv_free", *prev_conv(l, s, o)))
                    dve.wait_ge(*c.after("gated_conv", *prev_conv(l, s, o), 0))
                else:
                    dve.wait_ge(*c.after("sine", l, streams_of(l)[-1], 1))
                for r in range(2):
                    for m in range(nt):
                        n = r * nt + m
                        dve.wait_ge(*c.after("taps", l, s, o, n))
                        dve.wait_ge(*c.after("window", l, s, o, n))
                        dve.scalar_tensor_tensor(FW[:, n], TT[:, n % 2], 0.05, ps.of("taps", l, s, o, n), ALU.add, ALU.mult)\
                           .then_inc(*c.done("taps_windowed", l, s, o, n, also=[("freed", "taps", l, s, o, n)]))
                    dve.wait_ge(*c.after("tap_norm", l, s, o, r))
                    for m in range(nt):
                        n = r * nt + m
                        ins = dve.tensor_tensor(FW[:, n], FW[:, n], RN[:, r], ALU.mult)
                        ins.then_inc(*c.done("taps_normed", l, s, o, n))
                    dve.wait_ge(*c.after("taps_normed", l, s, o, (r + 1) * nt - 1))
                    for m in range(nt):
                        fill(l, "taps", s, o, r * nt + m)
                dve.wait_ge(*c.after("load_skip", l, s, o))
                link(dve.scalar_tensor_tensor(FW[0:1, 0], SKIP[0:1], 1.0 / (2 * T), FW[0:1, 0], ALU.mult, ALU.add))
                link(dve.memset(FW[0:1, nt], 0.0))
                if s == "ctx":
                    for m in range(2):
                        dve.tensor_tensor(R[:, m], FW[:, m], FW[:, m + 2], ALU.add).then_inc(*c.done("parts", l, s, o, m))
                        last = dve.tensor_tensor(R[:, 2 + m], FW[:, m], FW[:, m + 2], ALU.subtract)
                        last.then_inc(*c.done("parts", l, s, o, 2 + m, also=[("filter_parts", l, s, o)] if m == 1 else []))
                else:
                    for m in range(4):
                        dve.tensor_tensor(R[:, 4 + m], FW[:, m], FW[:, m + 4], ALU.subtract).then_inc(*c.done("parts", l, s, o, m))
                        link(dve.tensor_tensor(FW[:, m], FW[:, m], FW[:, m + 4], ALU.add))
                    for m in range(2):
                        dve.tensor_tensor(R[:, m], FW[:, m], FW[:, m + 2], ALU.add).then_inc(*c.done("parts", l, s, o, 4 + m))
                        dve.tensor_tensor(R[:, 2 + m], FW[:, m], FW[:, m + 2], ALU.subtract).then_inc(*c.done("parts", l, s, o, 6 + m))
                    link(dve.tensor_tensor(FW[:, 4], R[:, 4], R[:, 6], ALU.subtract))
                    link(dve.tensor_tensor(FW[:, 5], R[:, 5], R[:, 7], ALU.add))
                    link(dve.scalar_tensor_tensor(FW[:, 6], R[:, 7], -ROOT2, FW[:, 4], ALU.mult, ALU.add))
                    link(dve.scalar_tensor_tensor(FW[:, 7], R[:, 6], ROOT2, FW[:, 5], ALU.mult, ALU.add))
                    link(dve.scalar_tensor_tensor(R[:, 4], R[:, 7], ROOT2, FW[:, 4], ALU.mult, ALU.add))
                    dve.scalar_tensor_tensor(R[:, 5], R[:, 6], -ROOT2, FW[:, 5], ALU.mult, ALU.add).then_inc(
                        *c.done("parts", l, s, o, 8, also=[("filter_parts", l, s, o)]))
                fill(l, "parts", s, o)

            def convolve(l, s, o):
                T = STREAMS[s][1]
                nt, nf = T // P, FACTORS[s]
                ot = STREAMS[s][0] // P
                if o:
                    dve.wait_ge(*c.after("gated_conv", l, s, 0, nt - 1))
                dve.wait_ge(*c.after("fdft", l, s, o, nf - 1, 1))
                if o == 0:
                    dve.wait_ge(*c.after("u_tokens", l, 0, s, nt - 1))
                    dve.wait_ge(*c.after("u_tokens", l, 1, s, nt - 1))
                z = [TOKM[:, 0, ot + t] for t in range(nt)]
                if s == "ctx":
                    dve.tensor_copy(TT[:, 3, 0:1], z[0][:, 0:1]).then_inc(*c.done("signal_parts", l, s, o))
                else:
                    link(dve.tensor_tensor(R[:, 2], z[0], z[2], ALU.subtract))
                    link(dve.tensor_tensor(R[:, 1], z[1], z[3], ALU.add))
                    dve.tensor_tensor(R[:, 0], z[0], z[2], ALU.add).then_inc(*c.done("sig", l, s, o, 0))
                    dve.tensor_tensor(R[:, 3], z[1], z[3], ALU.subtract).then_inc(*c.done("sig", l, s, o, 1))
                    dve.scalar_tensor_tensor(R[:, 4], z[3], -ROOT2, R[:, 2], ALU.mult, ALU.add).then_inc(*c.done("sig", l, s, o, 2))
                    dve.scalar_tensor_tensor(R[:, 5], z[2], ROOT2, R[:, 1], ALU.mult, ALU.add).then_inc(*c.done("sig", l, s, o, 3))
                    dve.scalar_tensor_tensor(R[:, 6], z[3], ROOT2, R[:, 2], ALU.mult, ALU.add).then_inc(*c.done("sig", l, s, o, 4))
                    dve.scalar_tensor_tensor(R[:, 7], z[2], -ROOT2, R[:, 1], ALU.mult, ALU.add).then_inc(*c.done("signal_parts", l, s, o))
                for f in range(nf):
                    for p in range(2):
                        dve.wait_ge(*c.after("zdft", l, s, o, f, p))
                        dve.wait_ge(*c.after("filter_spec", l, s, o, f, p))
                    re, im = ps.of("zdft", l, s, o, f, 0), ps.of("zdft", l, s, o, f, 1)
                    if f:
                        dve.wait_ge(*c.after("spec", l, s, o, f - 1, 1))
                    dve.tensor_tensor(Y[:, 2 * f], re, FH[:, 2 * f], ALU.mult).then_inc(*c.done("prod", l, s, o, f, 0))
                    dve.tensor_tensor(Y[:, 2 * f + 1], re, FH[:, 2 * f + 1], ALU.mult).then_inc(
                        *c.done("prod", l, s, o, f, 1, also=[("freed", "zdft", l, s, o, f, 0)]))
                    dve.tensor_tensor(TT[:, 0], im, FH[:, 2 * f + 1], ALU.mult).then_inc(*c.done("prod", l, s, o, f, 2))
                    dve.tensor_tensor(TT[:, 1], im, FH[:, 8 if f == 0 else 2 * f], ALU.mult).then_inc(
                        *c.done("prod", l, s, o, f, 3, also=[("freed", "zdft", l, s, o, f, 1)]))
                fill(l, "spec", s, o)
                for m in range(nt if o == 0 else 4):
                    dve.wait_ge(*c.after("conv", l, s, o, m))
                    src = ps.of("conv", l, s, o, m)
                    also = [("freed", "conv", l, s, o, m)] + ([("conv_free", l, s, o)] if m == (nt if o == 0 else 4) - 1 else [])
                    if o == 0:
                        dve.tensor_tensor(TOKM[:, 0, ot + m], src, TOKM[:, 1, ot + m], ALU.mult).then_inc(
                            *c.done("gated_conv", l, s, o, m, also=also))
                    else:
                        off = STREAMS[s][0]
                        dve.wait_ge(*c.after("z_used", l, m, s))
                        dve.tensor_tensor(YBT[:, 8 + m, off:off + T], src[:, 0:T], YBT[:, 8 + m, off:off + T], ALU.mult).then_inc(
                            *c.done("gated_conv", l, s, o, m, also=also))

            def hyena(l):
                filter_nets(l)
                filter_spectrum(l, *cores_of(l)[0])
                norm(l, ["lat", "ctx"])
                for j in range(8):
                    conv_sides(l, j)
                for i, (s, o) in enumerate(cores_of(l)):
                    if i:
                        filter_spectrum(l, s, o)
                    convolve(l, s, o)

            def gla(l):
                barrier(dve, "gla", l)
                dve.memset(GA[32:33, :], 1.0).then_inc(*c.done("rank_one", l))
                link(dve.memset(ST[:, :, :, 0:P], 0.0))
                for s in ("lat", "ctx"):
                    off, T = STREAMS[s]
                    dve.wait_ge(*c.after("ga", l, 0, s))
                    dve.tensor_copy(GA[0:32, off:off + T], ps.of("ga", l, 0, s)[0:32, 0:T]).then_inc(
                        *c.done("rank", l, s, also=[("freed", "ga", l, 0, s)]))
                for j in range(4):
                    for s in ("lat", "ctx"):
                        off, T = STREAMS[s]
                        dve.wait_ge(*c.after("gv", l, j, s))
                        dve.tensor_copy(GV[:, off // P:(off + T) // P, j * P:(j + 1) * P],
                                        ps.of("gv", l, j, s)[:, 0:T].rearrange("p (t n) -> p t n", n=P)).then_inc(
                            *c.done("gv_kept", l, j, s, also=[("freed", "gv", l, j, s)]))
                for s in ("ctx", "lat"):
                    off, T = STREAMS[s]
                    nt = T // P
                    full = s in streams_of(l)
                    if s == "lat" and "ctx" in streams_of(l):
                        dve.wait_ge(*c.after("o", l, "ctx", 3))
                    elif s == "lat":
                        dve.wait_ge(*c.after("cum", l, "ctx", 1, 1))
                    for t in range(nt):
                        dve.wait_ge(*c.after("softplus", l, s, t))
                        dve.scalar_tensor_tensor(GG[:, t], ps.of("gpre", l, s, t), 0.0, GG[:, t], ALU.min, ALU.subtract).then_inc(
                            *c.done("log_decay", l, s, t, also=[("freed", "gpre", l, s, t)]))
                    for r in range(2):
                        for p in range(2):
                            dve.wait_ge(*c.after("cum_kept", l, s, r, p))

                    def split(ap, width):
                        return ap.rearrange("p (n w) -> p n w", w=width)

                    if s == "lat":
                        dve.wait_ge(*c.after("kT", l, "ctx", 1, 1))
                        if "ctx" in streams_of(l):
                            dve.wait_ge(*c.after("gla_y", l, "ctx", 3))
                    for r in range(2):
                        for p in range(2):
                            b = split(B[:, r, p, 0:T], P)
                            ref = b[:, :, P - 1:P] if r == 0 else b[:, :, 0:1]
                            dve.tensor_tensor(split(KH[:, r, p, 0:T], P), ref.to_broadcast([P, nt, P]), b, ALU.subtract).then_inc(
                                *c.done("k_offset", l, s, r, p, also=[("k_offsets", l, s)] if (r, p) == (1, 1) else []))
                    for r in range(2):
                        dve.wait_ge(*c.after("q_decay", l, s, r))
                        q = QH[:, r, :, 0:T].rearrange("p a (n w) -> p a n w", w=P)
                        dve.tensor_copy(DEC[:, r, :, 0:nt], q[:, :, :, P - 1 if r == 0 else 0]).then_inc(*c.done("decay_cols", l, s, r))
                    dve.wait_ge(*c.after("decay_cols", l, s, 1))
                    for r in range(2):
                        if full:
                            dve.tensor_tensor(QH[:, r, :, 0:T], QH[:, r, :, 0:T], GQ[:, :, off:off + T], ALU.mult).then_inc(
                                *c.done("q_decayed", l, s, r))
                    for j in range(2):
                        dve.wait_ge(*c.after("gk_kept", l, j, s))
                    for r in range(2):
                        dve.wait_ge(*c.after("k_decay", l, s, r))
                        dve.tensor_tensor(KH[:, r, :, 0:T], KH[:, r, :, 0:T], GK[:, :, off:off + T], ALU.mult).then_inc(
                            *c.done("k_dec", l, s, r, also=[("k_decayed", l, s)] if r == 1 else []))

                    def level_args(v):
                        w = LEVELS[v]
                        if v >= 2:
                            dve.wait_ge(*c.after("pairs", l, s, v - 2, nt - 1))
                        elif s == "lat" and "ctx" in streams_of(l):
                            pass
                        for p in range(2):
                            bf, bb = (B[:, r, p, 0:T].rearrange("p (n u w) -> p n u w", u=2, w=w) for r in range(2))
                            eq = EL[:, v % 2, p, 0:T].rearrange("p (n u w) -> p n u w", u=2, w=w)
                            ek = EL[:, v % 2, p, T:2 * T].rearrange("p (n u w) -> p n u w", u=2, w=w)
                            n = T // (2 * w)
                            rf = bf[:, :, 0, w - 1:w].to_broadcast([P, n, w])
                            rb = bb[:, :, 1, 0:1].to_broadcast([P, n, w])
                            for i, (dst, a, b) in enumerate([(eq[:, :, 0], bb[:, :, 0], rb), (eq[:, :, 1], bf[:, :, 1], rf),
                                                             (ek[:, :, 0], rf, bf[:, :, 0]), (ek[:, :, 1], rb, bb[:, :, 1])]):
                                dve.tensor_tensor(dst, a, b, ALU.subtract).then_inc(
                                    *c.done("level_arg", l, s, v, p, i, also=[("level_args", l, s, v)] if (p, i) == (1, 3) else []))

                    def select(v):
                        for t in range(nt):
                            dve.wait_ge(*c.after("pairs", l, s, v, t))
                            if v < 0:
                                a = ATT[:, t].rearrange("p (h n) -> p h n", h=4)
                                src = ps.of("pairs", l, s, v, t).rearrange("p (h n) -> p h n", h=4)
                                dve.tensor_tensor(a, src, DIAG2[:, :].unsqueeze(1).to_broadcast([P, 4, P]), ALU.mult).then_inc(
                                    *c.done("select", l, s, v, t, also=[("freed", "pairs", l, s, v, t)]))
                            else:
                                dve.wait_ge(*c.after("mask_kept"))
                                dve.wait_ge(*c.after("select", l, s, v - 1, t))
                                a = ATT[:, t].rearrange("p (h n) -> p h n", h=4)
                                src = ps.of("pairs", l, s, v, t).rearrange("p (h n) -> p h n", h=4)
                                dve.copy_predicated(a, MASK[:, v, :].unsqueeze(1).to_broadcast([P, 4, P]), src).then_inc(
                                    *c.done("select", l, s, v, t, also=[("freed", "pairs", l, s, v, t)] +
                                            ([("pairs_all", l, s)] if (v, t) == (len(LEVELS) - 1, nt - 1) else [])))

                    def states():
                        base = 0 if s == "ctx" else 2
                        for r in range(2):
                            for i in range(nt if s == "ctx" else nt - 1):
                                t = i if r == 0 else nt - 1 - i
                                dve.wait_ge(*c.after("kv", l, s, r, i))
                                if i:
                                    dve.wait_ge(*c.after("state", l, s, r, i - 1, 1))
                                for p in range(2):
                                    dve.scalar_tensor_tensor(ST[:, r, p, (base + i + 1) * P:(base + i + 2) * P],
                                                             ST[:, r, p, (base + i) * P:(base + i + 1) * P], DEC[:, r, p, t:t + 1],
                                                             ps.of("kv", l, s, r, i)[:, p * P:(p + 1) * P], ALU.mult, ALU.add).then_inc(
                                        *c.done("state", l, s, r, i, p, also=[("freed", "kv", l, s, r, i)] if p else []))

                    if not full:
                        states()
                        continue
                    level_args(0)
                    select(-1)
                    states()
                    for v in range(len(LEVELS)):
                        dve.wait_ge(*c.after("level_exp", l, s, v))
                        dve.tensor_tensor(EL[:, v % 2, :, 0:T], EL[:, v % 2, :, 0:T], GQ[:, :, off:off + T], ALU.mult).then_inc(
                            *c.done("level_q", l, s, v))
                        if v + 1 < len(LEVELS):
                            level_args(v + 1)
                        select(v)
                    for h in range(4):
                        dve.wait_ge(*c.after("o_rms", l, s, h))
                        o = OS[:, h, 0:T]
                        link(dve.scalar_tensor_tensor(o, o, GNORM, OS[:, 4 + h, 0:T], ALU.mult, ALU.mult))
                        y = YBT[:, h, off:off + T]
                        dve.tensor_tensor(y, y, o, ALU.mult).then_inc(*c.done("gla_y", l, s, h))

            def attn(l):
                barrier(dve, "attn", l)
                dve.wait_ge(*c.after("load_attn", l, "all"))
                link(dve.tensor_scalar(GAIN[:, 0:512], GAIN[:, 0:512], 0.125, None, ALU.mult))
                for s in ("lat", "ctx"):
                    off, T = STREAMS[s]
                    nt = T // P
                    lo, nh = (0, 10) if s in streams_of(l) else (512, 2)
                    qk = QK[:, off // P:off // P + nt, lo:640]
                    w = 640 - lo
                    dve.wait_ge(*c.after("proj_kept", l, "aq", 3, "lat"))
                    flat = TA.rearrange("p a b -> p (a b)")
                    sq = flat[:, 0:nt * w].rearrange("p (t n) -> p t n", t=nt)
                    if s == "ctx":
                        dve.wait_ge(*c.after("qk_normed", l, "lat"))
                    link(dve.tensor_tensor(sq, qk, qk, ALU.mult))
                    dve.tensor_reduce(MSQ[:, 0:nt * nh], flat[:, 0:nt * w].rearrange("p (t n) -> p t n", n=64), AX.X, ALU.add).then_inc(
                        *c.done("head_ms", l, s))
                    if s not in streams_of(l):
                        pass
                    dve.wait_ge(*c.after("head_rms", l, s))
                    for t in range(nt):
                        q = qk[:, t].rearrange("p (h n) -> p h n", n=64)
                        r = MSQ[:, t * nh:(t + 1) * nh].unsqueeze(2).to_broadcast([P, nh, 64])
                        dve.tensor_tensor(q, q, r, ALU.mult).then_inc(*c.done("head_scaled", l, s, t))
                    dve.wait_ge(*c.after("head_scaled", l, s, nt - 1))
                    last = dve.tensor_tensor(qk, qk, GAIN[:, lo:640].unsqueeze(1).to_broadcast([P, nt, w]), ALU.mult)
                    if s == "ctx":
                        last.then_inc(*c.done("qk_normed", l, s))
                        continue
                    link(last)
                    for t in range(nt):
                        q = qk[:, t].rearrange("p (h i e) -> p h i e", h=10, e=2)
                        a0, a1 = q[:, :, :, 0], q[:, :, :, 1]
                        cos, sin = (ROPE[:, i, t].unsqueeze(1).to_broadcast([P, 10, 32]) for i in range(2))
                        tmp = [TA[:, i, 320 * t:320 * (t + 1)].rearrange("p (h i) -> p h i", h=10) for i in range(4)]
                        for i, (a, b) in enumerate([(a0, cos), (a1, sin), (a0, sin), (a1, cos)]):
                            dve.tensor_tensor(tmp[i], a, b, ALU.mult).then_inc(*c.done("rotated", l, t, i))
                        dve.wait_ge(*c.after("rotated", l, t, 3))
                        dve.tensor_tensor(a0, tmp[0], tmp[1], ALU.subtract).then_inc(*c.done("rotated", l, t, 4))
                        dve.tensor_tensor(a1, tmp[2], tmp[3], ALU.add).then_inc(
                            *c.done("rotated", l, t, 5, also=[("qk_normed", l, s)] if t == nt - 1 else []))
                steps = attn_steps(l)

                def row_max(i):
                    s, t, hh = steps[i]
                    N = 768 if s == "lat" else 256
                    col = 8 * (t + (4 if s == "ctx" else 0)) + hh
                    dve.wait_ge(*c.after("score", l, s, t, hh))
                    dve.tensor_reduce(NMAX[:, col:col + 1], ps.of("score", l, s, t, hh)[:, 0:N], AX.X, ALU.max, negate=True).then_inc(
                        *c.done("row_max", l, s, t, hh))

                def finish(s, t):
                    col = 8 * (t + (4 if s == "ctx" else 0))
                    off = STREAMS[s][0] + t * P
                    link(dve.reciprocal(RINV[:, col:col + 8], SUMS[:, col:col + 8]))
                    dve.wait_ge(*c.after("ao", l, s, t))
                    dve.tensor_tensor(AO[:, t % 2].rearrange("p (h n) -> p h n", h=8), ps.of("ao", l, s, t).rearrange("p (h n) -> p h n", h=8),
                                      RINV[:, col:col + 8].unsqueeze(2).to_broadcast([P, 8, 64]), ALU.mult).then_inc(
                        *c.done("ao_kept", l, s, t, also=[("freed", "ao", l, s, t)]))

                def finish_transposed(s, t):
                    off = STREAMS[s][0] + t * P
                    dve.wait_ge(*c.after("aoT", l, s, t))
                    dve.wait_ge(*c.after("az_kept", l, 3, s))
                    dve.tensor_tensor(YBT[:, 4:8, off:off + P], ps.of("aoT", l, s, t).rearrange("p (j n) -> p j n", j=4),
                                      YBT[:, 4:8, off:off + P], ALU.mult).then_inc(
                        *c.done("attn_y", l, s, t, also=[("freed", "aoT", l, s, t)]))

                row_max(0)
                for i in range(len(steps)):
                    s, t, hh = steps[i]
                    if i + 1 < len(steps):
                        row_max(i + 1)
                    if i % 2:
                        N = 768 if s == "lat" else 256
                        dve.wait_ge(*c.after("probT", l, s, t, hh))
                        if i >= 2:
                            dve.wait_ge(*c.after("ao", l, *steps[i - 2]))
                        dve.tensor_copy(PT[:, i % 2, 0:N], ps.of("probT", l, s, t, hh)[:, 0:N]).then_inc(
                            *c.done("probT_kept2", l, s, t, hh, also=[("freed", "probT", l, s, t, hh), ("probT_kept", l, s, t, hh)]))
                    if hh == 2 and i > 8:
                        finish_transposed(*steps[i - 8][:2])
                    fill(l, "attn", i)
                    if hh == 7:
                        finish(s, t)
                finish_transposed(*steps[-1][:2])

            def merge(l):
                barrier(dve, "merge", l)
                ss = streams_for(l, ("m", 0))
                cols = sum(STREAMS[s][1] for s in ss)

                def weight_low(i):
                    n = SPLIT[l, i]
                    dve.wait_ge(*c.after("weight_high", l, i))
                    dve.tensor_tensor(WS[:, 2 * (i % 2) + 1], RING[:, n % NSLOT].rearrange("p a b -> p (a b)"),
                                      WS[:, 2 * (i % 2)], ALU.subtract).then_inc(
                        *c.done("weight_low", l, i, also=[("weights_used", n)]))

                def merged_low(k):
                    dve.wait_ge(*c.after("merged_high", l, k))
                    dve.tensor_tensor(HS[:, KD + k, 0:cols], YM[:, k, 0:cols], HS[:, k, 0:cols], ALU.subtract).then_inc(
                        *c.done("merged_low", l, k))

                for j in range(KD):
                    for i in range(max(0, 3 * j - 1), 3 * j + 2):
                        weight_low(i)
                    if j == 0:
                        dve.wait_ge(*c.after("h_low", l, KD - 1))
                        dve.wait_ge(*c.after("m", l, RAW - 1, ss[-1]))
                    if j == KD - 1:
                        for k in range(KD - 1):
                            merged_low(k)
                    for b in range(3):
                        for s in ss:
                            off, T = STREAMS[s]
                            dve.wait_ge(*c.after("branch", l, j, b, s))
                            dve.wait_ge(*c.after("gate", l, j, b, s))
                            dst = YM[:, j, off:off + T] if b == 0 else MT[:, b % 2, off:off + T]
                            if b:
                                if b == 1 and j:
                                    dve.wait_ge(*c.after("merge_add", l, j - 1, 1, s))
                                elif b == 2 and j:
                                    dve.wait_ge(*c.after("merge_add", l, j - 1, 2, s))
                            dve.tensor_tensor(dst, ps.of("branch", l, j, b, s)[:, 0:T], MG[:, j % 2, b, off:off + T], ALU.mult).then_inc(
                                *c.done("gated", l, j, b, s, also=[("freed", "branch", l, j, b, s)]))
                merged_low(KD - 1)
                dve.wait_ge(*c.after("load_x", "merge", l))
                for j in range(KD):
                    if 3 * KD - RAW + 2 + j < NSPLIT:
                        weight_low(3 * KD - RAW + 2 + j)
                    for s in ss:
                        off, T = STREAMS[s]
                        e = 0 if s == "lat" else 1
                        dve.wait_ge(*c.after("out", l, j, s))
                        dve.scalar_tensor_tensor(X[:, j, off:off + T], ps.of("out", l, j, s)[:, 0:T], ADAS[:, l, 16 + j, e:e + 1],
                                                 X[:, j, off:off + T], ALU.mult, ALU.add).then_inc(
                            *c.done("x_new", l, j, s, also=[("freed", "out", l, j, s)] +
                                    ([("x_new", l, "all")] if (j, s) == (KD - 1, ss[-1]) else [])))

            for l in range(DEPTH):
                hyena(l)
                c.phase_end(("hyena", l))
                gla(l)
                c.phase_end(("gla", l))
                attn(l)
                c.phase_end(("attn", l))
                merge(l)
                c.phase_end(("merge", l))
            norm(DEPTH, ["lat"])
            c.phase_end(("norm", DEPTH))

        @block.gpsimd
        def _(pool):
            c.engine = "pool"
            pool.memset(SMALL[:, 255:256], 0.0).then_inc(*c.done("pool_start"))
            for l in range(DEPTH):
                def fill(*point):
                    for kind, *j in FILL[l].get(point, []):
                        if kind == "hz":
                            for s in streams_for(l, ("hz", j[0])):
                                off, T = STREAMS[s]
                                pool.wait_ge(*c.after("hz_silu", l, j[0], s))
                                pool.wait_ge(*c.after("short_conv", l, 8 + j[0], s))
                                z = YBT[:, 8 + j[0], off:off + T]
                                pool.tensor_tensor(z, z, HZ[:, j[0] % 2, off:off + T], ALU.mult).then_inc(*c.done("z_used", l, j[0], s))

                for s, o in cores_of(l):
                    fill("parts", s, o)
                    nf = FACTORS[s]
                    for f in range(nf):
                        pool.wait_ge(*c.after("prod", l, s, o, f, 3))
                        pool.tensor_tensor(Y[:, 2 * f], Y[:, 2 * f], TT[:, 0], ALU.subtract).then_inc(*c.done("spec", l, s, o, f, 0))
                        pool.tensor_tensor(Y[:, 2 * f + 1], Y[:, 2 * f + 1], TT[:, 1], ALU.add).then_inc(
                            *c.done("spec", l, s, o, f, 1, also=[("spectrum", l, s, o)] if f == nf - 1 else []))
                    fill("spec", s, o)
                c.phase_end(("hyena", l))
                for s in streams_of(l):
                    off, T = STREAMS[s]
                    for v in range(len(LEVELS)):
                        pool.wait_ge(*c.after("level_exp", l, s, v))
                        pool.tensor_tensor(EL[:, v % 2, :, T:2 * T], EL[:, v % 2, :, T:2 * T], GK[:, :, off:off + T], ALU.mult).then_inc(
                            *c.done("level_k", l, s, v))
                c.phase_end(("gla", l))
                barrier(pool, "attn", l)
                cols = sum(STREAMS[s][1] for s in streams_for(l, ("m", 0)))
                for k in range(KD):
                    pool.tensor_copy(HS[:, k, 0:cols], H[:, k, 0:cols]).then_inc(*c.done("h_high", l, k))
                    pool.wait_ge(*c.after("h_high", l, k))
                    pool.tensor_tensor(HS[:, KD + k, 0:cols], H[:, k, 0:cols], HS[:, k, 0:cols], ALU.subtract).then_inc(
                        *c.done("h_low", l, k))
                c.phase_end(("attn", l))
                for j in range(KD):
                    for b in (1, 2):
                        for s in streams_for(l, ("m", 0)):
                            off, T = STREAMS[s]
                            pool.wait_ge(*c.after("gated", l, j, b, s))
                            if b == 2:
                                pool.wait_ge(*c.after("merge_add", l, j, 1, s))
                            y = YM[:, j, off:off + T]
                            pool.tensor_tensor(y, y, MT[:, b % 2, off:off + T], ALU.add).then_inc(
                                *c.done("merge_add", l, j, b, s, also=[("merged", l, "all")]
                                        if (j, b, s) == (KD - 1, 2, streams_for(l, ("m", 0))[-1]) else []))
                c.phase_end(("merge", l))
            c.phase_end(("norm", DEPTH))

        return c.at, list(c.sems)


def tables():
    f = np.float32
    i = np.arange(P)
    t = {}
    t["tri"] = np.stack([(i[:, None] <= i[None, :]), (i[:, None] >= i[None, :])], 1).astype(f) / f(16)
    t["ident"] = np.eye(P, dtype=f)
    t["diag2"] = 2 * np.eye(P, dtype=f)
    t["ones"] = np.broadcast_to(np.array([1 / 1024, 1 / 128, 1], f)[None, :, None], (P, 3, P)).copy()
    t["mask"] = np.stack([((i[:, None] // (2 * w)) == (i[None, :] // (2 * w))) & ((i[:, None] // w) != (i[None, :] // w))
                          for w in LEVELS], 1).astype(np.int32)
    half = 32
    inv = (f(10000.0) ** (-np.arange(0, half, 2, dtype=f) / f(half))).astype(f)
    tok = np.arange(LAT)
    ang = np.concatenate([(tok // GRID_W).astype(f)[:, None] * inv, (tok % GRID_W).astype(f)[:, None] * inv], -1)
    rope = np.stack([np.cos(ang), np.sin(ang)]).astype(f)
    t["rope"] = rope.reshape(2, 4, P, 32).transpose(2, 0, 1, 3).copy()
    emb, tcol = [], []
    for L in (LAT, CTX):
        lin = linspace(0.0, 1.0, L)
        w = (f(2.0 * math.pi) * np.arange(L, dtype=f) / f(L)).astype(f)
        fr = linspace(1e-4, 15, 16)
        e = np.concatenate([lin[:, None], np.cos(fr[None] * w[:, None]), -np.sin(fr[None] * w[:, None])], -1).astype(f)
        pos = np.concatenate([np.arange(L), [0], np.arange(L - 1, 0, -1)])
        emb.append(e[pos].T)
        tcol.append(-lin[pos].reshape(2 * L // P, P).T)
    t["emb"] = np.ascontiguousarray(np.concatenate(emb, 1))
    t["tcol"] = np.ascontiguousarray(np.concatenate(tcol, 1))
    t["delta"] = np.abs(linspace(math.log(1e-2) / 0.3, math.log(1e-2) / 1.5, 2048)).reshape(4, BW)
    freqs = [4 * i, 4 * i + 2, np.sort(np.concatenate([8 * np.arange(64) + 1, 8 * np.arange(64) + 7])),
             np.sort(np.concatenate([8 * np.arange(64) + 3, 8 * np.arange(64) + 5]))]
    FM, G = np.zeros((P, 16, P)), np.zeros((P, 8, LAT))
    for q, fq in enumerate(freqs):
        for b in range(2):
            a = 2 * np.pi * np.outer(i + P * b, fq) / 1024
            FM[:, 4 * q + 2 * b] = np.cos(a)
            FM[:, 4 * q + 2 * b + 1] = -np.sin(a)
            if q == 0:
                FM[:, 4 * q + 2 * b + 1, 0] = (-1.0) ** i
        a = 2 * np.pi * np.outer(fq, np.arange(LAT)) / 1024
        G[:, 2 * q], G[:, 2 * q + 1] = 2 * np.cos(a), -2 * np.sin(a)
        if q == 0:
            G[0, 0], G[0, 1] = 1.0, (-1.0) ** np.arange(LAT)
    t["FM"], t["G"] = FM.astype(f), G.astype(f)
    return t


def linspace(a, b, n):
    f = np.float32
    step = np.arange(n - 1, dtype=f) / f(n - 1)
    out = f(a) * (f(1) - step) + f(b) * step
    return np.append(out, f(b)).astype(f)


def kernel(**inputs):
    import numpy as _np
    import concourse.bacc as _bacc
    from concourse import mybir as _mybir
    from concourse.bass_utils import run_bass_kernel_spmd as _run

    a = {k: _np.asarray(v) for k, v in inputs.items()}
    tile = lambda w: _np.ascontiguousarray(w.reshape(w.shape[0] // P, P, w.shape[1] // P, P).transpose(2, 1, 0, 3))
    perm = _np.concatenate([_np.r_[64 * j:64 * j + 64, 64 * (j + 4):64 * (j + 4) + 64] for j in range(4)])
    widths = [256, 256, 512, 512, 16, 16, 512, 128, 128, 512, 1536, 512, 3072]
    edge = _np.cumsum([0] + widths)
    seg = [slice(edge[i], edge[i + 1]) for i in range(13)]
    w_in, w_br, wa, cols = [], [], [], []
    for l in range(DEPTH):
        w = a["w_in"][l]
        rank = _np.zeros((D, P), w.dtype)
        rank[:, 0:32] = w[:, edge[4]:edge[6]]
        gates = w[:, seg[12]].reshape(D, 3, KD, P).transpose(0, 2, 1, 3).reshape(D, 3 * D)
        order = [w[:, seg[10]], w[:, seg[11]], rank, w[:, seg[1]], w[:, seg[0]], w[:, seg[2]], w[:, seg[3]],
                 w[:, seg[7]], w[:, seg[8]], w[:, seg[6]][:, perm], w[:, seg[9]][:, perm], gates]
        w_in.append(tile(_np.concatenate(order, 1)))
        br = [tile(a["w_br_gla"][l]), tile(a["w_br_attn"][l][perm]), tile(a["w_br_hy"][l])]
        w_br.append(_np.concatenate(br, 2))
        m = _np.zeros((33, 512), _np.float32)
        m[0:16, 0:256], m[16:32, 256:512] = a["gla_wa_f"][l], a["gla_wa_b"][l]
        m[32, 0:256], m[32, 256:512] = a["gla_ba_f"][l], a["gla_ba_b"][l]
        wa.append(m)
        col = lambda v: v.reshape(-1, P).T
        eps, not0 = _np.full((P, 1), EPS, _np.float32), _np.ones((P, 1), _np.float32)
        not0[0] = 0
        cols.append(_np.concatenate([col(a["gla_norm"][l]), col(a["hy_conv_w"][l].reshape(-1)),
                                     col(a["hy_conv_b"][l]), col(a["final_norm"]), eps, not0], 1))
    x = _np.concatenate([a["x"][0], a["ctx"][0]], 0).T.reshape(KD, P, TOK).transpose(1, 0, 2)
    cond = _np.stack([a["c"][0], a["c_ctx"]], -1).reshape(KD, P, 2).transpose(1, 0, 2)
    gain = _np.concatenate([_np.tile(a["attn_qnorm"], (1, 8)), _np.tile(a["attn_knorm"], (1, 2))], 1)
    host = {
        "xT": x, "cond": cond, "w_in": _np.stack(w_in), "w_br": _np.stack(w_br), "wa": _np.stack(wa), "cols": _np.stack(cols),
        "b_ada": a["b_ada"].reshape(DEPTH, 24, P).transpose(2, 0, 1),
        "w_ada": _np.stack([tile(a["w_ada"][l]) for l in range(DEPTH)]),
        "w_out": _np.stack([tile(a["w_out"][l]) for l in range(DEPTH)]),
        "gain": gain, "f1": a["hy_f1_w"], "f2": a["hy_f2_w"], "f3": a["hy_f3_w"].reshape(DEPTH, 64, 4, BW),
        "c64": _np.stack([a["hy_f1_b"], a["hy_f1_freq"], a["hy_f2_b"], a["hy_f2_freq"]], -1), "skip": a["hy_skip"],
    }
    host.update(tables())

    def declare(nc):
        arrays, aps = {}, {}
        for name, v in host.items():
            v = _np.ascontiguousarray(v)
            arrays["in_" + name] = v
            aps[name] = nc.dram_tensor("in_" + name, v.shape, _mybir.dt.from_np(v.dtype), kind="ExternalInput").ap()
        aps["x_mid"] = nc.dram_tensor("x_mid", (P, KD, TOK), F32, kind="Internal").ap()
        aps["out"] = nc.dram_tensor("out_0", (KD, P, LAT), F32, kind="ExternalOutput").ap()
        return arrays, aps

    scratch = _bacc.Bacc("TRN2", target_bir_lowering=False, num_devices=1)
    known, stages = build_program(scratch, declare(scratch)[1])
    nc = _bacc.Bacc("TRN2", target_bir_lowering=False, num_devices=1)
    arrays, aps = declare(nc)
    build_program(nc, aps, known, [s for s in stages if s != "any"])
    r = _run(nc, [arrays], core_ids=[0])
    return r.results[0]["out_0"].reshape(D, LAT).T[None]
```

```python
import math
from contextlib import ExitStack

import numpy as np
import concourse.bass as bass
from concourse import mybir

F32 = mybir.dt.float32
F32R = mybir.dt.float32r
ALU = mybir.AluOpType
ACT = mybir.ActivationFunctionType
AX = mybir.AxisListType

P = 128
D = 1024
KD = D // P
DEPTH = 2
BW = 512
LAT, CTX = 512, 256
TOK = LAT + CTX
EPS = 1e-6
GRID_W = 64
STREAMS = {"lat": (0, LAT), "ctx": (LAT, CTX)}
LEVELS = [64, 32, 16, 8, 4, 2, 1]
FACTORS = {"lat": 4, "ctx": 2}
ROOT2 = math.sqrt(2.0)
TWO_PI_1, TWO_PI_2 = 6.28125, 0.0019350051879882812
TWO_PI_3 = 2 * math.pi - TWO_PI_1 - TWO_PI_2
ROUND_MAGIC = 1.5 * 2.0 ** 23
PI_BELOW = 3.1415925

HY_TILES = [("u", i) for i in range(12)] + [("hz", i) for i in range(4)]
GLA_TILES = [("ga", 0), ("gk", 0), ("gk", 1), ("gq", 0), ("gq", 1)] + [("gv", i) for i in range(4)] + [("gz", i) for i in range(4)]
ATT_TILES = [("ak", 0), ("av", 0)] + [("aq", i) for i in range(4)] + [("az", i) for i in range(4)]
GATE_TILES = [("m", 3 * j + b) for j in range(KD) for b in range(3)]
IN_TILES = HY_TILES + GLA_TILES + ATT_TILES + GATE_TILES
IN_INDEX = {t: i for i, t in enumerate(IN_TILES)}


def streams_of(layer):
    return ["ctx", "lat"] if layer < DEPTH - 1 else ["lat"]


def streams_for(layer, tile):
    return ["lat", "ctx"] if layer < DEPTH - 1 or tile[0] in ("ga", "gk", "gv", "ak", "av") else ["lat"]


def cores_of(layer):
    return [(s, o) for o in range(2) for s in streams_of(layer)]


ADA_ROWS = 4


def fillers(layer):
    at = {}
    u, hz = [("u", j) for j in range(12)], [("hz", j) for j in range(4)]
    att = [("ak", 0)] + [("aq", j) for j in range(4)] + [("av", 0)] + [("az", j) for j in range(4)]
    if layer == 0:
        ada = [("ada", 0, j) for j in range(24)]
        at["start",] = [("ada_rows", g) for g in range(ADA_ROWS - 1)]
        at["normed",] = [("ada_rows", ADA_ROWS - 1)] + [("ada_turn", g) for g in range(ADA_ROWS)]
        for i, p in enumerate([("mlp", s, i) for s in streams_of(0) for i in range(2)]):
            at[p] = u[i:i + 1]
        at["sum", "ctx", 0, 0] = [("uT", 0)]
        at["taps", "ctx", 0, 2] = u[4:5]
        at["taps", "ctx", 0, 3] = u[5:6]
        at["sum", "ctx", 0, 1] = u[6:7]
        at["parts", "ctx", 0] = u[7:8] + [("uT", 1)]
        at["spec", "ctx", 0] = u[8:9]
        at["taps", "lat", 0, 1] = u[9:10]
        at["taps", "lat", 0, 5] = u[10:11]
        at["parts", "lat", 0] = u[11:]
        at["spec", "lat", 0] = hz[0:1]
        at["taps", "ctx", 1, 0] = hz[1:2]
        at["taps", "ctx", 1, 2] = hz[2:3]
        at["parts", "ctx", 1] = hz[3:]
        for i in range(3):
            at["level", "ctx", i] = att[i:i + 1]
        for i in range(2):
            at["level", "lat", i] = att[3 + i:4 + i]
        at["prefix",] = att[5:]
        for i in range(4):
            at.setdefault(("level", "ctx", i), []).extend(ada[2 * KD + 2 * i:2 * KD + 2 * i + 2])
        ada = [("ada", 1, j) for j in range(24)]
        for i in range(7):
            at.setdefault(("level", "lat", i), []).extend(ada[3 * i:3 * i + 3])
        ada = ada[21:]
        for j in range(KD):
            at["merge", j] = ada[j::KD]
    else:
        at["mlp", "lat", 0] = u[0:1]
        at["mlp", "lat", 1] = u[1:3]
        at["taps", "lat", 0, 0] = u[3:4]
        at["sum", "lat", 0, 0] = [("uT", 0)]
        for i in range(3):
            at["taps", "lat", 0, 4 + i] = u[4 + i:5 + i]
        at["sum", "lat", 0, 1] = u[7:8]
        at["parts", "lat", 0] = [("uT", 1)]
        at["spec", "lat", 0] = u[8:9]
        at["taps", "lat", 1, 0] = u[9:10]
        at["taps", "lat", 1, 1] = u[10:11]
        at["sum", "lat", 1, 0] = u[11:]
        for i in range(3):
            at["taps", "lat", 1, 4 + i] = hz[i:i + 1]
        at["parts", "lat", 1] = hz[3:]
        for i, (a, b) in enumerate([(0, 1), (1, 2), (2, 3), (3, 4), (4, 5)]):
            at["level", "lat", i] = att[a:b]
        at["prefix",] = att[5:]
    return at


FILL = [fillers(l) for l in range(DEPTH)]


class Counts:

    def __init__(self, nc, stack, known=None, stages=()):
        self.nc, self.stack, self.known = nc, stack, known
        self.sems, self.count, self.at, self.latest, self.engine = {}, {}, {}, {}, None
        for s in stages:
            self.sem(s)

    def sem(self, stage):
        if stage not in self.sems:
            self.sems[stage] = self.stack.enter_context(self.nc.semaphore(stage))
            self.count[stage] = 0
        return self.sems[stage]

    def done(self, stage, *key, also=(), by=1):
        sem = self.sem(stage)
        self.count[stage] += by
        for label in [(stage, *key), *also]:
            self.at[label] = (stage, self.count[stage])
        if by == 1:
            self.latest[self.engine] = (stage, self.count[stage])
        return sem, by

    def after(self, *label):
        if self.known is None:
            return self.sem("any"), 1
        stage, n = self.known[label]
        return self.sem(stage), n

    def phase_end(self, phase):
        self.at[("end", self.engine, phase)] = self.latest[self.engine]


class Psum:

    def __init__(self, counts, banks):
        self.c, self.banks, self.next, self.holder = counts, banks, 0, {}
        self.where = {}

    def take(self, pe, *key, n=1, at=None):
        if at is None:
            at = self.next
            if at % 8 + n > 8 or (n == 2 and at % 2):
                at += 1
            self.next = (at + n) % 8
        at %= 8
        for b in range(at, at + n):
            if b in self.holder:
                pe.wait_ge(*self.c.after("freed", *self.holder[b]))
            self.holder[b] = key
        self.where[key] = (at, n)
        return self.banks[:, at:at + n, :].rearrange("p b n -> p (b n)")

    def of(self, *key):
        at, n = self.where[key]
        return self.banks[:, at:at + n, :].rearrange("p b n -> p (b n)")


def carve(tensor, at, *shape):
    n = int(np.prod(shape))
    v = tensor[:, at:at + n]
    if len(shape) == 2:
        v = v.rearrange("p (a b) -> p a b", a=shape[0])
    if len(shape) == 3:
        v = v.rearrange("p (a b c) -> p a b c", a=shape[0], b=shape[1])
    if len(shape) == 4:
        v = v.rearrange("p (a b c d) -> p a b c d", a=shape[0], b=shape[1], c=shape[2])
    return v, at + n


def build_program(nc, d, known=None, stages=()):
    stack = ExitStack()
    with stack:
        c = Counts(nc, stack, known, stages)

        def sb(name, *shape, dt=F32):
            return stack.enter_context(nc.sbuf_tensor(name, [P, *shape], dt))

        H = sb("H", KD, TOK)
        YB = sb("YB", 12 * TOK)
        YBT = YB[:, :].rearrange("p (a t) -> p a t", a=12)
        NSLOT = 4
        RING = sb("RING", NSLOT, KD, P)
        TRI = sb("TRI", 2, P)
        IDENT = sb("IDENT", P)
        ONES = sb("ONES", 3, P)
        MASK = sb("MASK", len(LEVELS), P, dt=mybir.dt.uint8)
        DIAG2 = sb("DIAG2", P)
        COLS = sb("COLS", 60)
        ADAS = sb("ADAS", DEPTH, 24, 2)
        BADA = sb("BADA", DEPTH, 24)
        SC = sb("SC", KD, 2)
        SMALL = sb("SMALL", 256)
        ARENA_N = 32136
        with nc.sbuf_tensor("AR", [P, ARENA_N], F32) as AR:
            pass
        with ExitStack() as attn_stack:
            def sba(name, *shape, dt=F32R):
                return attn_stack.enter_context(nc.sbuf_tensor(name, [P, *shape], dt))

            PTS = sba("PTS", 4, TOK)
            sba("AR_RAW", 6 * 640 + 6 * P - 4 * TOK, dt=F32)
            QKS = sba("QKS", 12, TOK)
            VS = sba("VS", 2, 12 * P)
        sb("AR_HEAD", ARENA_N - (4 * KD * P + 2 * KD * TOK))
        WS = sb("WS", 4, KD * P, dt=F32R)
        HS = sb("HS", 2 * KD, TOK, dt=F32R)
        banks = stack.enter_context(nc.psum_tensor("banks", [P, 8, 512], F32))
        ps = Psum(c, banks)
        GNORM, CONVW, CONVB, FINALN = COLS[:, 0:1], COLS[:, 1:37], COLS[:, 37:49], COLS[:, 49:57]
        EPSC, NOT0 = COLS[:, 57:58], COLS[:, 58:59]
        TCOL, _ = carve(SMALL, 0, 12)
        C64, _ = carve(SMALL, 12, 4)
        NMAX, _ = carve(SMALL, 16, 48)
        SUMS, _ = carve(SMALL, 64, 48)
        RINV, _ = carve(SMALL, 112, 48)
        MSQ, _ = carve(SMALL, 160, 60)
        DEC, _ = carve(SMALL, 220, 2, 2, 4)

        X, n0 = carve(AR, 0, KD, TOK)
        SQ, n = carve(AR, n0, 2, TOK)
        RS, n = carve(AR, n, TOK)
        YM = H
        BRW, n = carve(AR, n0, 2, 12, P)
        MG, n = carve(AR, n, 2, 3, TOK)
        MT, n = carve(AR, n, 2, TOK)
        OUTB, _ = carve(AR, n0 + 3 * TOK, KD, LAT)
        assert n <= ARENA_N - (4 * KD * P + 2 * KD * TOK)
        UD, n = carve(AR, 0, 4, TOK)
        TOKM, n = carve(AR, n, 2, 6, BW)
        assert n >= n0 + 3 * TOK
        G, n = carve(AR, n, 8, LAT)
        FM, n = carve(AR, n, 16, P)
        FW, n = carve(AR, n, 8, BW)
        EMB, _ = carve(FW.rearrange("p a b -> p (a b)"), 0, 1536)
        R, n = carve(AR, n, 8, BW)
        MASK32 = carve(R.rearrange("p a b -> p (a b)"), 4 * BW, len(LEVELS), P)[0].bitcast(mybir.dt.int32)
        HX, _ = carve(R.rearrange("p a b -> p (a b)"), 0, 3, 1024)
        FH, n = carve(AR, n, 9, BW)
        H2, n = carve(AR, n, 1536)
        HZ, n = carve(AR, n, 2, TOK)
        Y = FW
        assert n <= ARENA_N, n
        F3, n = carve(YB, 0, 4, BW)
        TT, n = carve(YB, n, 4, BW)
        RN, n = carve(YB, n, 2, BW)
        DEL, n = carve(YB, n, BW)
        F12, n = carve(YB, n, 2, 64)
        assert n <= 8 * TOK
        ROWS, _ = carve(YB, 8 * TOK, ADA_ROWS, BW)
        SKIP, _ = carve(TT.rearrange("p a b -> p (a b)"), 3 * BW, BW)
        QK, n = carve(AR, 0, 6, 640)
        VA, nqk = carve(AR, n, 6, P)
        TA, nta = carve(AR, nqk + 12 * TOK, 4, 4 * 320)
        PR, n = carve(AR, nqk + 12 * TOK + 2 * 12 * P, 2, TOK)
        n = max(n, nta)
        GAIN, n = carve(AR, n, 640)
        ROPE, n = carve(AR, n, 2, 4, 32)
        assert n <= ARENA_N - 2 * KD * TOK
        GK, n = carve(AR, nqk, 2, TOK)
        GQ, n = carve(AR, n, 2, TOK)
        GV, n = carve(AR, n, 6, BW)
        GA, n = carve(AR, n, TOK)
        WA, n = carve(AR, n, BW)
        GG, n = carve(AR, n, 4, BW)
        ATT = GG
        B, n = carve(AR, n, 2, 2, LAT)
        EL, n = carve(AR, n, 2, 2, 2 * LAT)
        QH, n = carve(AR, n, 2, 2, LAT)
        KH, nk = carve(AR, n, 2, 2, LAT)
        OS, n = carve(AR, n, 8, BW)
        KT, n = carve(AR, n, 2, 2, LAT)
        ST, n = carve(AR, n, 2, 2, 6 * P)
        assert n <= ARENA_N, n

        block = stack.enter_context(nc.Block())

        PHASES = []
        for l in range(DEPTH):
            PHASES += [("hyena", l), ("gla", l), ("attn", l), ("merge", l)]
        PHASES.append(("norm", DEPTH))
        BEFORE = dict(zip(PHASES[1:], PHASES[:-1]))

        ORDER = []
        SPLIT = {}
        RAW = 3
        NSPLIT = 3 * KD - RAW + KD

        def barrier(eng, *phase):
            if phase in BEFORE:
                for e in ("pe", "act", "dve", "pool"):
                    if e != c.engine:
                        eng.wait_ge(*c.after("end", e, BEFORE[phase]))

        def prev_conv(l, s, o):
            return (l, *cores_of(l)[cores_of(l).index((s, o)) - 1])

        def pair_group(nt, g):
            b, u = divmod(g, nt // 2)
            return [(64 * b, 2 * u + i, p, (2 * i + p) * P) for i in range(2) for p in range(2)]

        def att_of(nt, h, t):
            col = (2 * (t % 2) + h // 2) * P
            return ATT[:, (h % 2) * (nt // 2) + t // 2, col:col + P]

        def filter_blocks(s, f):
            if s == "ctx" or f < 2:
                return R[:, 2 * f], R[:, 2 * f + 1]
            return (FW[:, 6], FW[:, 7]) if f == 2 else (R[:, 4], R[:, 5])

        def signal_blocks(s, f, o):
            if s == "ctx":
                return TOKM[:, 0, 4], TOKM[:, 0, 5]
            return R[:, 2 * f], R[:, 2 * f + 1]

        def attn_steps(l):
            return [(s, t, hh) for s in ("lat", "ctx") if s in streams_of(l) for t in range(STREAMS[s][1] // P) for hh in range(8)]

        @block.tensor
        def _(pe):
            c.engine = "pe"
            n_w = [0]

            def weights(l, kind, j):
                n = n_w[0]
                ORDER.append((l, kind, j))
                n_w[0] += 1
                pe.wait_ge(*c.after(f"load_slot{n % NSLOT}", n))
                return RING[:, n % NSLOT], ("weights_used", n)

            def project(l, kind, j, m=P):
                w, used = weights(l, kind, j)
                ss = streams_for(l, (kind, j))
                for s in ss:
                    off, T = STREAMS[s]
                    out = ps.take(pe, kind, l, j, s)
                    for k in range(KD):
                        mm = pe.matmul(out[0:m, 0:T], w[:, k, 0:m], H[:, k, off:off + T], start=k == 0, stop=k == KD - 1)
                    mm.then_inc(*c.done(kind, l, j, s, also=[used] if s == ss[-1] else []))

            def split_product(l, i, psum_key, label):
                SPLIT[l, i] = n_w[0]
                n_w[0] += 1
                pe.wait_ge(*c.after("weight_low", l, i))
                ss = streams_for(l, ("m", 0))
                for s in ss:
                    off, T = STREAMS[s]
                    out = ps.take(pe, *psum_key, s)
                    for k in range(KD):
                        if i == 0 and s == ss[0]:
                            pe.wait_ge(*c.after("h_low", l, k))
                        if i == 3 * KD - RAW and s == ss[0]:
                            pe.wait_ge(*c.after("merged_low", l, k))
                        for n, (a, b) in enumerate(((0, 0), (0, 1), (1, 0))):
                            mm = pe.matmul(out[:, 0:T], WS[:, 2 * (i % 2) + a, k * P:(k + 1) * P], HS[:, b * KD + k, off:off + T],
                                           start=(k, n) == (0, 0), stop=(k, n) == (KD - 1, 2))
                    mm.then_inc(*c.done(*label, s, also=[("split_used", l, i)] if s == ss[-1] else []))

            def project_tokens(l, kind, j):
                w, used = weights(l, kind, j)
                ss = streams_for(l, (kind, j))
                for s in ss:
                    off, T = STREAMS[s]
                    out = ps.take(pe, kind, l, j, s)
                    for t in range(T // P):
                        for k in range(KD):
                            mm = pe.matmul(out[:, t * P:(t + 1) * P], H[:, k, off + t * P:off + (t + 1) * P], w[:, k, :],
                                           start=k == 0, stop=k == KD - 1)
                    mm.then_inc(*c.done(kind, l, j, s, also=[used] if s == ss[-1] else []))

            def norm(l, ss):
                outs = {s: ps.take(pe, "ms", l, s) for s in ss}
                for k in range(KD):
                    pe.wait_ge(*c.after("squares", l, k))
                    for s in ss:
                        off, T = STREAMS[s]
                        mm = pe.matmul(outs[s][:, 0:T], ONES[:, 0, :], SQ[:, k % 2, off:off + T], start=k == 0, stop=k == KD - 1)
                        mm.then_inc(*c.done("ms", l, s, k, also=([("squares_used", l, k)] if s == ss[-1] else []) +
                                            ([("ms", l, s)] if k == KD - 1 else [])))

            def ada_tile(l, j):
                pe.wait_ge(*c.after("cond_silu"))
                w, used = weights(l, "ada", j)
                out = ps.take(pe, "ada", l, j)
                for k in range(KD):
                    mm = pe.matmul(out[:, 0:2], w[:, k, :], SC[:, k, :], start=k == 0, stop=k == KD - 1)
                mm.then_inc(*c.done("ada", l, j, also=[used]))

            def ada_rows(g):
                pe.wait_ge(*c.after("cond_silu"))
                out = ps.take(pe, "ada_rows", g)
                for jj in range(4):
                    w, used = weights(0, "ada", 4 * g + jj)
                    for k in range(KD):
                        mm = pe.matmul(out[0:2, jj * P:(jj + 1) * P], SC[:, k, :], w[:, k, :], start=k == 0, stop=k == KD - 1)
                    mm.then_inc(*c.done("ada_rows", g, jj, also=[used]))

            def ada_turn(g):
                pe.wait_ge(*c.after("rows_kept", g))
                out = ps.take(pe, "ada_turned", g)
                for jj in range(4):
                    mm = pe.transpose(out[:, 2 * jj:2 * jj + 2], ROWS[0:2, g, jj * P:(jj + 1) * P], IDENT[0:2, 0:2])
                mm.then_inc(*c.done("ada_turned", g))

            def fill(l, *point):
                for kind, *j in FILL[l].get(point, []):
                    if kind == "ada":
                        ada_tile(*j)
                    elif kind == "ada_rows":
                        ada_rows(*j)
                    elif kind == "ada_turn":
                        ada_turn(*j)
                    elif kind in ("ak", "av", "aq"):
                        project_tokens(l, kind, *j)
                    elif kind == "uT":
                        token_major(l, *j)
                    else:
                        project(l, kind, *j)

            def token_major(l, which):
                for s in streams_of(l):
                    off, T = STREAMS[s]
                    pe.wait_ge(*c.after("short_conv", l, 4 * which + 3, s))
                    for t in range(T // P):
                        out = ps.take(pe, "uT", l, which, s, t)
                        for j in range(4):
                            mm = pe.transpose(out[:, j * P:(j + 1) * P], UD[:, j, off + t * P:off + (t + 1) * P], IDENT[:, :])
                        mm.then_inc(*c.done("uT", l, which, s, t))

            def filter_nets(l):
                pe.wait_ge(*c.after("load_hy", l, "all"))
                for s in streams_of(l):
                    T = STREAMS[s][1]
                    for layer in range(2):
                        for h in range(2 * T // BW):
                            out = ps.take(pe, "ffn", l, s, layer, h)
                            at = (0 if s == "lat" else 2 * LAT) + h * BW
                            if layer == 0:
                                mm = pe.matmul(out[0:64, :], F12[0:33, 0], EMB[0:33, at:at + BW], start=True, stop=True)
                            else:
                                pe.wait_ge(*c.after("sine", l, s, 0))
                                mm = pe.matmul(out[0:64, :], F12[0:64, 1], H2[0:64, at:at + BW], start=True, stop=True)
                            mm.then_inc(*c.done("ffn", l, s, layer, h))
                        fill(l, "mlp", s, layer)

            def filter_spectrum(l, s, o):
                nt, nf = STREAMS[s][1] // P, FACTORS[s]
                pe.wait_ge(*c.after("sine", l, s, 1))
                base = 0 if s == "lat" else 2 * LAT

                def magnitudes(r, m):
                    pe.wait_ge(*c.after("magnitude", l, s, o, r * nt + m))
                    mm = pe.matmul(total, ONES[:, 2, :], TT[:, 2], start=m == 0, stop=m == nt - 1)
                    mm.then_inc(*c.done("tap_sum", l, s, o, r, m, also=[("tap_sum", l, s, o, r)] if m == nt - 1 else []))

                for r in range(2):
                    total = ps.take(pe, "tap_sum", l, s, o, r)
                    for m in range(nt):
                        out = ps.take(pe, "taps", l, s, o, r * nt + m)
                        at = base + (r * nt + m) * P
                        mm = pe.matmul(out, H2[0:64, at:at + P], F3[0:64, 2 * o + r], start=True, stop=True)
                        mm.then_inc(*c.done("taps", l, s, o, r * nt + m))
                        if m:
                            magnitudes(r, m - 1)
                        fill(l, "taps", s, o, r * nt + m)
                    magnitudes(r, nt - 1)
                    fill(l, "sum", s, o, r)
                fill(l, "parts", s, o)
                pe.wait_ge(*c.after("filter_parts", l, s, o))
                for f in range(nf):
                    blocks = filter_blocks(s, f)
                    for p in range(2):
                        out = ps.take(pe, "fdft", l, s, o, f, p)
                        for b in range(2):
                            mm = pe.matmul(out, FM[:, 4 * f + 2 * b + p], blocks[b], start=b == 0, stop=b == 1)
                        mm.then_inc(*c.done("fdft", l, s, o, f, p))

            def convolve(l, s, o):
                off, T = STREAMS[s]
                nt, nf = T // P, FACTORS[s]
                pe.wait_ge(*c.after("signal_parts", l, s, o))
                for f in range(nf):
                    blocks = signal_blocks(s, f, o)
                    for p in range(2):
                        out = ps.take(pe, "zdft", l, s, o, f, p)
                        for b in range(2):
                            mm = pe.matmul(out, FM[:, 4 * f + 2 * b + p], blocks[b], start=b == 0, stop=b == 1)
                        mm.then_inc(*c.done("zdft", l, s, o, f, p))
                fill(l, "spec", s, o)
                pe.wait_ge(*c.after("spectrum", l, s, o))
                for m in range(nt if o == 0 else 4):
                    out = ps.take(pe, "conv", l, s, o, m)
                    for q in range(2 * nf):
                        if o == 0:
                            mm = pe.matmul(out, G[:, q, m * P:(m + 1) * P], Y[:, q], start=q == 0, stop=q == 2 * nf - 1)
                        else:
                            mm = pe.matmul(out[:, 0:T], Y[:, q, m * P:(m + 1) * P], G[:, q, 0:T], start=q == 0, stop=q == 2 * nf - 1)
                    mm.then_inc(*c.done("conv", l, s, o, m))

            def hyena(l):
                norm(l, ["lat", "ctx"])
                fill(l, "normed")
                pe.wait_ge(*c.after("h", l, "all"))
                filter_nets(l)
                for s, o in cores_of(l):
                    filter_spectrum(l, s, o)
                    convolve(l, s, o)

            def gla(l):
                for t in GLA_TILES:
                    if t[0] == "ga":
                        project(l, *t, m=32)
                    elif t[0] == "gv":
                        project_tokens(l, *t)
                    else:
                        project(l, *t)
                for s in ("ctx", "lat"):
                    off, T = STREAMS[s]
                    nt = T // P
                    full = s in streams_of(l)
                    pe.wait_ge(*c.after("load_gla", l))
                    pe.wait_ge(*c.after("rank", l, s))
                    for t in range(nt):
                        out = ps.take(pe, "gpre", l, s, t)
                        pe.matmul(out, GA[0:33, off + t * P:off + (t + 1) * P], WA[0:33], start=True, stop=True)\
                          .then_inc(*c.done("gpre", l, s, t))
                    for r in range(2):
                        for p in range(2):
                            out = ps.take(pe, "cum", l, s, r, p)
                            for t in range(nt):
                                pe.wait_ge(*c.after("log_decay", l, s, t))
                                mm = pe.matmul(out[:, t * P:(t + 1) * P], GG[:, t, r * 256 + p * P:r * 256 + (p + 1) * P],
                                               TRI[:, r, :], start=True, stop=True)
                            mm.then_inc(*c.done("cum", l, s, r, p))
                    if full:
                        pe.wait_ge(*c.after("qk_ready", l, s))
                        for t in range(nt):
                            out = ps.take(pe, "pairs", l, s, -1, t)
                            for b, chunk, p, col in pair_group(nt, t):
                                cols = slice(off + chunk * P, off + (chunk + 1) * P)
                                mm = pe.matmul(out[:, col:col + P], GK[b:b + 64, p, cols], GQ[b:b + 64, p, cols], start=True, stop=True)
                            mm.then_inc(*c.done("pairs", l, s, -1, t))
                    for r in range(2):
                        for p in range(2):
                            pe.wait_ge(*c.after("k_decayed", l, s))
                            out = ps.take(pe, "kT", l, s, r, p)
                            for t in range(nt):
                                mm = pe.transpose(out[:, t * P:(t + 1) * P], KH[:, r, p, t * P:(t + 1) * P], IDENT[:, :])
                            mm.then_inc(*c.done("kT", l, s, r, p))
                    for r in range(2):
                        for i in range(nt if s == "ctx" else nt - 1):
                            t = i if r == 0 else nt - 1 - i
                            pe.wait_ge(*c.after("k_tokens", l, s, r, 1))
                            out = ps.take(pe, "kv", l, s, r, i)
                            for h in range(4):
                                b, p = 64 * (h % 2), h // 2
                                mm = pe.matmul(out[b:b + 64, p * P:(p + 1) * P], KT[:, r, p, t * P + b:t * P + b + 64],
                                               GV[:, off // P + t, h * P:(h + 1) * P], start=True, stop=True)
                            mm.then_inc(*c.done("kv", l, s, r, i))
                    if not full:
                        continue
                    for v in range(len(LEVELS)):
                        fill(l, "level", s, v)
                        pe.wait_ge(*c.after("level_q", l, s, v))
                        pe.wait_ge(*c.after("level_k", l, s, v))
                        for t in range(nt):
                            out = ps.take(pe, "pairs", l, s, v, t)
                            for b, chunk, p, col in pair_group(nt, t):
                                mm = pe.matmul(out[:, col:col + P], EL[b:b + 64, v % 2, p, T + chunk * P:T + (chunk + 1) * P],
                                               EL[b:b + 64, v % 2, p, chunk * P:(chunk + 1) * P], start=True, stop=True)
                            mm.then_inc(*c.done("pairs", l, s, v, t))
                    pe.wait_ge(*c.after("pairs_all", l, s))
                    pe.wait_ge(*c.after("state", l, s, 1, nt - 2 if s == "lat" else nt - 1, 1))
                    for h in range(4):
                        b, p = 64 * (h % 2), h // 2
                        out = ps.take(pe, "o", l, s, h)
                        for t in range(nt):
                            cols = slice(t * P, (t + 1) * P)
                            first = 0 if s == "ctx" else 2
                            pe.matmul(out[:, cols], GV[:, off // P + t, h * P:(h + 1) * P], att_of(nt, h, t), start=True, stop=False)
                            for r in range(2):
                                at = first + (t if r == 0 else nt - 1 - t)
                                mm = pe.matmul(out[:, cols], ST[b:b + 64, r, p, at * P:(at + 1) * P], QH[b:b + 64, r, p, cols],
                                               start=False, stop=r == 1)
                        mm.then_inc(*c.done("o", l, s, h))
                    for h in range(4):
                        gla_ms(l, s, h, T)

            def gla_ms(l, s, h, T):
                pe.wait_ge(*c.after("o_sq", l, s, h))
                out = ps.take(pe, "oms", l, s, h)
                pe.matmul(out[:, 0:T], ONES[:, 1, :], OS[:, 4 + h, 0:T], start=True, stop=True).then_inc(*c.done("oms", l, s, h))

            def attn(l):
                fill(l, "prefix")
                for s in ("lat", "ctx"):
                    off, T = STREAMS[s]
                    pe.wait_ge(*c.after("qk_normed", l, s))
                    for j in ([4] if s not in streams_of(l) else [4, 0, 1, 2, 3]):
                        out = ps.take(pe, "qkT", l, s, j)
                        for t in range(T // P):
                            mm = pe.transpose(out[:, t * P:(t + 1) * P], QK[:, off // P + t, j * P:(j + 1) * P], IDENT[:, :])
                        mm.then_inc(*c.done("qkT", l, s, j))
                steps = attn_steps(l)

                def scores(i):
                    s, t, hh = steps[i]
                    off, b = STREAMS[s][0] + t * P, hh % 2
                    if i == 0:
                        for s2 in ("lat", "ctx"):
                            pe.wait_ge(*c.after("qkT_kept", l, s2, 4))
                    if t == 0 and hh == 0:
                        pe.wait_ge(*c.after("qkT_kept", l, s, 3))
                    out = ps.take(pe, "score", l, s, t, hh, n=2, at=2 * (i % 2))
                    for a, e in ((0, 512), (512, 768)) if s == "lat" else ((512, 768),):
                        for part in range(2):
                            mm = pe.matmul(out[:, a - (0 if s == "lat" else LAT):e - (0 if s == "lat" else LAT)], QKS[:, hh, off:off + P], QKS[:, 8 + 2 * b + part, a:e],
                                           start=part == 0, stop=part == 1)
                    mm.then_inc(*c.done("score", l, s, t, hh))

                def transposes(i):
                    s, t, hh = steps[i]
                    pe.wait_ge(*c.after("prob_scaled", l, s, t, hh))
                    out = ps.take(pe, "probT", l, s, t, hh, n=2, at=4)
                    for k in range(6 if s == "lat" else 2):
                        mm = pe.transpose(out[:, k * P:(k + 1) * P], PR[:, i % 2, k * P:(k + 1) * P], IDENT[:, :])
                    mm.then_inc(*c.done("probT", l, s, t, hh))

                def values(i):
                    s, t, hh = steps[i]
                    pe.wait_ge(*c.after("probT_kept", l, s, t, hh))
                    if i == 0:
                        pe.wait_ge(*c.after("v_low", l))
                    if hh % 4 == 0:
                        values.out = ps.take(pe, "ao", l, s, t, hh // 4, at=6 + hh // 4)
                    tiles = range(6) if s == "lat" else range(4, 6)
                    for k in tiles:
                        for n, (a, v) in enumerate(((0, 0), (0, 1), (1, 0))):
                            at = (k - tiles[0]) * P
                            mm = pe.matmul(values.out[:, (hh % 4) * P:(hh % 4 + 1) * P], VS[:, v, (2 * k + hh % 2) * P:(2 * k + hh % 2 + 1) * P],
                                           PTS[:, 2 * (i % 2) + a, at:at + P],
                                           start=(k, n) == (tiles[0], 0), stop=(k, n) == (tiles[-1], 2))
                    mm.then_inc(*c.done("ao", l, s, t, hh, also=[("ao_group", l, s, t, hh // 4)] if hh % 4 == 3 else []))

                scores(0)
                scores(1)
                for i in range(len(steps)):
                    transposes(i)
                    if i + 2 < len(steps):
                        scores(i + 2)
                    if i:
                        values(i - 1)
                values(len(steps) - 1)

            def merge(l):
                ss = streams_for(l, ("m", 0))
                for j in range(KD):
                    for b in range(3):
                        g = 3 * j + b
                        if b == 2:
                            fill(l, "merge", j)
                        if g < RAW:
                            project(l, "m", g)
                        else:
                            ORDER.append((l, "m", g))
                            split_product(l, g - RAW, ("m", l, g), ("m", l, g))
                    ORDER.append((l, "branch", j))
                    pe.wait_ge(*c.after(f"load_branch{j % 2}", l, j))
                    for b in range(3):
                        for s in ss:
                            off, T = STREAMS[s]
                            out = ps.take(pe, "branch", l, j, b, s)
                            for k in range(4):
                                mm = pe.matmul(out[:, 0:T], BRW[:, j % 2, 4 * b + k, :], YBT[:, 4 * b + k, off:off + T], start=k == 0, stop=k == 3)
                            mm.then_inc(*c.done("branch", l, j, b, s, also=[("branch_used", l, j)] if b == 2 and s == ss[-1] else []))
                for j in range(KD):
                    ORDER.append((l, "out", j))
                    split_product(l, 3 * KD - RAW + j, ("out", l, j), ("out", l, j))

            fill(0, "start")
            pe.wait_ge(*c.after("load_const", "all"))
            for l in range(DEPTH):
                hyena(l)
                c.phase_end(("hyena", l))
                gla(l)
                c.phase_end(("gla", l))
                attn(l)
                c.phase_end(("attn", l))
                merge(l)
                c.phase_end(("merge", l))
            norm(DEPTH, ["lat"])
            c.phase_end(("norm", DEPTH))

        @block.sync
        def _(sp):
            c.engine = "sp"
            sources = {"ada": d["w_ada"], "out": d["w_out"], "branch": d["w_br"]}
            ring = []
            for n, (l, kind, j) in enumerate(ORDER):
                if kind == "branch":
                    if j >= 2:
                        sp.wait_ge(*c.after("branch_used", l, j - 2))
                    else:
                        for e in ("dve", "act", "pe"):
                            sp.wait_ge(*c.after("end", e, ("attn", l)))
                    sp.dma_start(BRW[:, j % 2], sources[kind][l, j]).then_inc(*c.done(f"load_branch{j % 2}", l, j, by=16))
                    continue
                m = len(ring)
                if m >= NSLOT:
                    sp.wait_ge(*c.after("weights_used", m - NSLOT))
                src = sources[kind][l, j] if kind in sources else d["w_in"][l, IN_INDEX[kind, j]]
                sp.dma_start(RING[:, m % NSLOT], src).then_inc(*c.done(f"load_slot{m % NSLOT}", m, by=16))
                ring.append((l, kind, j))
            for k in range(KD):
                sp.wait_ge(*c.after("final", k))
                sp.dma_start(d["out"][k], OUTB[:, k]).then_inc(*c.done("store_out", k, by=16))
            sp.wait_ge(*c.after("store_out", KD - 1))

        @block.scalar
        def _(act):
            c.engine = "act"
            chain = [0]

            def link(ins):
                ins.then_inc(*c.done("act_chain", chain[0]))
                act.wait_ge(*c.after("act_chain", chain[0]))
                chain[0] += 1

            def norm(l, ss):
                off, T = (0, TOK) if len(ss) == 2 else (0, LAT)
                if l == DEPTH:
                    barrier(act, "norm", l)
                for k in range(KD):
                    if k >= 2:
                        act.wait_ge(*c.after("squares_used", l, k - 2))
                    act.activation(SQ[:, k % 2, off:off + T], X[:, k, off:off + T], ACT.Square).then_inc(*c.done("squares", l, k))
                for s in ss:
                    o, t = STREAMS[s]
                    act.wait_ge(*c.after("ms", l, s))
                    act.wait_ge(*c.after("squares_used", l, KD - 1))
                    link(act.activation(SQ[:, 0, o:o + t], ps.of("ms", l, s)[:, 0:t], ACT.Ln, bias=EPSC))
                    act.activation(RS[:, o:o + t], SQ[:, 0, o:o + t], ACT.Exp, scale=-0.5).then_inc(
                        *c.done("rms", l, s, also=[("freed", "ms", l, s)]))

            def load(name, dst, src, *key):
                act.dma_start(dst, src).then_inc(*c.done("load_" + name, *key, by=16))

            def start():
                load("cond", SC[:, :, :], d["cond"])
                load("x", X, d["xT"], 0)
                load("const", BADA[:, :, :], d["b_ada"])
                load("const", TRI[:, :, :], d["tri"])
                load("const", IDENT[:, :], d["ident"])
                load("const", ONES[:, :, :], d["ones"])
                load("const", DIAG2[:, :], d["diag2"])
                load("const", TCOL, d["tcol"], "all")
                load("mask", MASK32, d["mask"])
                act.wait_ge(*c.after("load_cond"))
                cond = SC[:, :, :].rearrange("p a b -> p (a b)")
                link(act.activation(RS[:, 0:16], cond, ACT.Silu))
                act.activation(cond, RS[:, 0:16], ACT.Copy).then_inc(*c.done("cond_silu"))

            def fill(l, *point):
                for kind, *j in FILL[l].get(point, []):
                    if kind == "u":
                        conv_centre(l, *j)
                    elif kind == "uT":
                        token_major(l, *j)
                    elif kind == "hz":
                        branch_gate(l, *j)
                    elif kind[0:3] != "ada":
                        keep_attn(l, kind, *j)

            def token_major(l, which):
                for s in streams_of(l):
                    o = STREAMS[s][0] // P
                    for t in range(STREAMS[s][1] // P):
                        act.wait_ge(*c.after("uT", l, which, s, t))
                        act.activation(TOKM[:, which, o + t], ps.of("uT", l, which, s, t), ACT.Copy).then_inc(
                            *c.done("u_tokens", l, which, s, t, also=[("freed", "uT", l, which, s, t)]))

            def branch_gate(l, j):
                for s in streams_for(l, ("hz", j)):
                    off, T = STREAMS[s]
                    if j >= 2:
                        act.wait_ge(*c.after("z_used", l, j - 2, s))
                    act.wait_ge(*c.after("hz", l, j, s))
                    act.activation(HZ[:, j % 2, off:off + T], ps.of("hz", l, j, s)[:, 0:T], ACT.Silu).then_inc(
                        *c.done("hz_silu", l, j, s, also=[("freed", "hz", l, j, s)]))

            def keep_attn(l, kind, j):
                for s in streams_for(l, (kind, j)):
                    off, T = STREAMS[s]
                    act.wait_ge(*c.after(kind, l, j, s))
                    src = ps.of(kind, l, j, s)[:, 0:T]
                    if kind == "az":
                        act.activation(YBT[:, 4 + j, off:off + T], src, ACT.Silu).then_inc(
                            *c.done("az_kept", l, j, s, also=[("freed", kind, l, j, s)]))
                        continue
                    a, b = off // P, (off + T) // P
                    col = 0 if kind == "av" else (4 if kind == "ak" else j) * P
                    dst = VA[:, a:b] if kind == "av" else QK[:, a:b, col:col + P]
                    act.activation(dst, src.rearrange("p (t n) -> p t n", n=P), ACT.Copy).then_inc(
                        *c.done("proj_kept", l, kind, j, s, also=[("freed", kind, l, j, s)]))

            def begin(l):
                barrier(act, "hyena", l)
                load("cols", COLS[:, 0:59], d["cols"][l], l)
                load("hy", C64[0:64], d["c64"][l], l, 2)
                load("hy", EMB[0:33], d["emb"], l, 3)
                load("hy", F12[0:33, 0], d["f1"][l], l, 4)
                load("hy", F12[0:64, 1], d["f2"][l], l, 5)
                load("hy", F3[0:64], d["f3"][l], l, 6)

            def filter_nets(l):
                for s in streams_of(l):
                    T2 = 2 * STREAMS[s][1]
                    base = 0 if s == "lat" else 2 * LAT
                    for layer in range(2):
                        act.wait_ge(*c.after("reduced", l, s, layer))
                        act.activation(H2[0:64, base:base + T2], HX[0:64, 2, 0:T2], ACT.Sin).then_inc(*c.done("sine", l, s, layer))
                        fill(l, "mlp", s, layer)

            def filter_spectrum(l, s, o):
                T = STREAMS[s][1]
                nt, nf = T // P, FACTORS[s]
                tbase = 0 if s == "lat" else 8
                if (s, o) != cores_of(l)[0]:
                    act.wait_ge(*c.after("conv_free", *prev_conv(l, s, o)))
                load("skip", SKIP[0:1], d["skip"][l, o:o + 1], l, s, o)
                for r in range(2):
                    if r:
                        act.wait_ge(*c.after("window_last", l, s, o, 0))
                    elif (s, o) != cores_of(l)[0]:
                        act.wait_ge(*c.after("window_last", *prev_conv(l, s, o), 1))
                    load("delta", DEL, d["delta"][2 * o + r:2 * o + r + 1].to_broadcast([P, BW]), l, s, o, r)
                    act.wait_ge(*c.after("load_delta", l, s, o, r))
                    for m in range(nt):
                        n = r * nt + m
                        if n >= 2:
                            act.wait_ge(*c.after("taps_windowed", l, s, o, n - 2))
                        act.activation(TT[:, n % 2], DEL, ACT.Exp, scale=TCOL[:, tbase + n:tbase + n + 1]).then_inc(
                            *c.done("window", l, s, o, n, also=[("window_last", l, s, o, r)] if m == nt - 1 else []))
                        act.wait_ge(*c.after("taps_windowed", l, s, o, n))
                        if m:
                            act.wait_ge(*c.after("tap_sum", l, s, o, r, m - 1))
                        elif r:
                            act.wait_ge(*c.after("tap_sum", l, s, o, 0))
                        act.activation(TT[:, 2], FW[:, n], ACT.Abs).then_inc(*c.done("magnitude", l, s, o, n))
                        fill(l, "taps", s, o, n)
                    act.wait_ge(*c.after("tap_sum", l, s, o, r))
                    link(act.activation(RN[:, r], ps.of("tap_sum", l, s, o, r), ACT.Ln, scale=float(2 * T)))
                    act.activation(RN[:, r], RN[:, r], ACT.Exp, scale=-1.0).then_inc(
                        *c.done("tap_norm", l, s, o, r, also=[("freed", "tap_sum", l, s, o, r)]))
                    fill(l, "sum", s, o, r)
                fill(l, "parts", s, o)
                act.wait_ge(*c.after("load_cols", l))
                for f in range(nf):
                    for p in range(2):
                        act.wait_ge(*c.after("fdft", l, s, o, f, p))
                        src = ps.of("fdft", l, s, o, f, p)
                        if f == 0 and p == 1:
                            link(act.activation(FH[:, 1], src, ACT.Copy, scale=NOT0))
                            act.activation(FH[0:1, 8], src[0:1], ACT.Copy).then_inc(
                                *c.done("filter_spec", l, s, o, f, p, also=[("freed", "fdft", l, s, o, f, p)]))
                            continue
                        if f == 0:
                            link(act.activation(FH[:, 8], src, ACT.Copy))
                        act.activation(FH[:, 2 * f + p], src, ACT.Copy).then_inc(
                            *c.done("filter_spec", l, s, o, f, p, also=[("freed", "fdft", l, s, o, f, p)]))

            def hyena(l):
                begin(l)
                if l:
                    act.wait_ge(*c.after("x_new", l - 1, "all"))
                    act.dma_start(d["x_mid"], X).then_inc(*c.done("store_x", l, by=16))
                    act.wait_ge(*c.after("load_cols", l))
                    norm(l, ["lat", "ctx"])
                    act.wait_ge(*c.after("store_x", l))
                else:
                    act.wait_ge(*c.after("load_x", 0))
                    act.wait_ge(*c.after("load_cols", l))
                    norm(l, ["lat", "ctx"])
                load("hy", FM, d["FM"], l, "all")
                load("G", G, d["G"], l)
                for s in ("lat", "ctx"):
                    off, T = STREAMS[s]
                    for k in range(KD):
                        h = H[:, k, off:off + T]
                        act.wait_ge(*c.after("h_scaled", l, s, k))
                        act.activation(h, h, ACT.Identity, bias=ADAS[:, l, k, int(s == "ctx"):int(s == "ctx") + 1]).then_inc(
                            *c.done("h", l, s, k, also=[("h", l, "all")] if (s, k) == ("ctx", KD - 1) else []))
                filter_nets(l)
                for s, o in cores_of(l):
                    filter_spectrum(l, s, o)
                    fill(l, "spec", s, o)

            def conv_centre(l, j):
                for s in streams_for(l, ("u", j)):
                    off, T = STREAMS[s]
                    act.wait_ge(*c.after("u", l, j, s))
                    if 4 <= j < 8:
                        act.wait_ge(*c.after("uT", l, 0, s, T // P - 1))
                    dst = UD[:, j % 4, off:off + T] if j < 8 else YBT[:, j, off:off + T]
                    act.activation(dst, ps.of("u", l, j, s)[:, 0:T], ACT.Identity, bias=CONVB[:, j:j + 1],
                                   scale=CONVW[:, 12 + j:13 + j]).then_inc(*c.done("centre", l, j, s))

            def gla(l):
                barrier(act, "gla", l)
                load("gla", WA[0:33], d["wa"][l], l)
                for kind, j in GLA_TILES:
                    if kind in ("gq", "gk", "gz"):
                        dst = {"gq": GQ, "gk": GK, "gz": YBT}[kind]
                        for s in streams_for(l, (kind, j)):
                            off, T = STREAMS[s]
                            act.wait_ge(*c.after(kind, l, j, s))
                            act.activation(dst[:, j, off:off + T], ps.of(kind, l, j, s)[:, 0:T],
                                           ACT.Silu if kind == "gz" else ACT.Copy,
                                           scale=0.125 if kind == "gq" else 1.0).then_inc(
                                *c.done(kind + "_kept", l, j, s, also=[("freed", kind, l, j, s)] +
                                        ([("qk_ready", l, s)] if (kind, j) == ("gq", 1) else [])))
                for s in ("ctx", "lat"):
                    T = STREAMS[s][1]
                    nt = T // P
                    full = s in streams_of(l)
                    if s == "lat":
                        act.wait_ge(*c.after("o" if "ctx" in streams_of(l) else "cum", l, "ctx", *((3,) if "ctx" in streams_of(l) else (1, 1))))
                    for t in range(nt):
                        act.wait_ge(*c.after("gpre", l, s, t))
                        act.activation(GG[:, t], ps.of("gpre", l, s, t), ACT.Abs).then_inc(*c.done("gate_abs", l, s, t))
                    for t in range(nt):
                        act.wait_ge(*c.after("gate_abs", l, s, t))
                        act.activation(GG[:, t], GG[:, t], ACT.Exp, scale=-1.0).then_inc(*c.done("gate_exp", l, s, t))
                    for t in range(nt):
                        act.wait_ge(*c.after("gate_exp", l, s, t))
                        act.activation(GG[:, t], GG[:, t], ACT.Ln, bias=1.0).then_inc(*c.done("softplus", l, s, t))
                    if s == "lat" and streams_of(l)[0] == "ctx":
                        act.wait_ge(*c.after("k_tokens", l, "ctx", 1, 1))
                    for r in range(2):
                        for p in range(2):
                            act.wait_ge(*c.after("cum", l, s, r, p))
                            act.activation(B[:, r, p, 0:T], ps.of("cum", l, s, r, p)[:, 0:T], ACT.Copy).then_inc(
                                *c.done("cum_kept", l, s, r, p, also=[("freed", "cum", l, s, r, p)]))
                    act.wait_ge(*c.after("cum_kept", l, s, 1, 1))
                    if s == "lat" and "ctx" in streams_of(l):
                        act.wait_ge(*c.after("oms", l, "ctx", 3))
                    for r in range(2):
                        act.activation(QH[:, r, :, 0:T], B[:, r, :, 0:T], ACT.Exp).then_inc(*c.done("q_decay", l, s, r))
                    act.wait_ge(*c.after("k_offsets", l, s))
                    for r in range(2):
                        act.activation(KH[:, r, :, 0:T], KH[:, r, :, 0:T], ACT.Exp).then_inc(*c.done("k_decay", l, s, r))
                    for r in range(2):
                        for p in range(2):
                            act.wait_ge(*c.after("kT", l, s, r, p))
                            if s == "lat":
                                act.wait_ge(*c.after("kv", l, "ctx", 1, 1))
                            act.activation(KT[:, r, p, 0:T], ps.of("kT", l, s, r, p)[:, 0:T], ACT.Copy).then_inc(
                                *c.done("k_tokens", l, s, r, p, also=[("freed", "kT", l, s, r, p)]))
                    if not full:
                        continue
                    for v in range(len(LEVELS)):
                        fill(l, "level", s, v)
                        act.wait_ge(*c.after("level_args", l, s, v))
                        act.activation(EL[:, v % 2, :, 0:2 * T], EL[:, v % 2, :, 0:2 * T], ACT.Exp).then_inc(*c.done("level_exp", l, s, v))
                    act.wait_ge(*c.after("kT", l, s, 1, 1))
                    if s == "lat" and "ctx" in streams_of(l):
                        act.wait_ge(*c.after("gla_y", l, "ctx", 3))
                    for h in range(4):
                        act.wait_ge(*c.after("o", l, s, h))
                        act.activation(OS[:, h, 0:T], ps.of("o", l, s, h)[:, 0:T], ACT.Copy).then_inc(*c.done("o_kept", l, s, h))
                        act.activation(OS[:, 4 + h, 0:T], ps.of("o", l, s, h)[:, 0:T], ACT.Square).then_inc(
                            *c.done("o_sq", l, s, h, also=[("freed", "o", l, s, h)]))
                    for h in range(4):
                        act.wait_ge(*c.after("oms", l, s, h))
                        act.activation(OS[:, 4 + h, 0:T], ps.of("oms", l, s, h)[:, 0:T], ACT.Ln, bias=EPSC).then_inc(
                            *c.done("o_log", l, s, h, also=[("freed", "oms", l, s, h)]))
                    for h in range(4):
                        act.wait_ge(*c.after("o_log", l, s, h))
                        act.activation(OS[:, 4 + h, 0:T], OS[:, 4 + h, 0:T], ACT.Exp, scale=-0.5).then_inc(*c.done("o_rms", l, s, h))

            def attn(l):
                barrier(act, "attn", l)
                load("attn", GAIN, d["gain"][l:l + 1].to_broadcast([P, 640]), l, 0)
                load("attn", ROPE, d["rope"], l, "all")
                for s in ("lat", "ctx"):
                    nh = (STREAMS[s][1] // P) * 10
                    act.wait_ge(*c.after("head_ms", l, s))
                    link(act.activation(MSQ[:, 0:nh], MSQ[:, 0:nh], ACT.Ln, scale=1.0 / 64, bias=EPSC))
                    act.activation(MSQ[:, 0:nh], MSQ[:, 0:nh], ACT.Exp, scale=-0.5).then_inc(*c.done("head_rms", l, s))
                fill(l, "prefix")
                for s in ("lat", "ctx"):
                    off, T = STREAMS[s]
                    for j in ([4] if s not in streams_of(l) else [4, 0, 1, 2, 3]):
                        act.wait_ge(*c.after("qkT", l, s, j))
                        for b in range(2):
                            src = ps.of("qkT", l, s, j)[64 * b:64 * b + 64, 0:T]
                            for at, head in [(b, 2 * j + b)] if j < 4 else [(0, 8 + 2 * b), (1, 8 + 2 * b)]:
                                act.activation(QKS[64 * at:64 * at + 64, head, off:off + T], src, ACT.Copy).then_inc(
                                    *c.done("qk_high", l, s, j, b))
                act.wait_ge(*c.after("qk_normed", l, "ctx"))
                for s in ("lat", "ctx"):
                    act.wait_ge(*c.after("proj_kept", l, "av", 0, s))
                for b in range(2):
                    v = VA[:, :, 64 * b:64 * b + 64].unsqueeze(2).to_broadcast([P, 6, 2, 64])
                    high = VS[:, 0].rearrange("p (a b e n) -> p a b e n", a=6, b=2, e=2)[:, :, b]
                    act.activation(high, v, ACT.Copy).then_inc(*c.done("v_high", l, b))
                steps = attn_steps(l)

                def keep(i):
                    s, t, hh = steps[i]
                    N = 768 if s == "lat" else 256
                    act.wait_ge(*c.after("probT", l, s, t, hh))
                    if i >= 2:
                        act.wait_ge(*c.after("ao", l, *steps[i - 2]))
                    act.activation(PTS[:, 2 * (i % 2), 0:N], ps.of("probT", l, s, t, hh)[:, 0:N], ACT.Copy).then_inc(
                        *c.done("probT_high", l, s, t, hh))

                def exponentials(i):
                    s, t, hh = steps[i]
                    N = 768 if s == "lat" else 256
                    col = 8 * (t + (4 if s == "ctx" else 0)) + hh
                    act.wait_ge(*c.after("row_max", l, s, t, hh))
                    if i >= 2:
                        act.wait_ge(*c.after("probT", l, *steps[i - 2]))
                    act.activation(PR[:, i % 2, 0:N], ps.of("score", l, s, t, hh)[:, 0:N], ACT.Exp, bias=NMAX[:, col:col + 1],
                                   accum_out=SUMS[:, col:col + 1]).then_inc(
                        *c.done("prob", l, s, t, hh, also=[("freed", "score", l, s, t, hh)]))

                exponentials(0)
                exponentials(1)
                for i in range(len(steps)):
                    keep(i)
                    if i + 2 < len(steps):
                        exponentials(i + 2)

            def merge(l):
                barrier(act, "merge", l)
                load("x", X, d["xT"] if l == 0 else d["x_mid"], "merge", l)

                def weight_high(i):
                    n = SPLIT[l, i]
                    act.wait_ge(*c.after(f"load_slot{n % NSLOT}", n))
                    if i >= 2:
                        act.wait_ge(*c.after("split_used", l, i - 2))
                    act.activation(WS[:, 2 * (i % 2)], RING[:, n % NSLOT].rearrange("p a b -> p (a b)"), ACT.Copy).then_inc(
                        *c.done("weight_high", l, i))

                weight_high(0)
                weight_high(1)
                for j in range(KD):
                    for b in range(3):
                        if 3 * j + b > RAW - 1:
                            weight_high(3 * j + b - RAW + 2)
                        for s in streams_for(l, ("m", 0)):
                            off, T = STREAMS[s]
                            act.wait_ge(*c.after("m", l, 3 * j + b, s))
                            if j >= 2:
                                act.wait_ge(*c.after("gated", l, j - 2, b, s))
                            act.activation(MG[:, j % 2, b, off:off + T], ps.of("m", l, 3 * j + b, s)[:, 0:T], ACT.Sigmoid).then_inc(
                                *c.done("gate", l, j, b, s, also=[("freed", "m", l, 3 * j + b, s)]))
                ss = streams_for(l, ("m", 0))
                cols = sum(STREAMS[s][1] for s in ss)
                for k in range(KD):
                    act.wait_ge(*c.after("merge_add", l, k, 2, ss[-1]))
                    act.activation(HS[:, k, 0:cols], YM[:, k, 0:cols], ACT.Copy).then_inc(*c.done("merged_high", l, k))
                for i in range(3 * KD - RAW + 2, NSPLIT):
                    weight_high(i)

            start()
            for l in range(DEPTH):
                hyena(l)
                c.phase_end(("hyena", l))
                gla(l)
                c.phase_end(("gla", l))
                attn(l)
                c.phase_end(("attn", l))
                merge(l)
                c.phase_end(("merge", l))
            norm(DEPTH, ["lat"])
            c.phase_end(("norm", DEPTH))

        @block.vector
        def _(dve):
            c.engine = "dve"
            chain = [0]

            def link(ins):
                ins.then_inc(*c.done("dve_chain", chain[0]))
                dve.wait_ge(*c.after("dve_chain", chain[0]))
                chain[0] += 1

            def norm(l, ss):
                if l < DEPTH:
                    ADA = ADAS[:, l]
                    dve.wait_ge(*c.after("adaln", l, 2 * KD - 1))
                else:
                    barrier(dve, "norm", l)
                for s in ss:
                    off, T = STREAMS[s]
                    e = 0 if s == "lat" else 1
                    dve.wait_ge(*c.after("rms", l, s))
                    for k in range(KD):
                        x, rs = X[:, k, off:off + T], RS[:, off:off + T]
                        if l == DEPTH:
                            dve.scalar_tensor_tensor(OUTB[:, k], x, FINALN[:, k:k + 1], rs, ALU.mult, ALU.mult).then_inc(
                                *c.done("final", k))
                        else:
                            h = H[:, k, off:off + T]
                            dve.scalar_tensor_tensor(h, x, ADA[:, 8 + k, e:e + 1], rs, ALU.mult, ALU.mult).then_inc(
                                *c.done("h_scaled", l, s, k))

            def conv_sides(l, j):
                for s in streams_for(l, ("u", j)):
                    off, T = STREAMS[s]
                    dst = UD[:, j % 4, off:off + T] if j < 8 else YBT[:, j, off:off + T]
                    u = ps.of("u", l, j, s)
                    dve.wait_ge(*c.after("centre", l, j, s))
                    link(dve.scalar_tensor_tensor(dst[:, 1:T], u[:, 0:T - 1], CONVW[:, j:j + 1], dst[:, 1:T], ALU.mult, ALU.add))
                    dve.scalar_tensor_tensor(dst[:, 0:T - 1], u[:, 1:T], CONVW[:, 24 + j:25 + j], dst[:, 0:T - 1], ALU.mult, ALU.add)\
                       .then_inc(*c.done("short_conv", l, j, s, also=[("freed", "u", l, j, s)]))

            def fill(l, *point):
                for kind, *j in FILL[l].get(point, []):
                    if kind == "u":
                        conv_sides(l, *j)
                    elif kind == "ada":
                        ada_tile(*j)
                    elif kind == "ada_rows":
                        dve.wait_ge(*c.after("ada_rows", *j, 3))
                        dve.tensor_copy(ROWS[0:2, j[0]], ps.of("ada_rows", *j)[0:2]).then_inc(
                            *c.done("rows_kept", *j, also=[("freed", "ada_rows", *j)]))
                    elif kind == "ada_turn":
                        ada_turned(*j)

            def ada_turned(g):
                if g == 0:
                    dve.wait_ge(*c.after("load_const", "all"))
                dve.wait_ge(*c.after("ada_turned", g))
                for jj in range(4):
                    j = 4 * g + jj
                    dve.tensor_scalar(ADAS[:, 0, j], ps.of("ada_turned", g)[:, 2 * jj:2 * jj + 2], BADA[:, 0, j:j + 1],
                                      1.0 if 8 <= j < 16 else 0.0, ALU.add, ALU.add).then_inc(
                        *c.done("adaln", 0, j, also=[("freed", "ada_turned", g)] if jj == 3 else []))

            def ada_tile(l, j):
                dve.wait_ge(*c.after("ada", l, j))
                dve.tensor_scalar(ADAS[:, l, j], ps.of("ada", l, j)[:, 0:2], BADA[:, l, j:j + 1], 1.0 if 8 <= j < 16 else 0.0,
                                  ALU.add, ALU.add).then_inc(*c.done("adaln", l, j, also=[("freed", "ada", l, j)]))

            def filter_nets(l):
                if l == 0:
                    dve.wait_ge(*c.after("load_mask"))
                    dve.tensor_copy(MASK[:, :, :], MASK32).then_inc(*c.done("mask_kept"))
                    dve.wait_ge(*c.after("mask_kept"))
                barrier(dve, "hyena", l)
                dve.wait_ge(*c.after("load_hy", l, "all"))
                for s in streams_of(l):
                    T2 = 2 * STREAMS[s][1]
                    for layer in range(2):
                        if (s, layer) != (streams_of(l)[0], 0):
                            dve.wait_ge(*c.after("sine", l, *((s, 0) if layer else (streams_of(l)[0], 1))))
                        for h in range(T2 // BW):
                            dve.wait_ge(*c.after("ffn", l, s, layer, h))
                            dve.tensor_scalar(HX[0:64, 0, h * BW:(h + 1) * BW], ps.of("ffn", l, s, layer, h)[0:64],
                                              C64[0:64, 2 * layer:2 * layer + 1], C64[0:64, 2 * layer + 1:2 * layer + 2],
                                              ALU.add, ALU.mult).then_inc(
                                *c.done("phase", l, s, layer, h, also=[("freed", "ffn", l, s, layer, h)]))
                        dve.wait_ge(*c.after("phase", l, s, layer, T2 // BW - 1))
                        x, k, r = (HX[0:64, i, 0:T2] for i in range(3))
                        link(dve.tensor_scalar(k, x, 1.0 / (2 * math.pi), ROUND_MAGIC, ALU.mult, ALU.add))
                        link(dve.tensor_scalar(k, k, ROUND_MAGIC, None, ALU.subtract))
                        link(dve.scalar_tensor_tensor(r, k, -TWO_PI_1, x, ALU.mult, ALU.add))
                        link(dve.scalar_tensor_tensor(r, k, -TWO_PI_2, r, ALU.mult, ALU.add))
                        link(dve.scalar_tensor_tensor(r, k, -TWO_PI_3, r, ALU.mult, ALU.add))
                        dve.tensor_scalar(r, r, -PI_BELOW, PI_BELOW, ALU.max, ALU.min).then_inc(*c.done("reduced", l, s, layer))
                        fill(l, "mlp", s, layer)

            def filter_spectrum(l, s, o):
                T = STREAMS[s][1]
                nt, nf = T // P, FACTORS[s]
                if (s, o) != cores_of(l)[0]:
                    dve.wait_ge(*c.after("conv_free", *prev_conv(l, s, o)))
                    dve.wait_ge(*c.after("gated_conv", *prev_conv(l, s, o), 0))
                else:
                    dve.wait_ge(*c.after("sine", l, streams_of(l)[-1], 1))
                for r in range(2):
                    for m in range(nt):
                        n = r * nt + m
                        dve.wait_ge(*c.after("taps", l, s, o, n))
                        dve.wait_ge(*c.after("window", l, s, o, n))
                        dve.scalar_tensor_tensor(FW[:, n], TT[:, n % 2], 0.05, ps.of("taps", l, s, o, n), ALU.add, ALU.mult)\
                           .then_inc(*c.done("taps_windowed", l, s, o, n, also=[("freed", "taps", l, s, o, n)]))
                        fill(l, "taps", s, o, n)
                    dve.wait_ge(*c.after("tap_norm", l, s, o, r))
                    for m in range(nt):
                        n = r * nt + m
                        ins = dve.tensor_tensor(FW[:, n], FW[:, n], RN[:, r], ALU.mult)
                        ins.then_inc(*c.done("taps_normed", l, s, o, n))
                    dve.wait_ge(*c.after("taps_normed", l, s, o, (r + 1) * nt - 1))
                    fill(l, "sum", s, o, r)
                dve.wait_ge(*c.after("load_skip", l, s, o))
                link(dve.scalar_tensor_tensor(FW[0:1, 0], SKIP[0:1], 1.0 / (2 * T), FW[0:1, 0], ALU.mult, ALU.add))
                link(dve.memset(FW[0:1, nt], 0.0))
                if s == "ctx":
                    for m in range(2):
                        dve.tensor_tensor(R[:, m], FW[:, m], FW[:, m + 2], ALU.add).then_inc(*c.done("parts", l, s, o, m))
                        last = dve.tensor_tensor(R[:, 2 + m], FW[:, m], FW[:, m + 2], ALU.subtract)
                        last.then_inc(*c.done("parts", l, s, o, 2 + m, also=[("filter_parts", l, s, o)] if m == 1 else []))
                else:
                    for m in range(4):
                        dve.tensor_tensor(R[:, 4 + m], FW[:, m], FW[:, m + 4], ALU.subtract).then_inc(*c.done("parts", l, s, o, m))
                        link(dve.tensor_tensor(FW[:, m], FW[:, m], FW[:, m + 4], ALU.add))
                    for m in range(2):
                        dve.tensor_tensor(R[:, m], FW[:, m], FW[:, m + 2], ALU.add).then_inc(*c.done("parts", l, s, o, 4 + m))
                        dve.tensor_tensor(R[:, 2 + m], FW[:, m], FW[:, m + 2], ALU.subtract).then_inc(*c.done("parts", l, s, o, 6 + m))
                    link(dve.tensor_tensor(FW[:, 4], R[:, 4], R[:, 6], ALU.subtract))
                    link(dve.tensor_tensor(FW[:, 5], R[:, 5], R[:, 7], ALU.add))
                    link(dve.scalar_tensor_tensor(FW[:, 6], R[:, 7], -ROOT2, FW[:, 4], ALU.mult, ALU.add))
                    link(dve.scalar_tensor_tensor(FW[:, 7], R[:, 6], ROOT2, FW[:, 5], ALU.mult, ALU.add))
                    link(dve.scalar_tensor_tensor(R[:, 4], R[:, 7], ROOT2, FW[:, 4], ALU.mult, ALU.add))
                    dve.scalar_tensor_tensor(R[:, 5], R[:, 6], -ROOT2, FW[:, 5], ALU.mult, ALU.add).then_inc(
                        *c.done("parts", l, s, o, 8, also=[("filter_parts", l, s, o)]))
                fill(l, "parts", s, o)

            def convolve(l, s, o):
                T = STREAMS[s][1]
                nt, nf = T // P, FACTORS[s]
                ot = STREAMS[s][0] // P
                if o:
                    dve.wait_ge(*c.after("gated_conv", l, s, 0, nt - 1))
                dve.wait_ge(*c.after("fdft", l, s, o, nf - 1, 1))
                if o == 0:
                    dve.wait_ge(*c.after("u_tokens", l, 0, s, nt - 1))
                    dve.wait_ge(*c.after("u_tokens", l, 1, s, nt - 1))
                z = [TOKM[:, 0, ot + t] for t in range(nt)]
                if s == "ctx":
                    dve.tensor_copy(TT[:, 3, 0:1], z[0][:, 0:1]).then_inc(*c.done("signal_parts", l, s, o))
                else:
                    link(dve.tensor_tensor(R[:, 2], z[0], z[2], ALU.subtract))
                    link(dve.tensor_tensor(R[:, 1], z[1], z[3], ALU.add))
                    dve.tensor_tensor(R[:, 0], z[0], z[2], ALU.add).then_inc(*c.done("sig", l, s, o, 0))
                    dve.tensor_tensor(R[:, 3], z[1], z[3], ALU.subtract).then_inc(*c.done("sig", l, s, o, 1))
                    dve.scalar_tensor_tensor(R[:, 4], z[3], -ROOT2, R[:, 2], ALU.mult, ALU.add).then_inc(*c.done("sig", l, s, o, 2))
                    dve.scalar_tensor_tensor(R[:, 5], z[2], ROOT2, R[:, 1], ALU.mult, ALU.add).then_inc(*c.done("sig", l, s, o, 3))
                    dve.scalar_tensor_tensor(R[:, 6], z[3], ROOT2, R[:, 2], ALU.mult, ALU.add).then_inc(*c.done("sig", l, s, o, 4))
                    dve.scalar_tensor_tensor(R[:, 7], z[2], -ROOT2, R[:, 1], ALU.mult, ALU.add).then_inc(*c.done("signal_parts", l, s, o))
                for f in range(nf):
                    for p in range(2):
                        dve.wait_ge(*c.after("zdft", l, s, o, f, p))
                        dve.wait_ge(*c.after("filter_spec", l, s, o, f, p))
                    re, im = ps.of("zdft", l, s, o, f, 0), ps.of("zdft", l, s, o, f, 1)
                    if f:
                        dve.wait_ge(*c.after("spec", l, s, o, f - 1, 1))
                    dve.tensor_tensor(Y[:, 2 * f], re, FH[:, 2 * f], ALU.mult).then_inc(*c.done("prod", l, s, o, f, 0))
                    dve.tensor_tensor(Y[:, 2 * f + 1], re, FH[:, 2 * f + 1], ALU.mult).then_inc(
                        *c.done("prod", l, s, o, f, 1, also=[("freed", "zdft", l, s, o, f, 0)]))
                    dve.tensor_tensor(TT[:, 0], im, FH[:, 2 * f + 1], ALU.mult).then_inc(*c.done("prod", l, s, o, f, 2))
                    dve.tensor_tensor(TT[:, 1], im, FH[:, 8 if f == 0 else 2 * f], ALU.mult).then_inc(
                        *c.done("prod", l, s, o, f, 3, also=[("freed", "zdft", l, s, o, f, 1)]))
                fill(l, "spec", s, o)
                for m in range(nt if o == 0 else 4):
                    dve.wait_ge(*c.after("conv", l, s, o, m))
                    src = ps.of("conv", l, s, o, m)
                    also = [("freed", "conv", l, s, o, m)] + ([("conv_free", l, s, o)] if m == (nt if o == 0 else 4) - 1 else [])
                    if o == 0:
                        dve.tensor_tensor(TOKM[:, 0, ot + m], src, TOKM[:, 1, ot + m], ALU.mult).then_inc(
                            *c.done("gated_conv", l, s, o, m, also=also))
                    else:
                        off = STREAMS[s][0]
                        dve.wait_ge(*c.after("z_used", l, m, s))
                        dve.tensor_tensor(YBT[:, 8 + m, off:off + T], src[:, 0:T], YBT[:, 8 + m, off:off + T], ALU.mult).then_inc(
                            *c.done("gated_conv", l, s, o, m, also=also))

            def hyena(l):
                fill(l, "normed")
                norm(l, ["lat", "ctx"])
                filter_nets(l)
                for s, o in cores_of(l):
                    filter_spectrum(l, s, o)
                    convolve(l, s, o)

            def gla(l):
                barrier(dve, "gla", l)
                dve.memset(GA[32:33, :], 1.0).then_inc(*c.done("rank_one", l))
                link(dve.memset(ST[:, :, :, 0:P], 0.0))
                for s in ("lat", "ctx"):
                    off, T = STREAMS[s]
                    dve.wait_ge(*c.after("ga", l, 0, s))
                    dve.tensor_copy(GA[0:32, off:off + T], ps.of("ga", l, 0, s)[0:32, 0:T]).then_inc(
                        *c.done("rank", l, s, also=[("freed", "ga", l, 0, s)]))
                for j in range(4):
                    for s in ("lat", "ctx"):
                        off, T = STREAMS[s]
                        dve.wait_ge(*c.after("gv", l, j, s))
                        dve.tensor_copy(GV[:, off // P:(off + T) // P, j * P:(j + 1) * P],
                                        ps.of("gv", l, j, s)[:, 0:T].rearrange("p (t n) -> p t n", n=P)).then_inc(
                            *c.done("gv_kept", l, j, s, also=[("freed", "gv", l, j, s)]))
                for s in ("ctx", "lat"):
                    off, T = STREAMS[s]
                    nt = T // P
                    full = s in streams_of(l)
                    if s == "lat" and "ctx" in streams_of(l):
                        dve.wait_ge(*c.after("o", l, "ctx", 3))
                    elif s == "lat":
                        dve.wait_ge(*c.after("cum", l, "ctx", 1, 1))
                    for t in range(nt):
                        dve.wait_ge(*c.after("softplus", l, s, t))
                        dve.scalar_tensor_tensor(GG[:, t], ps.of("gpre", l, s, t), 0.0, GG[:, t], ALU.min, ALU.subtract).then_inc(
                            *c.done("log_decay", l, s, t, also=[("freed", "gpre", l, s, t)]))
                    for r in range(2):
                        for p in range(2):
                            dve.wait_ge(*c.after("cum_kept", l, s, r, p))

                    def split(ap, width):
                        return ap.rearrange("p (n w) -> p n w", w=width)

                    if s == "lat":
                        dve.wait_ge(*c.after("kT", l, "ctx", 1, 1))
                        if "ctx" in streams_of(l):
                            dve.wait_ge(*c.after("gla_y", l, "ctx", 3))
                    for r in range(2):
                        for p in range(2):
                            b = split(B[:, r, p, 0:T], P)
                            ref = b[:, :, P - 1:P] if r == 0 else b[:, :, 0:1]
                            dve.tensor_tensor(split(KH[:, r, p, 0:T], P), ref.to_broadcast([P, nt, P]), b, ALU.subtract).then_inc(
                                *c.done("k_offset", l, s, r, p, also=[("k_offsets", l, s)] if (r, p) == (1, 1) else []))
                    for r in range(2):
                        dve.wait_ge(*c.after("q_decay", l, s, r))
                        q = QH[:, r, :, 0:T].rearrange("p a (n w) -> p a n w", w=P)
                        dve.tensor_copy(DEC[:, r, :, 0:nt], q[:, :, :, P - 1 if r == 0 else 0]).then_inc(*c.done("decay_cols", l, s, r))
                    dve.wait_ge(*c.after("decay_cols", l, s, 1))
                    for r in range(2):
                        if full:
                            dve.tensor_tensor(QH[:, r, :, 0:T], QH[:, r, :, 0:T], GQ[:, :, off:off + T], ALU.mult).then_inc(
                                *c.done("q_decayed", l, s, r))
                    for j in range(2):
                        dve.wait_ge(*c.after("gk_kept", l, j, s))
                    for r in range(2):
                        dve.wait_ge(*c.after("k_decay", l, s, r))
                        dve.tensor_tensor(KH[:, r, :, 0:T], KH[:, r, :, 0:T], GK[:, :, off:off + T], ALU.mult).then_inc(
                            *c.done("k_dec", l, s, r, also=[("k_decayed", l, s)] if r == 1 else []))

                    def level_args(v):
                        w = LEVELS[v]
                        if v >= 2:
                            dve.wait_ge(*c.after("pairs", l, s, v - 2, nt - 1))
                        for p in range(2):
                            bf, bb = (B[:, r, p, 0:T].rearrange("p (n u w) -> p n u w", u=2, w=w) for r in range(2))
                            eq = EL[:, v % 2, p, 0:T].rearrange("p (n u w) -> p n u w", u=2, w=w)
                            ek = EL[:, v % 2, p, T:2 * T].rearrange("p (n u w) -> p n u w", u=2, w=w)
                            n = T // (2 * w)
                            rf = bf[:, :, 0, w - 1:w].to_broadcast([P, n, w])
                            rb = bb[:, :, 1, 0:1].to_broadcast([P, n, w])
                            for i, (dst, a, b) in enumerate([(eq[:, :, 0], bb[:, :, 0], rb), (eq[:, :, 1], bf[:, :, 1], rf),
                                                             (ek[:, :, 0], rf, bf[:, :, 0]), (ek[:, :, 1], rb, bb[:, :, 1])]):
                                dve.tensor_tensor(dst, a, b, ALU.subtract).then_inc(
                                    *c.done("level_arg", l, s, v, p, i, also=[("level_args", l, s, v)] if (p, i) == (1, 3) else []))

                    def select(v):
                        for t in range(nt):
                            dve.wait_ge(*c.after("pairs", l, s, v, t))
                            if v < 0:
                                a = ATT[:, t].rearrange("p (h n) -> p h n", h=4)
                                src = ps.of("pairs", l, s, v, t).rearrange("p (h n) -> p h n", h=4)
                                dve.tensor_tensor(a, src, DIAG2[:, :].unsqueeze(1).to_broadcast([P, 4, P]), ALU.mult).then_inc(
                                    *c.done("select", l, s, v, t, also=[("freed", "pairs", l, s, v, t)]))
                            else:
                                dve.wait_ge(*c.after("mask_kept"))
                                dve.wait_ge(*c.after("select", l, s, v - 1, t))
                                a = ATT[:, t].rearrange("p (h n) -> p h n", h=4)
                                src = ps.of("pairs", l, s, v, t).rearrange("p (h n) -> p h n", h=4)
                                dve.copy_predicated(a, MASK[:, v, :].unsqueeze(1).to_broadcast([P, 4, P]), src).then_inc(
                                    *c.done("select", l, s, v, t, also=[("freed", "pairs", l, s, v, t)] +
                                            ([("pairs_all", l, s)] if (v, t) == (len(LEVELS) - 1, nt - 1) else [])))

                    def states():
                        base = 0 if s == "ctx" else 2
                        for r in range(2):
                            for i in range(nt if s == "ctx" else nt - 1):
                                t = i if r == 0 else nt - 1 - i
                                dve.wait_ge(*c.after("kv", l, s, r, i))
                                if i:
                                    dve.wait_ge(*c.after("state", l, s, r, i - 1, 1))
                                for p in range(2):
                                    dve.scalar_tensor_tensor(ST[:, r, p, (base + i + 1) * P:(base + i + 2) * P],
                                                             ST[:, r, p, (base + i) * P:(base + i + 1) * P], DEC[:, r, p, t:t + 1],
                                                             ps.of("kv", l, s, r, i)[:, p * P:(p + 1) * P], ALU.mult, ALU.add).then_inc(
                                        *c.done("state", l, s, r, i, p, also=[("freed", "kv", l, s, r, i)] if p else []))

                    if not full:
                        states()
                        continue
                    level_args(0)
                    select(-1)
                    states()
                    for v in range(len(LEVELS)):
                        dve.wait_ge(*c.after("level_exp", l, s, v))
                        dve.tensor_tensor(EL[:, v % 2, :, 0:T], EL[:, v % 2, :, 0:T], GQ[:, :, off:off + T], ALU.mult).then_inc(
                            *c.done("level_q", l, s, v))
                        if v + 1 < len(LEVELS):
                            level_args(v + 1)
                        fill(l, "level", s, v)
                        select(v)
                    for h in range(4):
                        dve.wait_ge(*c.after("o_rms", l, s, h))
                        o = OS[:, h, 0:T]
                        link(dve.scalar_tensor_tensor(o, o, GNORM, OS[:, 4 + h, 0:T], ALU.mult, ALU.mult))
                        y = YBT[:, h, off:off + T]
                        dve.tensor_tensor(y, y, o, ALU.mult).then_inc(*c.done("gla_y", l, s, h))

            def attn(l):
                barrier(dve, "attn", l)
                dve.wait_ge(*c.after("load_attn", l, "all"))
                link(dve.tensor_scalar(GAIN[:, 0:512], GAIN[:, 0:512], 0.125, None, ALU.mult))
                for s in ("lat", "ctx"):
                    off, T = STREAMS[s]
                    nt = T // P
                    lo, nh = (0, 10) if s in streams_of(l) else (512, 2)
                    qk = QK[:, off // P:off // P + nt, lo:640]
                    w = 640 - lo
                    dve.wait_ge(*c.after("proj_kept", l, "aq", 3, "lat"))
                    flat = TA.rearrange("p a b -> p (a b)")
                    sq = flat[:, 0:nt * w].rearrange("p (t n) -> p t n", t=nt)
                    if s == "ctx":
                        dve.wait_ge(*c.after("qk_normed", l, "lat"))
                    link(dve.tensor_tensor(sq, qk, qk, ALU.mult))
                    dve.tensor_reduce(MSQ[:, 0:nt * nh], flat[:, 0:nt * w].rearrange("p (t n) -> p t n", n=64), AX.X, ALU.add).then_inc(
                        *c.done("head_ms", l, s))
                    dve.wait_ge(*c.after("head_rms", l, s))
                    for t in range(nt):
                        q = qk[:, t].rearrange("p (h n) -> p h n", n=64)
                        r = MSQ[:, t * nh:(t + 1) * nh].unsqueeze(2).to_broadcast([P, nh, 64])
                        dve.tensor_tensor(q, q, r, ALU.mult).then_inc(*c.done("head_scaled", l, s, t))
                    dve.wait_ge(*c.after("head_scaled", l, s, nt - 1))
                    last = dve.tensor_tensor(qk, qk, GAIN[:, lo:640].unsqueeze(1).to_broadcast([P, nt, w]), ALU.mult)
                    if s == "ctx":
                        last.then_inc(*c.done("qk_normed", l, s))
                        continue
                    link(last)
                    for t in range(nt):
                        q = qk[:, t].rearrange("p (h i e) -> p h i e", h=10, e=2)
                        a0, a1 = q[:, :, :, 0], q[:, :, :, 1]
                        cos, sin = (ROPE[:, i, t].unsqueeze(1).to_broadcast([P, 10, 32]) for i in range(2))
                        tmp = [TA[:, i, 320 * t:320 * (t + 1)].rearrange("p (h i) -> p h i", h=10) for i in range(4)]
                        for i, (a, b) in enumerate([(a0, cos), (a1, sin), (a0, sin), (a1, cos)]):
                            dve.tensor_tensor(tmp[i], a, b, ALU.mult).then_inc(*c.done("rotated", l, t, i))
                        dve.wait_ge(*c.after("rotated", l, t, 3))
                        dve.tensor_tensor(a0, tmp[0], tmp[1], ALU.subtract).then_inc(*c.done("rotated", l, t, 4))
                        dve.tensor_tensor(a1, tmp[2], tmp[3], ALU.add).then_inc(
                            *c.done("rotated", l, t, 5, also=[("qk_normed", l, s)] if t == nt - 1 else []))
                steps = attn_steps(l)

                def row_max(i):
                    s, t, hh = steps[i]
                    N = 768 if s == "lat" else 256
                    col = 8 * (t + (4 if s == "ctx" else 0)) + hh
                    dve.wait_ge(*c.after("score", l, s, t, hh))
                    dve.tensor_reduce(NMAX[:, col:col + 1], ps.of("score", l, s, t, hh)[:, 0:N], AX.X, ALU.max, negate=True).then_inc(
                        *c.done("row_max", l, s, t, hh))

                def finish(s, t, g):
                    off = STREAMS[s][0] + t * P
                    dve.wait_ge(*c.after("ao_group", l, s, t, g))
                    if t == 0 and g == 0:
                        dve.wait_ge(*c.after("az_kept", l, 3, s))
                    for b in range(2):
                        y = YBT[64 * b:64 * b + 64, 4 + 2 * g:6 + 2 * g, off:off + P]
                        out = ps.of("ao", l, s, t, g)[64 * b:64 * b + 64].rearrange("p (j b n) -> p j b n", j=2, b=2)[:, :, b]
                        dve.tensor_tensor(y, out, y, ALU.mult).then_inc(
                            *c.done("attn_y", l, s, t, g, b, also=[("freed", "ao", l, s, t, g)]))

                for s in ("lat", "ctx"):
                    off, T = STREAMS[s]
                    for j in ([4] if s not in streams_of(l) else [4, 0, 1, 2, 3]):
                        for b in range(2):
                            dve.wait_ge(*c.after("qk_high", l, s, j, b))
                            src = ps.of("qkT", l, s, j)[64 * b:64 * b + 64, 0:T]
                            for at, head in [(1 - b, 2 * j + b)] if j < 4 else [(0, 9 + 2 * b), (1, 9 + 2 * b)]:
                                high = QKS[64 * b:64 * b + 64, head - (j == 4), off:off + T]
                                dve.tensor_tensor(QKS[64 * at:64 * at + 64, head, off:off + T], src, high, ALU.subtract).then_inc(
                                    *c.done("qkT_kept", l, s, j, also=[("freed", "qkT", l, s, j)] if b else []))
                row_max(0)
                row_max(1)
                for b in range(2):
                    dve.wait_ge(*c.after("v_high", l, b))
                    v = VA[:, :, 64 * b:64 * b + 64].unsqueeze(2).to_broadcast([P, 6, 2, 64])
                    high, low = (VS[:, i].rearrange("p (a b e n) -> p a b e n", a=6, b=2, e=2)[:, :, b] for i in range(2))
                    dve.tensor_tensor(low, v, high, ALU.subtract).then_inc(*c.done("v_low", l, b, also=[("v_low", l)]))

                def scale(i):
                    s, t, hh = steps[i]
                    N = 768 if s == "lat" else 256
                    col = 8 * (t + (4 if s == "ctx" else 0)) + hh
                    dve.wait_ge(*c.after("prob", l, s, t, hh))
                    link(dve.reciprocal(RINV[:, col:col + 1], SUMS[:, col:col + 1]))
                    dve.tensor_scalar(PR[:, i % 2, 0:N], PR[:, i % 2, 0:N], RINV[:, col:col + 1], None, ALU.mult).then_inc(
                        *c.done("prob_scaled", l, s, t, hh))

                scale(0)
                for i in range(len(steps)):
                    s, t, hh = steps[i]
                    N = 768 if s == "lat" else 256
                    if i + 1 < len(steps):
                        scale(i + 1)
                    dve.wait_ge(*c.after("probT_high", l, s, t, hh))
                    dve.tensor_tensor(PTS[:, 2 * (i % 2) + 1, 0:N], ps.of("probT", l, s, t, hh)[:, 0:N],
                                      PTS[:, 2 * (i % 2), 0:N], ALU.subtract).then_inc(
                        *c.done("probT_kept", l, s, t, hh, also=[("freed", "probT", l, s, t, hh)]))
                    if i + 2 < len(steps):
                        row_max(i + 2)
                    if hh % 4 == 1 and i > 4:
                        s0, t0, h0 = steps[i - 2]
                        finish(s0, t0, h0 // 4)
                finish(*steps[-1][:2], 1)

            def merge(l):
                barrier(dve, "merge", l)
                ss = streams_for(l, ("m", 0))
                cols = sum(STREAMS[s][1] for s in ss)

                def weight_low(i):
                    n = SPLIT[l, i]
                    dve.wait_ge(*c.after("weight_high", l, i))
                    dve.tensor_tensor(WS[:, 2 * (i % 2) + 1], RING[:, n % NSLOT].rearrange("p a b -> p (a b)"),
                                      WS[:, 2 * (i % 2)], ALU.subtract).then_inc(
                        *c.done("weight_low", l, i, also=[("weights_used", n)]))

                def merged_low(k):
                    dve.wait_ge(*c.after("merged_high", l, k))
                    dve.tensor_tensor(HS[:, KD + k, 0:cols], YM[:, k, 0:cols], HS[:, k, 0:cols], ALU.subtract).then_inc(
                        *c.done("merged_low", l, k))

                for j in range(KD):
                    if j:
                        weight_low(3 * j - 1)
                    fill(l, "merge", j)
                    weight_low(3 * j)
                    weight_low(3 * j + 1)
                    if j == 0:
                        dve.wait_ge(*c.after("h_low", l, KD - 1))
                        dve.wait_ge(*c.after("m", l, RAW - 1, ss[-1]))
                    if j == KD - 1:
                        for k in range(KD - 1):
                            merged_low(k)
                    for b in range(3):
                        for s in ss:
                            off, T = STREAMS[s]
                            dve.wait_ge(*c.after("branch", l, j, b, s))
                            dve.wait_ge(*c.after("gate", l, j, b, s))
                            dst = YM[:, j, off:off + T] if b == 0 else MT[:, b % 2, off:off + T]
                            if b:
                                if b == 1 and j:
                                    dve.wait_ge(*c.after("merge_add", l, j - 1, 1, s))
                                elif b == 2 and j:
                                    dve.wait_ge(*c.after("merge_add", l, j - 1, 2, s))
                            dve.tensor_tensor(dst, ps.of("branch", l, j, b, s)[:, 0:T], MG[:, j % 2, b, off:off + T], ALU.mult).then_inc(
                                *c.done("gated", l, j, b, s, also=[("freed", "branch", l, j, b, s)]))
                merged_low(KD - 1)
                dve.wait_ge(*c.after("load_x", "merge", l))
                dve.wait_ge(*c.after("adaln", l, 3 * KD - 1))
                for j in range(KD):
                    if 3 * KD - RAW + 2 + j < NSPLIT:
                        weight_low(3 * KD - RAW + 2 + j)
                    for s in ss:
                        off, T = STREAMS[s]
                        e = 0 if s == "lat" else 1
                        dve.wait_ge(*c.after("out", l, j, s))
                        dve.scalar_tensor_tensor(X[:, j, off:off + T], ps.of("out", l, j, s)[:, 0:T], ADAS[:, l, 16 + j, e:e + 1],
                                                 X[:, j, off:off + T], ALU.mult, ALU.add).then_inc(
                            *c.done("x_new", l, j, s, also=[("freed", "out", l, j, s)] +
                                    ([("x_new", l, "all")] if (j, s) == (KD - 1, ss[-1]) else [])))

            fill(0, "start")
            for l in range(DEPTH):
                hyena(l)
                c.phase_end(("hyena", l))
                gla(l)
                c.phase_end(("gla", l))
                attn(l)
                c.phase_end(("attn", l))
                merge(l)
                c.phase_end(("merge", l))
            norm(DEPTH, ["lat"])
            c.phase_end(("norm", DEPTH))

        @block.gpsimd
        def _(pool):
            c.engine = "pool"
            pool.memset(SMALL[:, 255:256], 0.0).then_inc(*c.done("pool_start"))
            for l in range(DEPTH):
                def fill(*point):
                    for kind, *j in FILL[l].get(point, []):
                        if kind == "hz":
                            for s in streams_for(l, ("hz", j[0])):
                                off, T = STREAMS[s]
                                pool.wait_ge(*c.after("hz_silu", l, j[0], s))
                                pool.wait_ge(*c.after("short_conv", l, 8 + j[0], s))
                                z = YBT[:, 8 + j[0], off:off + T]
                                pool.tensor_tensor(z, z, HZ[:, j[0] % 2, off:off + T], ALU.mult).then_inc(*c.done("z_used", l, j[0], s))

                for s, o in cores_of(l):
                    for n in range(2 * STREAMS[s][1] // P):
                        fill("taps", s, o, n)
                    fill("parts", s, o)
                    nf = FACTORS[s]
                    for f in range(nf):
                        pool.wait_ge(*c.after("prod", l, s, o, f, 3))
                        pool.tensor_tensor(Y[:, 2 * f], Y[:, 2 * f], TT[:, 0], ALU.subtract).then_inc(*c.done("spec", l, s, o, f, 0))
                        pool.tensor_tensor(Y[:, 2 * f + 1], Y[:, 2 * f + 1], TT[:, 1], ALU.add).then_inc(
                            *c.done("spec", l, s, o, f, 1, also=[("spectrum", l, s, o)] if f == nf - 1 else []))
                    fill("spec", s, o)
                c.phase_end(("hyena", l))
                for s in streams_of(l):
                    off, T = STREAMS[s]
                    for v in range(len(LEVELS)):
                        pool.wait_ge(*c.after("level_exp", l, s, v))
                        pool.tensor_tensor(EL[:, v % 2, :, T:2 * T], EL[:, v % 2, :, T:2 * T], GK[:, :, off:off + T], ALU.mult).then_inc(
                            *c.done("level_k", l, s, v))
                c.phase_end(("gla", l))
                barrier(pool, "attn", l)
                cols = sum(STREAMS[s][1] for s in streams_for(l, ("m", 0)))
                for k in range(KD):
                    pool.tensor_copy(HS[:, k, 0:cols], H[:, k, 0:cols]).then_inc(*c.done("h_high", l, k))
                    pool.wait_ge(*c.after("h_high", l, k))
                    pool.tensor_tensor(HS[:, KD + k, 0:cols], H[:, k, 0:cols], HS[:, k, 0:cols], ALU.subtract).then_inc(
                        *c.done("h_low", l, k))
                c.phase_end(("attn", l))
                for j in range(KD):
                    for b in (1, 2):
                        for s in streams_for(l, ("m", 0)):
                            off, T = STREAMS[s]
                            pool.wait_ge(*c.after("gated", l, j, b, s))
                            if b == 2:
                                pool.wait_ge(*c.after("merge_add", l, j, 1, s))
                            y = YM[:, j, off:off + T]
                            pool.tensor_tensor(y, y, MT[:, b % 2, off:off + T], ALU.add).then_inc(
                                *c.done("merge_add", l, j, b, s, also=[("merged", l, "all")]
                                        if (j, b, s) == (KD - 1, 2, streams_for(l, ("m", 0))[-1]) else []))
                c.phase_end(("merge", l))
            c.phase_end(("norm", DEPTH))

        return c.at, list(c.sems)


def tables():
    f = np.float32
    i = np.arange(P)
    t = {}
    t["tri"] = np.stack([(i[:, None] <= i[None, :]), (i[:, None] >= i[None, :])], 1).astype(f) / f(16)
    t["ident"] = np.eye(P, dtype=f)
    t["diag2"] = 2 * np.eye(P, dtype=f)
    t["ones"] = np.broadcast_to(np.array([1 / 1024, 1 / 128, 1], f)[None, :, None], (P, 3, P)).copy()
    t["mask"] = np.stack([((i[:, None] // (2 * w)) == (i[None, :] // (2 * w))) & ((i[:, None] // w) != (i[None, :] // w))
                          for w in LEVELS], 1).astype(np.int32)
    half = 32
    inv = (f(10000.0) ** (-np.arange(0, half, 2, dtype=f) / f(half))).astype(f)
    tok = np.arange(LAT)
    ang = np.concatenate([(tok // GRID_W).astype(f)[:, None] * inv, (tok % GRID_W).astype(f)[:, None] * inv], -1)
    rope = np.stack([np.cos(ang), np.sin(ang)]).astype(f)
    t["rope"] = rope.reshape(2, 4, P, 32).transpose(2, 0, 1, 3).copy()
    emb, tcol = [], []
    for L in (LAT, CTX):
        lin = linspace(0.0, 1.0, L)
        w = (f(2.0 * math.pi) * np.arange(L, dtype=f) / f(L)).astype(f)
        fr = linspace(1e-4, 15, 16)
        e = np.concatenate([lin[:, None], np.cos(fr[None] * w[:, None]), -np.sin(fr[None] * w[:, None])], -1).astype(f)
        pos = np.concatenate([np.arange(L), [0], np.arange(L - 1, 0, -1)])
        emb.append(e[pos].T)
        tcol.append(-lin[pos].reshape(2 * L // P, P).T)
    t["emb"] = np.ascontiguousarray(np.concatenate(emb, 1))
    t["tcol"] = np.ascontiguousarray(np.concatenate(tcol, 1))
    t["delta"] = np.abs(linspace(math.log(1e-2) / 0.3, math.log(1e-2) / 1.5, 2048)).reshape(4, BW)
    freqs = [4 * i, 4 * i + 2, np.sort(np.concatenate([8 * np.arange(64) + 1, 8 * np.arange(64) + 7])),
             np.sort(np.concatenate([8 * np.arange(64) + 3, 8 * np.arange(64) + 5]))]
    FM, G = np.zeros((P, 16, P)), np.zeros((P, 8, LAT))
    for q, fq in enumerate(freqs):
        for b in range(2):
            a = 2 * np.pi * np.outer(i + P * b, fq) / 1024
            FM[:, 4 * q + 2 * b] = np.cos(a)
            FM[:, 4 * q + 2 * b + 1] = -np.sin(a)
            if q == 0:
                FM[:, 4 * q + 2 * b + 1, 0] = (-1.0) ** i
        a = 2 * np.pi * np.outer(fq, np.arange(LAT)) / 1024
        G[:, 2 * q], G[:, 2 * q + 1] = 2 * np.cos(a), -2 * np.sin(a)
        if q == 0:
            G[0, 0], G[0, 1] = 1.0, (-1.0) ** np.arange(LAT)
    t["FM"], t["G"] = FM.astype(f), G.astype(f)
    return t


def linspace(a, b, n):
    f = np.float32
    step = np.arange(n - 1, dtype=f) / f(n - 1)
    out = f(a) * (f(1) - step) + f(b) * step
    return np.append(out, f(b)).astype(f)


def kernel(**inputs):
    import numpy as _np
    import concourse.bacc as _bacc
    from concourse import mybir as _mybir
    from concourse.bass_utils import run_bass_kernel_spmd as _run

    a = {k: _np.asarray(v) for k, v in inputs.items()}
    tile = lambda w: _np.ascontiguousarray(w.reshape(w.shape[0] // P, P, w.shape[1] // P, P).transpose(2, 1, 0, 3))
    perm = _np.concatenate([_np.r_[64 * j:64 * j + 64, 64 * (j + 4):64 * (j + 4) + 64] for j in range(4)])
    widths = [256, 256, 512, 512, 16, 16, 512, 128, 128, 512, 1536, 512, 3072]
    edge = _np.cumsum([0] + widths)
    seg = [slice(edge[i], edge[i + 1]) for i in range(13)]
    w_in, w_br, wa, cols = [], [], [], []
    for l in range(DEPTH):
        w = a["w_in"][l]
        rank = _np.zeros((D, P), w.dtype)
        rank[:, 0:32] = w[:, edge[4]:edge[6]]
        gates = w[:, seg[12]].reshape(D, 3, KD, P).transpose(0, 2, 1, 3).reshape(D, 3 * D)
        order = [w[:, seg[10]], w[:, seg[11]], rank, w[:, seg[1]], w[:, seg[0]], w[:, seg[2]], w[:, seg[3]],
                 w[:, seg[7]], w[:, seg[8]], w[:, seg[6]][:, perm], w[:, seg[9]][:, perm], gates]
        w_in.append(tile(_np.concatenate(order, 1)))
        br = [tile(a["w_br_gla"][l]), tile(a["w_br_attn"][l][perm]), tile(a["w_br_hy"][l])]
        w_br.append(_np.concatenate(br, 2))
        m = _np.zeros((33, 512), _np.float32)
        m[0:16, 0:256], m[16:32, 256:512] = a["gla_wa_f"][l], a["gla_wa_b"][l]
        m[32, 0:256], m[32, 256:512] = a["gla_ba_f"][l], a["gla_ba_b"][l]
        wa.append(m)
        col = lambda v: v.reshape(-1, P).T
        eps, not0 = _np.full((P, 1), EPS, _np.float32), _np.ones((P, 1), _np.float32)
        not0[0] = 0
        cols.append(_np.concatenate([col(a["gla_norm"][l]), col(a["hy_conv_w"][l].reshape(-1)),
                                     col(a["hy_conv_b"][l]), col(a["final_norm"]), eps, not0], 1))
    x = _np.concatenate([a["x"][0], a["ctx"][0]], 0).T.reshape(KD, P, TOK).transpose(1, 0, 2)
    cond = _np.stack([a["c"][0], a["c_ctx"]], -1).reshape(KD, P, 2).transpose(1, 0, 2)
    gain = _np.concatenate([_np.tile(a["attn_qnorm"], (1, 8)), _np.tile(a["attn_knorm"], (1, 2))], 1)
    host = {
        "xT": x, "cond": cond, "w_in": _np.stack(w_in), "w_br": _np.stack(w_br), "wa": _np.stack(wa), "cols": _np.stack(cols),
        "b_ada": a["b_ada"].reshape(DEPTH, 24, P).transpose(2, 0, 1),
        "w_ada": _np.stack([tile(a["w_ada"][l]) for l in range(DEPTH)]),
        "w_out": _np.stack([tile(a["w_out"][l]) for l in range(DEPTH)]),
        "gain": gain, "f1": a["hy_f1_w"], "f2": a["hy_f2_w"], "f3": a["hy_f3_w"].reshape(DEPTH, 64, 4, BW),
        "c64": _np.stack([a["hy_f1_b"], a["hy_f1_freq"], a["hy_f2_b"], a["hy_f2_freq"]], -1), "skip": a["hy_skip"],
    }
    host.update(tables())

    def declare(nc):
        arrays, aps = {}, {}
        for name, v in host.items():
            v = _np.ascontiguousarray(v)
            arrays["in_" + name] = v
            aps[name] = nc.dram_tensor("in_" + name, v.shape, _mybir.dt.from_np(v.dtype), kind="ExternalInput").ap()
        aps["x_mid"] = nc.dram_tensor("x_mid", (P, KD, TOK), F32, kind="Internal").ap()
        aps["out"] = nc.dram_tensor("out_0", (KD, P, LAT), F32, kind="ExternalOutput").ap()
        return arrays, aps

    scratch = _bacc.Bacc("TRN2", target_bir_lowering=False, num_devices=1)
    known, stages = build_program(scratch, declare(scratch)[1])
    nc = _bacc.Bacc("TRN2", target_bir_lowering=False, num_devices=1)
    arrays, aps = declare(nc)
    build_program(nc, aps, known, [s for s in stages if s != "any"])
    r = _run(nc, [arrays], core_ids=[0])
    return r.results[0]["out_0"].reshape(D, LAT).T[None]
```
